# Optimizing a Trainium2 kernel written in Bass

```python
import math
import jax, jax.numpy as jnp
from jax import lax
import numpy as np

D_MODEL = 1024
BATCH = 1
SEQ = 256
DEPTH = 1
DEC_BATCH = 1
DEC_SEQ = 64
PAST_LEN = 256

CHUNK = 64
QBLOCK = 128
RMS_EPS = 1e-6
SSM_GROUPS = 32
SSM_GROUP_CH = 16
SSM_WIDTH = SSM_GROUPS * SSM_GROUP_CH
SSM_STATE = 64
DT_MIN = 0.001
DT_MAX = 0.1
MLA_HEADS = 8
QK_NOPE = 64
QK_ROPE = 32
QK_HEAD = QK_NOPE + QK_ROPE
V_HEAD = 64
Q_LORA = 384
KV_LORA = 256
ROPE_BASE = 10000.0
MLA_WIDTH = MLA_HEADS * V_HEAD
MEM_TOKENS = 256
MEM_HEADS = 4
MEM_HEAD = 128
MEM_WIDTH = MEM_HEADS * MEM_HEAD
N_BRANCHES = 3
IN_WIDTH = SSM_WIDTH + Q_LORA + KV_LORA + QK_ROPE + MEM_WIDTH + N_BRANCHES * D_MODEL
N_EXPERT_GROUPS = 4
EXPERTS_PER_GROUP = 8
N_EXPERTS = N_EXPERT_GROUPS * EXPERTS_PER_GROUP
TOP_K_IN_GROUP = 2
EXPERT_FF = 256

kernel_name = "hybrid_s5_mla_memxattn_hiermoe_stream_step"

def rmsnorm(x, g):
    xf = x.astype(jnp.float32)
    xf = xf * lax.rsqrt(jnp.mean(xf * xf, axis=-1, keepdims=True) + RMS_EPS)
    return (xf * g.astype(jnp.float32)).astype(x.dtype)

def apply_rope(x, pos):
    half = x.shape[-1] // 2
    inv = ROPE_BASE ** (-jnp.arange(half, dtype=jnp.float32) / half)
    ang = pos.astype(jnp.float32)[:, None] * inv[None, :]
    cos = jnp.cos(ang)[None, :, None, :]
    sin = jnp.sin(ang)[None, :, None, :]
    xf = x.astype(jnp.float32)
    x1, x2 = xf[..., :half], xf[..., half:]
    return jnp.concatenate([x1 * cos - x2 * sin, x2 * cos + x1 * sin], axis=-1).astype(x.dtype)

def _complex_affine_combine(earlier, later):
    a1r, a1i, b1r, b1i = earlier
    a2r, a2i, b2r, b2i = later
    ar = a1r * a2r - a1i * a2i
    ai = a1r * a2i + a1i * a2r
    br = a2r * b1r - a2i * b1i + b2r
    bi = a2r * b1i + a2i * b1r + b2i
    return (ar, ai, br, bi)

def s5_branch(u, h0_re, h0_im, p):
    b_, l_, _ = u.shape
    uf = u.astype(jnp.float32).reshape(b_, l_, SSM_GROUPS, SSM_GROUP_CH)
    dt = jnp.exp(p["ssm_log_dt"].astype(jnp.float32))[:, None]
    lr = p["ssm_a_re"].astype(jnp.float32)
    li = p["ssm_a_im"].astype(jnp.float32)
    mag = jnp.exp(lr * dt)
    ab_re, ab_im = mag * jnp.cos(li * dt), mag * jnp.sin(li * dt)
    den = lr * lr + li * li
    nr, ni = ab_re - 1.0, ab_im
    f_re = (nr * lr + ni * li) / den
    f_im = (ni * lr - nr * li) / den
    br = p["ssm_b_re"].astype(jnp.float32)
    bi = p["ssm_b_im"].astype(jnp.float32)
    bb_re = f_re[..., None] * br - f_im[..., None] * bi
    bb_im = f_re[..., None] * bi + f_im[..., None] * br
    bu_re = jnp.einsum('blgc,gpc->blgp', uf, bb_re)
    bu_im = jnp.einsum('blgc,gpc->blgp', uf, bb_im)
    a_re_b = jnp.broadcast_to(ab_re, bu_re.shape)
    a_im_b = jnp.broadcast_to(ab_im, bu_re.shape)
    acc_re, acc_im, s_re, s_im = lax.associative_scan(
        _complex_affine_combine, (a_re_b, a_im_b, bu_re, bu_im), axis=1)
    h0r = h0_re.astype(jnp.float32)[:, None]
    h0i = h0_im.astype(jnp.float32)[:, None]
    h_re = s_re + acc_re * h0r - acc_im * h0i
    h_im = s_im + acc_re * h0i + acc_im * h0r
    y = (jnp.einsum('blgp,gcp->blgc', h_re, p["ssm_c_re"].astype(jnp.float32))
         - jnp.einsum('blgp,gcp->blgc', h_im, p["ssm_c_im"].astype(jnp.float32)))
    y = y.reshape(b_, l_, SSM_WIDTH) + p["ssm_d"].astype(jnp.float32) * uf.reshape(b_, l_, SSM_WIDTH)
    z = jax.nn.gelu(y).astype(u.dtype)
    zz = z @ p["w_glu"]
    out = zz[..., :D_MODEL] * jax.nn.sigmoid(zz[..., D_MODEL:])
    return out, h_re[:, -1], h_im[:, -1]

def mla_queries(q_lat, pos, p):
    q = rmsnorm(q_lat, p["g_qlat"]) @ p["w_uq"]
    q = q.reshape(q.shape[0], q.shape[1], MLA_HEADS, QK_HEAD)
    q = rmsnorm(q, p["g_qn"])
    return jnp.concatenate([q[..., :QK_NOPE], apply_rope(q[..., QK_NOPE:], pos)], axis=-1)

def mla_keys_values(c_kv, k_pe, pos, p):
    b_, s_, _ = c_kv.shape
    kv = (c_kv @ p["w_ukv"]).reshape(b_, s_, MLA_HEADS, QK_NOPE + V_HEAD)
    k_nope, v = kv[..., :QK_NOPE], kv[..., QK_NOPE:]
    kpe = jnp.broadcast_to(k_pe[:, :, None, :], (b_, s_, MLA_HEADS, QK_ROPE))
    k = rmsnorm(jnp.concatenate([k_nope, kpe], axis=-1), p["g_kn"])
    k = jnp.concatenate([k[..., :QK_NOPE], apply_rope(k[..., QK_NOPE:], pos)], axis=-1)
    return k, v

def attention_blocked(q, k, v):
    b_, l_, h_, _ = q.shape
    scale = 1.0 / math.sqrt(QK_HEAD)
    k_chunk = jnp.arange(l_) // CHUNK

    def one_block(i):
        qb = lax.dynamic_slice_in_dim(q, i * QBLOCK, QBLOCK, axis=1)
        s = jnp.einsum('bqhd,bkhd->bhqk', qb, k).astype(jnp.float32) * scale
        q_chunk = (i * QBLOCK + jnp.arange(QBLOCK)) // CHUNK
        mask = k_chunk[None, :] <= q_chunk[:, None]
        s = jnp.where(mask[None, None], s, -1e30)
        pr = jax.nn.softmax(s, axis=-1).astype(v.dtype)
        return jnp.einsum('bhqk,bkhd->bqhd', pr, v)

    out = lax.map(one_block, jnp.arange(l_ // QBLOCK))
    return out.transpose(1, 0, 2, 3, 4).reshape(b_, l_, h_, v.shape[-1])

def attention_with_past(q, k, v, q_pos, k_pos):
    scale = 1.0 / math.sqrt(QK_HEAD)
    s = jnp.einsum('bqhd,bkhd->bhqk', q, k).astype(jnp.float32) * scale
    mask = (k_pos // CHUNK)[None, :] <= (q_pos // CHUNK)[:, None]
    s = jnp.where(mask[None, None], s, -1e30)
    pr = jax.nn.softmax(s, axis=-1).astype(v.dtype)
    return jnp.einsum('bhqk,bkhd->bqhd', pr, v)

def memory_kv(mem, p):
    b_, m_, _ = mem.shape
    kv = (rmsnorm(mem, p["g_mem"]) @ p["w_mem_kv"]).reshape(b_, m_, 2, MEM_HEADS, MEM_HEAD)
    k = rmsnorm(kv[:, :, 0], p["g_mkn"])
    return k, kv[:, :, 1]

def memory_attention(q_mem, mem_k, mem_v, p):
    b_, l_, _ = q_mem.shape
    q = rmsnorm(q_mem.reshape(b_, l_, MEM_HEADS, MEM_HEAD), p["g_mqn"])
    s = jnp.einsum('bqhd,bkhd->bhqk', q, mem_k).astype(jnp.float32) * (1.0 / math.sqrt(MEM_HEAD))
    pr = jax.nn.softmax(s, axis=-1).astype(mem_v.dtype)
    o = jnp.einsum('bhqk,bkhd->bqhd', pr, mem_v).reshape(b_, l_, MEM_WIDTH)
    return o @ p["w_o_mem"]

def hierarchical_moe(h, p):
    lg = (h @ p["w_rg"]).astype(jnp.float32) + p["b_rg"].astype(jnp.float32)
    pg = jax.nn.softmax(lg, axis=-1)
    g_onehot = jax.nn.one_hot(jnp.argmax(lg, axis=-1), N_EXPERT_GROUPS, dtype=jnp.float32)
    p_top = jnp.sum(pg * g_onehot, axis=-1, keepdims=True)
    le = (h @ p["w_re"]).astype(jnp.float32).reshape(*h.shape[:-1], N_EXPERT_GROUPS, EXPERTS_PER_GROUP)
    le = le + p["b_re"].astype(jnp.float32)
    le_sel = jnp.sum(le * g_onehot[..., None], axis=-2)
    tv, ti = lax.top_k(le_sel, TOP_K_IN_GROUP)
    qv = jax.nn.softmax(tv, axis=-1)
    w_grp = jnp.sum(jax.nn.one_hot(ti, EXPERTS_PER_GROUP, dtype=jnp.float32) * qv[..., None], axis=-2)
    gate = (g_onehot[..., :, None] * (p_top * w_grp)[..., None, :]).reshape(*h.shape[:-1], N_EXPERTS)
    gate = gate.astype(h.dtype)
    y = jnp.zeros_like(h)
    for e in range(N_EXPERTS):
        hid = jax.nn.silu(h @ p["w_e1"][e]) * (h @ p["w_e3"][e])
        y = y + gate[..., e:e + 1] * (hid @ p["w_e2"][e])
    return y

def layer_forward(x, pos, h0_re, h0_im, mem_k, mem_v, past_ckv, past_kpe, p):
    b_, l_, _ = x.shape
    h = rmsnorm(x, p["g_attn"])
    proj = h @ p["w_in"]
    o1 = SSM_WIDTH
    o2 = o1 + Q_LORA
    o3 = o2 + KV_LORA
    o4 = o3 + QK_ROPE
    o5 = o4 + MEM_WIDTH
    u, q_lat, kv_lat = proj[..., :o1], proj[..., o1:o2], proj[..., o2:o3]
    k_pe, q_mem, g_logit = proj[..., o3:o4], proj[..., o4:o5], proj[..., o5:]
    br_a, h_re, h_im = s5_branch(u, h0_re, h0_im, p)
    c_kv = rmsnorm(kv_lat, p["g_kvlat"])
    q = mla_queries(q_lat, pos, p)
    if past_ckv is None:
        k, v = mla_keys_values(c_kv, k_pe, pos, p)
        o = attention_blocked(q, k, v)
    else:
        k_pos = jnp.concatenate([jnp.arange(past_ckv.shape[1]), pos])
        k, v = mla_keys_values(jnp.concatenate([past_ckv, c_kv], axis=1),
                               jnp.concatenate([past_kpe, k_pe], axis=1), k_pos, p)
        o = attention_with_past(q, k, v, pos, k_pos)
    br_b = o.reshape(b_, l_, MLA_WIDTH) @ p["w_o_mla"]
    br_c = memory_attention(q_mem, mem_k, mem_v, p)
    gates = jax.nn.sigmoid(g_logit).reshape(b_, l_, N_BRANCHES, D_MODEL)
    merged = gates[..., 0, :] * br_a + gates[..., 1, :] * br_b + gates[..., 2, :] * br_c
    x = x + merged @ p["w_out"]
    x = x + hierarchical_moe(rmsnorm(x, p["g_ffn"]), p)
    return x, c_kv, k_pe, h_re.astype(x.dtype), h_im.astype(x.dtype)

def setup_inputs(seed: int = 0) -> dict:
    key = jax.random.key(seed)
    ks = iter(jax.random.split(key, 48))
    f32 = jnp.float32

    def nrm(shape, scale):
        return jax.random.normal(next(ks), shape, f32) * scale

    def gain(shape):
        return 1.0 + 0.05 * jax.random.normal(next(ks), shape, f32)

    n_idx = jnp.arange(SSM_STATE, dtype=f32)
    return {
        "x_prompt": nrm((BATCH, SEQ, D_MODEL), 1.0),
        "x_sample": nrm((DEC_BATCH, DEC_SEQ, D_MODEL), 1.0),
        "cache_mla_ckv": nrm((DEPTH, DEC_BATCH, PAST_LEN, KV_LORA), 1.0),
        "cache_mla_kpe": nrm((DEPTH, DEC_BATCH, PAST_LEN, QK_ROPE), 1.0),
        "cache_ssm_re": nrm((DEPTH, DEC_BATCH, SSM_GROUPS, SSM_STATE), 0.3),
        "cache_ssm_im": nrm((DEPTH, DEC_BATCH, SSM_GROUPS, SSM_STATE), 0.3),
        "cache_mem_k": nrm((DEPTH, DEC_BATCH, MEM_TOKENS, MEM_HEADS, MEM_HEAD), 1.0),
        "cache_mem_v": nrm((DEPTH, DEC_BATCH, MEM_TOKENS, MEM_HEADS, MEM_HEAD), 1.0),
        "mem_prompt": nrm((BATCH, MEM_TOKENS, D_MODEL), 1.0),
        "g_attn": gain((DEPTH, D_MODEL)),
        "w_in": nrm((DEPTH, D_MODEL, IN_WIDTH), D_MODEL ** -0.5),
        "ssm_a_re": -0.5 * jnp.exp(nrm((DEPTH, SSM_GROUPS, SSM_STATE), 0.01)),
        "ssm_a_im": math.pi * n_idx + nrm((DEPTH, SSM_GROUPS, SSM_STATE), 0.01),
        "ssm_log_dt": jax.random.uniform(next(ks), (DEPTH, SSM_GROUPS), f32,
                                         minval=math.log(DT_MIN), maxval=math.log(DT_MAX)),
        "ssm_b_re": nrm((DEPTH, SSM_GROUPS, SSM_STATE, SSM_GROUP_CH), (2.0 * SSM_GROUP_CH) ** -0.5),
        "ssm_b_im": nrm((DEPTH, SSM_GROUPS, SSM_STATE, SSM_GROUP_CH), (2.0 * SSM_GROUP_CH) ** -0.5),
        "ssm_c_re": nrm((DEPTH, SSM_GROUPS, SSM_GROUP_CH, SSM_STATE), (2.0 * SSM_STATE) ** -0.5),
        "ssm_c_im": nrm((DEPTH, SSM_GROUPS, SSM_GROUP_CH, SSM_STATE), (2.0 * SSM_STATE) ** -0.5),
        "ssm_d": nrm((DEPTH, SSM_WIDTH), 1.0),
        "w_glu": nrm((DEPTH, SSM_WIDTH, 2 * D_MODEL), SSM_WIDTH ** -0.5),
        "g_qlat": gain((DEPTH, Q_LORA)),
        "w_uq": nrm((DEPTH, Q_LORA, MLA_HEADS * QK_HEAD), Q_LORA ** -0.5),
        "g_kvlat": gain((DEPTH, KV_LORA)),
        "w_ukv": nrm((DEPTH, KV_LORA, MLA_HEADS * (QK_NOPE + V_HEAD)), KV_LORA ** -0.5),
        "g_qn": gain((DEPTH, QK_HEAD)),
        "g_kn": gain((DEPTH, QK_HEAD)),
        "w_o_mla": nrm((DEPTH, MLA_WIDTH, D_MODEL), MLA_WIDTH ** -0.5),
        "g_mem": gain((DEPTH, D_MODEL)),
        "w_mem_kv": nrm((DEPTH, D_MODEL, 2 * MEM_WIDTH), D_MODEL ** -0.5),
        "g_mqn": gain((DEPTH, MEM_HEAD)),
        "g_mkn": gain((DEPTH, MEM_HEAD)),
        "w_o_mem": nrm((DEPTH, MEM_WIDTH, D_MODEL), MEM_WIDTH ** -0.5),
        "w_out": nrm((DEPTH, D_MODEL, D_MODEL), D_MODEL ** -0.5),
        "g_ffn": gain((DEPTH, D_MODEL)),
        "w_rg": nrm((DEPTH, D_MODEL, N_EXPERT_GROUPS), D_MODEL ** -0.5),
        "b_rg": nrm((DEPTH, N_EXPERT_GROUPS), 0.01),
        "w_re": nrm((DEPTH, D_MODEL, N_EXPERTS), D_MODEL ** -0.5),
        "b_re": nrm((DEPTH, N_EXPERT_GROUPS, EXPERTS_PER_GROUP), 0.01),
        "w_e1": nrm((DEPTH, N_EXPERTS, D_MODEL, EXPERT_FF), D_MODEL ** -0.5),
        "w_e3": nrm((DEPTH, N_EXPERTS, D_MODEL, EXPERT_FF), D_MODEL ** -0.5),
        "w_e2": nrm((DEPTH, N_EXPERTS, EXPERT_FF, D_MODEL), EXPERT_FF ** -0.5),
    }

def reference(x_prompt, x_sample, cache_mla_ckv, cache_mla_kpe, cache_ssm_re, cache_ssm_im,
              cache_mem_k, cache_mem_v, mem_prompt, g_attn, w_in, ssm_a_re, ssm_a_im, ssm_log_dt,
              ssm_b_re, ssm_b_im, ssm_c_re, ssm_c_im, ssm_d, w_glu, g_qlat, w_uq, g_kvlat, w_ukv,
              g_qn, g_kn, w_o_mla, g_mem, w_mem_kv, g_mqn, g_mkn, w_o_mem, w_out, g_ffn,
              w_rg, b_rg, w_re, b_re, w_e1, w_e3, w_e2):
    xp, xs = x_prompt, x_sample
    pos_p = jnp.arange(xp.shape[1])
    pos_s = cache_mla_ckv.shape[2] + jnp.arange(xs.shape[1])
    p_ckv, p_kpe, p_sre, p_sim, p_mk, p_mv = [], [], [], [], [], []
    s_ckv, s_kpe, s_sre, s_sim = [], [], [], []
    for l in range(DEPTH):
        p = {
            "g_attn": g_attn[l], "w_in": w_in[l], "ssm_a_re": ssm_a_re[l], "ssm_a_im": ssm_a_im[l],
            "ssm_log_dt": ssm_log_dt[l], "ssm_b_re": ssm_b_re[l], "ssm_b_im": ssm_b_im[l],
            "ssm_c_re": ssm_c_re[l], "ssm_c_im": ssm_c_im[l], "ssm_d": ssm_d[l], "w_glu": w_glu[l],
            "g_qlat": g_qlat[l], "w_uq": w_uq[l], "g_kvlat": g_kvlat[l], "w_ukv": w_ukv[l],
            "g_qn": g_qn[l], "g_kn": g_kn[l], "w_o_mla": w_o_mla[l], "g_mem": g_mem[l],
            "w_mem_kv": w_mem_kv[l], "g_mqn": g_mqn[l], "g_mkn": g_mkn[l], "w_o_mem": w_o_mem[l],
            "w_out": w_out[l], "g_ffn": g_ffn[l], "w_rg": w_rg[l], "b_rg": b_rg[l],
            "w_re": w_re[l], "b_re": b_re[l], "w_e1": w_e1[l], "w_e3": w_e3[l], "w_e2": w_e2[l],
        }
        mk, mv = memory_kv(mem_prompt, p)
        h0 = jnp.zeros((xp.shape[0], SSM_GROUPS, SSM_STATE), jnp.float32)
        xp, ckv_p, kpe_p, sre_p, sim_p = layer_forward(xp, pos_p, h0, h0, mk, mv, None, None, p)
        xs, ckv_s, kpe_s, sre_s, sim_s = layer_forward(
            xs, pos_s, cache_ssm_re[l], cache_ssm_im[l], cache_mem_k[l], cache_mem_v[l],
            cache_mla_ckv[l], cache_mla_kpe[l], p)
        p_ckv.append(ckv_p); p_kpe.append(kpe_p); p_sre.append(sre_p); p_sim.append(sim_p)
        p_mk.append(mk); p_mv.append(mv)
        s_ckv.append(ckv_s); s_kpe.append(kpe_s); s_sre.append(sre_s); s_sim.append(sim_s)
    return (xp, xs, jnp.stack(p_ckv), jnp.stack(p_kpe), jnp.stack(p_sre), jnp.stack(p_sim),
            jnp.stack(p_mk), jnp.stack(p_mv), jnp.stack(s_ckv), jnp.stack(s_kpe),
            jnp.stack(s_sre), jnp.stack(s_sim))


_drawn_inputs = setup_inputs


def setup_inputs(seed=0):
    import zlib

    import numpy as np

    out = dict(_drawn_inputs(seed))
    spreads = {}
    factors = {'ssm_a_re': 64.0,
     'g_mqn': 4.036,
     'b_rg': 2.982,
     'g_qlat': 8.0,
     'g_qn': 2.841,
     'g_kn': 5.105,
     'b_re': 4.498}
    for name, (base, spread) in spreads.items():
        noise = np.random.default_rng([zlib.crc32(name.encode()), seed]).standard_normal(out[name].shape)
        drawn = base * np.exp(spread * noise) if base else spread * noise
        out[name] = __import__('jax').numpy.asarray(drawn.astype(out[name].dtype))
    for name, factor in factors.items():
        out[name] = (out[name] * factor).astype(out[name].dtype)
    return out
```

```python
import math
from contextlib import ExitStack

import numpy as np

import concourse.bass as bass
from concourse import mybir

F32 = mybir.dt.float32
U32 = mybir.dt.uint32
I32 = mybir.dt.int32
ALU = mybir.AluOpType
ACT = mybir.ActivationFunctionType
AX = mybir.AxisListType

D = 1024
KD = D // 128
SEQ, DEC, PAST, MEMT = 256, 64, 256, 256
TOK = SEQ + DEC
TILES = [(0, 128), (128, 128), (256, 64)]
NT = len(TILES)
G, CH, ST = 32, 16, 64
GP = G // 2
WIN, NWIN = 64, TOK // 64
H, NOPE, ROPE, QK, VH = 8, 64, 32, 96, 64
QL, KVL = 384, 256
MH, MD = 4, 128
EPS = 1e-6
SCALE_MLA = 1.0 / math.sqrt(QK)
SCALE_MEM = 1.0 / math.sqrt(MD)
NEG = -1e30
NG, EPG = 4, 8
NE, FF = NG * EPG, 256
B = 64
NJ = (TOK - 1) // B
NOV = (2 * TOK - NE) // B
NBLK = NE + NOV
FILLS = [(f, min(128, NBLK * B - f)) for f in range(NE * B, NBLK * B, 128)]

KEYS = [(0, 128), (128, 128), (256, 128), (384, 128), (512, 64)]
KEY_OF_TILE = [0, 1, 4]
POS_OF_KEY = [0, 1, 0, 1, 2]

C_U, C_QL, C_KV, C_QM, C_GATE = 0, 512, 896, 1184, 1696
DGROUPS = [(0, 3), (3, 3), (6, 2)]
BRANCH_C, BRANCH_B, BRANCH_A = 2, 1, 0


def layout(parts):
    at, out = 0, {}
    for name, n in parts:
        out[name] = (at, at + n)
        at += n
    return out, at


CONST, NCONST = layout([("ident", 128), ("upper", 128), ("ones", 128), ("rope", 3 * 2 * ROPE),
                        ("mask0", 128), ("mask1", 256), ("iotab", B), ("iotablk", NBLK), ("iotae", NE),
                        ("sel_b", 2), ("sel_c", 4), ("valid", NT), ("tokid", NT), ("half", 8)])


def constants():
    c = np.zeros((128, NCONST), np.float32)

    def put(name, value):
        a, b = CONST[name]
        c[:, a:b] = np.asarray(value, np.float32).reshape(128, b - a)

    p = np.arange(128)
    put("ident", np.eye(128))
    put("upper", p[:, None] < p[None, :])
    put("ones", np.ones((128, 128)))
    inv = (10000.0 ** (-np.arange(ROPE // 2, dtype=np.float32) / (ROPE // 2))).astype(np.float32)
    rope = np.zeros((128, 3, 2, ROPE), np.float32)
    for n in range(3):
        ang = (p + 128 * n).astype(np.float32)[:, None] * inv[None, :]
        rope[:, n, 0] = np.concatenate([np.cos(ang), np.cos(ang)], 1)
        rope[:, n, 1] = np.concatenate([-np.sin(ang), np.sin(ang)], 1)
    put("rope", rope)
    chunk = p[:, None] // 64
    put("mask0", np.where(p[None, :] // 64 <= chunk, 0, NEG))
    put("mask1", np.where(np.arange(256)[None, :] // 64 <= 2 + chunk, 0, NEG))
    put("iotab", np.tile(np.arange(B), (128, 1)))
    put("iotablk", np.tile(np.arange(NBLK), (128, 1)))
    put("iotae", np.tile(np.arange(NE), (128, 1)))
    put("sel_b", np.stack([p // ST == 0, p // ST == 1], 1))
    even = (p // CH) % 2 == 0
    put("sel_c", np.stack([even, ~even, -1.0 * even, -1.0 * ~even], 1))
    put("valid", np.stack([p < n for _, n in TILES], 1))
    put("tokid", np.stack([np.where(p < n, p + f, 0) for f, n in TILES], 1))
    put("half", np.full((128, 8), -0.5))
    return c


CHUNKS = [("u0", KD, 256), ("u1", KD, 256), ("ql", KD, QL), ("kv", KD, KVL + ROPE), ("qm0", KD, 256),
          ("qm1", KD, 256), ("mk0", KD, 256), ("mk1", KD, 256), ("mv0", KD, 256), ("mv1", KD, 256),
          ("ukv", 2, H * (NOPE + VH)), ("uq", 3, H * QK)]
for br in ("C", "B"):
    for g, (d0, nd) in enumerate(DGROUPS):
        CHUNKS += [(f"gate{br}{g}", KD, 128 * nd), (f"out{br}{g}", 4, 128 * nd)]
for g, (d0, nd) in enumerate(DGROUPS):
    CHUNKS += [(f"glu{g}", 4, 256 * nd), (f"gateA{g}", KD, 128 * nd)]
for g, (d0, nd) in enumerate(DGROUPS):
    CHUNKS += [(f"wout{g}", KD, 128 * nd)]
CHUNK_NO = {c[0]: n for n, c in enumerate(CHUNKS)}
WSLOTS, WSLOT = 3, 3072

MEM_UNITS = [("mem", t, h, 2) for t in range(NT) for h in (0, 2)]
MLA_UNITS = ([("mla", 0, h, 4) for h in (0, 4)] + [("mla", 1, h, 2) for h in (0, 2, 4, 6)]
             + [("mla", 2, h, 1) for h in range(H)])
KQ_UNITS = [("k", j, half) for j in range(5) for half in (0, 1)] + [("q", t, half) for t in range(NT) for half in (0, 1)]
KQ_LAG, KQ_BUFS = 2, 4
RING = 5


def key_blocks(unit):
    kind, t = unit[0], unit[1]
    if kind == "mem":
        return [128, 128]
    return [[128], [128, 128], [128, 128, 64]][t]


def attention_order(units):
    for n in range(len(units) + 1):
        if n < len(units):
            yield "S", n
        if n >= 1:
            yield "PT", n - 1
            yield "O", n - 1
            if n == len(units) or units[n][1] != units[n - 1][1]:
                yield "OT", units[n - 1][1]


def units_in_order():
    out = [("par", "act")]
    out += [(("xT", t, g), "act") for t in range(NT) for g in range(2)]
    out += [(("u", m), "act") for m in range(4)]
    out += [((c, t), "act") for c in ("ql", "kv", "qm0", "qm1") for t in range(NT)]
    out += [(("memT", t, g), "act") for t in range(2) for g in range(2)]
    out += [((c, t), "act") for c in ("mk0", "mk1", "mv0", "mv1") for t in range(2)]
    out += [(("s5T", n), "act") for n in range(4)]
    out += [(("mkT", s, kt), "act") for s in range(2) for kt in range(2)]
    out += [(("qmT", t), "act") for t in range(NT)]
    for kind, units in (("mem", MEM_UNITS), ("mla", MLA_UNITS)):
        if kind == "mla":
            out += [(("qlT", t), "act") for t in range(NT)]
            out += [(("ckT", j), "act") for j in range(5)]
            for n in range(len(KQ_UNITS) + KQ_LAG):
                if n < len(KQ_UNITS):
                    out.append((("kq", n), "act"))
                if n >= KQ_LAG:
                    out.append((("kqT", n - KQ_LAG), "act"))
        for step, n in attention_order(units):
            out.append(((kind, step, n), {"S": "act", "PT": "act", "O": "dve", "OT": "act"}[step]))
    for br in ("C", "B"):
        for d in range(KD):
            out += [((f"gate{br}", d), "act"), ((f"out{br}", d), "dve")]
    for d in range(KD):
        out += [(("glug", d), "act"), (("gluv", d), "dve"), (("gateA", d), "act")]
    out += [(("wout", g, t), "dve") for g in range(3) for t in range(NT)]
    out += [(("h2T", t, g), "act") for t in range(NT) for g in range(2)]
    out += [(("route", t), "dve") for t in range(NT)] + [("rank", "dve"), ("table", "dve")]
    return out


UNITS = units_in_order()
UNIT_NO = {k: n for n, (k, _) in enumerate(UNITS)}


def last_use():
    out = {f"u{n}": ("u", 2 * n + 1) for n in range(2)}
    out |= {c: (c, NT - 1) for c in ("ql", "kv", "qm0", "qm1")}
    out |= {c: (c, 1) for c in ("mk0", "mk1", "mv0", "mv1")}
    out |= {"ukv": ("kq", 9), "uq": ("kq", len(KQ_UNITS) - 1)}
    for g, (d0, nd) in enumerate(DGROUPS):
        for br in "CB":
            out |= {f"gate{br}{g}": (f"gate{br}", d0 + nd - 1), f"out{br}{g}": (f"out{br}", d0 + nd - 1)}
        out |= {f"glu{g}": ("gluv", d0 + nd - 1), f"gateA{g}": ("gateA", d0 + nd - 1), f"wout{g}": ("wout", g, NT - 1)}
    return out


LAST_USE = last_use()

NORMS = ([("x", t) for t in range(NT)] + [("m", t) for t in range(2)] + [("ql", t) for t in range(NT)]
         + [("ck", t) for t in range(NT)] + [("qm", t) for t in range(NT)] + [("mk", t) for t in range(2)]
         + [("kq", n) for n in range(len(KQ_UNITS))] + [("f", t) for t in range(NT)])
NORM_NO = {k: n for n, k in enumerate(NORMS)}
NORM_WIDTH = {"x": D, "m": D, "ql": QL, "ck": KVL, "qm": MD, "mk": MD, "kq": QK, "f": D}
NORM_HEADS = {"x": 1, "m": 1, "ql": 1, "ck": 1, "qm": MH, "mk": MH, "kq": 4, "f": 1}
NORMS_BEFORE_S5 = NORM_NO["ql", 0]


def norm_rows(key):
    kind, n = key
    if kind == "m" or kind == "mk":
        return 128
    if kind == "kq":
        what, j, _ = KQ_UNITS[n]
        return KEYS[j][1] if what == "k" else TILES[j][1]
    return TILES[n][1]


class Steps:

    def __init__(self, eng, own):
        self.eng, self.own, self.count = eng, own, {}

    def mark(self, ins, sem=None, by=1):
        sem = self.own if sem is None else sem
        ins.then_inc(sem, by)
        self.count[sem] = self.count.get(sem, 0) + by
        return sem, self.count[sem]

    def after(self, *marks):
        for sem, n in marks:
            self.eng.wait_ge(sem, n)


class S5Turns:

    def __init__(self, turn, every):
        self.turn, self.every, self.beats, self.done = turn, every, 0, 0

    def beat(self):
        if self.beats % self.every == 0 and self.done < GP:
            self.turn(self.done)
            self.done += 1
        self.beats += 1

    def finish(self):
        while self.done < GP:
            self.turn(self.done)
            self.done += 1


S5_EVERY = 3


def build(nc, a, o, scratch):
    ctx = ExitStack()
    with ctx:
        def sem(name):
            return ctx.enter_context(nc.semaphore(name))

        def alloc(stack, name, shape, dt=F32):
            return stack.enter_context(nc.sbuf_tensor(name, shape, dt))

        def width(shape):
            return 4 * int(np.prod(shape[1:]))

        def overlay(stack, *groups):
            out, sizes = {}, [sum(width(s) for _, s in g) for g in groups]
            for n, group in enumerate(groups):
                own = stack if n == len(groups) - 1 else ExitStack()
                for name, shape in group:
                    if name in out:
                        alloc(own, f"{name}_again", shape)
                    else:
                        out[name] = alloc(own, name, shape)
                if n == len(groups) - 1:
                    if sizes[n] < max(sizes):
                        alloc(own, f"pad_{group[0][0]}", [128, (max(sizes) - sizes[n]) // 4])
                else:
                    own.close()
            return out

        X = alloc(ctx, "X", [128, NT, D])
        cst = alloc(ctx, "cst", [128, NCONST])
        sums = alloc(ctx, "sums", [128, len(NORMS), 4])
        rstd = alloc(ctx, "rstd", [128, len(NORMS), 4])
        means = alloc(ctx, "means", [128, len(NORMS), 4])
        grow = alloc(ctx, "grow", [128, D])
        junk = ctx.enter_context(nc.sbuf_tensor("junk", [128, D], mybir.dt.bfloat16))
        pre = ExitStack()
        hT = alloc(pre, "hT", [128, KD, TOK])
        uT = alloc(pre, "uT", [128, 4, TOK])
        qlat = alloc(pre, "qlat", [128, NT, QL])
        ckv = alloc(pre, "ckv", [128, 5, KVL + ROPE])
        oTmem = alloc(pre, "oTmem", [128, 4, TOK])
        oTmla = alloc(pre, "oTmla", [128, 4, TOK])
        W = [alloc(pre, f"W{i}", [128, WSLOT]) for i in range(WSLOTS)]
        gsmall = alloc(pre, "gsmall", [128, QL + KVL + 2 * QK + 2 * MD])
        s5par = alloc(pre, "s5par", [128, 5, GP])
        s5tmp = alloc(pre, "s5tmp", [128, 24, GP])
        cosT = alloc(pre, "cosT", [128, GP, WIN])
        sinT = alloc(pre, "sinT", [128, GP, WIN])
        wB = alloc(pre, "wB", [128, 2, 4, 128])
        wC = alloc(pre, "wC", [128, 2, 4, 128])
        dskip = alloc(pre, "dskip", [128, 4])
        rotA = alloc(pre, "rotA", [128, 2, TOK])
        rotB = alloc(pre, "rotB", [128, 2, TOK])
        rotC = alloc(pre, "rotC", [128, 2, TOK])
        hS = alloc(pre, "hS", [128, 2, 2, TOK])
        carry = alloc(pre, "carry", [128, 2, 3, 4])
        finals = alloc(pre, "finals", [128, 2, 2, GP])
        soft = alloc(pre, "soft", [128, 4, 3, 4])
        v = overlay(pre, [("Hn", [128, NT, D])],
                    [("bbar", [128, 2, GP, CH]), ("btmp", [128, 4, GP, CH])],
                    [("KQ", [128, KQ_BUFS, 4, QK]), ("ropet", [128, 2, 2, 4, ROPE])],
                    [("sig", [128, 2, TOK]), ("gsig", [128, 2, TOK]), ("mtmp", [128, 2, TOK])])
        Hn, bbar, btmp, KQ, ropet, sig, gsig, mtmp = (
            v[k] for k in ("Hn", "bbar", "btmp", "KQ", "ropet", "sig", "gsig", "mtmp"))
        v = overlay(pre, [("s5raw", [GP, 5, 128]), ("dtraw", [GP, 2]), ("braw", [128, 2, GP, CH]),
                          ("bpad", [128, 2, GP, 2, CH]), ("craw", [128, 2, 4, ST]), ("cpad", [128, 2, 4, 2, ST])],
                    [("P", [128, 2, 512]), ("PT", [128, 2, 512]), ("O", [128, NT, 512])])
        s5raw, dtraw, braw, bpad, craw, cpad = (v[k] for k in ("s5raw", "dtraw", "braw", "bpad", "craw", "cpad"))
        P, PT, O = v["P"], v["PT"], v["O"]
        kv = [("mk", [128, 2, 2, 512]), ("mv", [128, 2, 2, 512]), ("qmem", [128, NT, MH * MD])]
        v = overlay(pre, kv + [("mem", [128, 2, D]), ("memT", [128, KD, MEMT])],
                    kv + [("mkT", [128, 2, MH, MEMT]), ("qmT", [128, MH, TOK])],
                    [("ckT", [128, 2, 576]), ("qlT", [128, 3, TOK]), ("V", [128, 5, 512]),
                     ("qT", [128, H, TOK]), ("kT", [128, H, 576])],
                    [("mergedT", [128, KD, TOK]), ("gelu", [128, 4, TOK]), ("finrow", [GP, 4, 128])])
        mem, memT, mk, mv, qmem, mkT, qmT = (v[k] for k in ("mem", "memT", "mk", "mv", "qmem", "mkT", "qmT"))
        ckT, qlT, V, qT, kT = (v[k] for k in ("ckT", "qlT", "V", "qT", "kT"))
        mergedT, gelu, finrow = v["mergedT"], v["gelu"], v["finrow"]
        pre.close()
        moe = ExitStack()
        ctx.enter_context(moe)
        h2 = alloc(moe, "h2", [128, NT, D])
        h2T = alloc(moe, "h2T", [128, KD, TOK])
        wr = alloc(moe, "wr", [128, KD, NG + NE])
        brow = alloc(moe, "brow", [128, NG + NE])
        E13 = [alloc(moe, f"E13_{i}", [128, 2, KD, FF]) for i in range(4)]
        E2 = [alloc(moe, f"E2_{i}", [128, 2, D]) for i in range(4)]
        xg = alloc(moe, "xg", [B, 2, D])
        xT = alloc(moe, "xT", [128, 2, KD, B])
        tg = alloc(moe, "tg", [128, 2, 2, B])
        ug = alloc(moe, "ug", [128, 2, 2, B])
        hid = alloc(moe, "hid", [128, 2, 2, B])
        yb = alloc(moe, "yb", [B, 2, D])
        lg = alloc(moe, "lg", [128, NT, 40])
        r8 = alloc(moe, "r8", [128, 4, NT, 8])
        i8 = alloc(moe, "i8", [128, 2, NT, 8], U32)
        rs = alloc(moe, "rs", [128, 24, NT])
        ex4 = alloc(moe, "ex4", [128, 3, NT, NG])
        prod = alloc(moe, "prod", [128, NT, EPG, NG])
        Ek = alloc(moe, "Ek", [128, 3, NT, NE])
        rk = alloc(moe, "rk", [128, 8, NT, NE])
        cnt = alloc(moe, "cnt", [128, 6, NE])
        tp = alloc(moe, "tp", [128, 4, NT, NE])
        ohs = alloc(moe, "ohs", [128, 2, NT, B])
        ohb = alloc(moe, "ohb", [128, 4, NT, NBLK])
        idx = alloc(moe, "idx", [B, NBLK], U32)
        idx_ov = alloc(moe, "idx_ov", [B, 2], U32)
        pos = alloc(moe, "pos", [128, 2, NT], U32)
        ovcmp = alloc(moe, "ovcmp", [1, NOV, NE])
        ovf = alloc(moe, "ovf", [1, 2, NOV])
        ovi = alloc(moe, "ovi", [1, NOV + 1], I32)
        rows = alloc(moe, "rows", [128, 2, NT, D])
        PS = ctx.enter_context(nc.psum_tensor("PS", [128, 8, 512], F32))
        BU, YB = 5, 7

        def const(name, rows_=128):
            x, y = CONST[name]
            return cst[0:rows_, x:y]

        ident = const("ident")
        rope = const("rope").rearrange("p (n c d) -> p n c d", n=3, c=2)
        g_ql = gsmall[:, 0:QL]
        g_kv = gsmall[:, QL:QL + KVL]
        o1 = QL + KVL
        g_qn, g_kn = gsmall[:, o1:o1 + QK], gsmall[:, o1 + QK:o1 + 2 * QK]
        g_mq, g_mk = gsmall[:, o1 + 2 * QK:o1 + 2 * QK + MD], gsmall[:, o1 + 2 * QK + MD:]

        names = """x_loaded params_loaded const_loaded gains_loaded mem_loaded s5_loaded cache_loaded
            gffn_loaded router_loaded psum_full emptied_act emptied_dve sums_ready rstd_ready h_ready mem_ready
            s5_raw_ready s5_scaled s5_mag_ready s5_reduced s5_sin_ready s5_den s5_rden s5_tables s5_padded
            bu_full bu_free h_state y_full y_skipped y_square y_inner y_tanh z_ready finals_copied finals_full
            finals_out ql_ready ck_ready qm_ready mk_ready scores_max kq_ready merged h2_ready
            logits_in logits_exp onehot_ready tables_in idx_ready gathered0 gathered1 xt_full xt_ready
            ab_full tanh_ready hid_ready y_mm y_act y_dve y_filled y_stored0 y_stored1 h2_stored ov_idx ov_gathered ov_xt_full ov_xt_ready
            ov_ab ov_tanh ov_hid ov_y_mm ov_y_act ov_y_dve ov_stored ov_w rows_gathered0 rows_gathered1 rows_gathered2 out_ready
            stored pe_passed pool_passed act_step dve_step pool_step dve_moe ov_half""".split()
        s = {n: sem(n) for n in names}
        chunk_loaded = [sem(f"chunk_loaded{i}") for i in range(WSLOTS)]
        expert_loaded = [sem(f"expert_loaded{i}") for i in range(4)]

        def bank(key):
            return PS[:, UNIT_NO[key] % RING, :]

        def emptied_at(n):
            who = UNITS[n][1]
            return s["emptied_" + who], sum(1 for _, w in UNITS[:n + 1] if w == who)

        def chunk(name, kt, cols):
            return W[CHUNK_NO[name] % WSLOTS][:, 0:kt * cols].rearrange("p (k n) -> p k n", k=kt)

        def chunk_view(name):
            _, kt, cols = CHUNKS[CHUNK_NO[name]]
            return chunk(name, kt, cols)

        def chunk_source(name):
            w_in = a["w_in"][0].rearrange("(p k) n -> p k n", k=KD)
            w_mem = a["w_mem_kv"][0].rearrange("(p k) n -> p k n", k=KD)
            dst = chunk_view(name)
            cols = CHUNKS[CHUNK_NO[name]][2]
            first = {"u0": C_U, "u1": C_U + 256, "ql": C_QL, "kv": C_KV, "qm0": C_QM, "qm1": C_QM + 256}
            if name in first:
                return [(dst, w_in[:, :, first[name]:first[name] + cols])]
            if name[:2] in ("mk", "mv"):
                c = (512 if name[1] == "v" else 0) + 256 * int(name[2])
                return [(dst, w_mem[:, :, c:c + cols])]
            if name == "ukv":
                return [(dst, a["w_ukv"][0].rearrange("(k p) n -> p k n", p=128))]
            if name == "uq":
                return [(dst, a["w_uq"][0].rearrange("(k p) n -> p k n", p=128))]
            d0, nd = DGROUPS[int(name[-1])]
            if name.startswith("gate"):
                c = C_GATE + D * {"A": BRANCH_A, "B": BRANCH_B, "C": BRANCH_C}[name[4]] + 128 * d0
                return [(dst, w_in[:, :, c:c + cols])]
            if name.startswith("out"):
                w = a["w_o_mem"] if name[3] == "C" else a["w_o_mla"]
                return [(dst, w[0].rearrange("(k p) n -> p k n", p=128)[:, :, 128 * d0:128 * d0 + cols])]
            if name.startswith("glu"):
                w = a["w_glu"][0].rearrange("(k p) n -> p k n", p=128)
                n = 128 * nd
                return [(dst[:, :, 0:n], w[:, :, 128 * d0:128 * d0 + n]),
                        (dst[:, :, n:2 * n], w[:, :, D + 128 * d0:D + 128 * d0 + n])]
            w = a["w_out"][0].rearrange("(k p) n -> p k n", p=128)
            return [(dst, w[:, :, 128 * d0:128 * d0 + cols])]

        DMAS_OF = [len(chunk_source(c[0])) for c in CHUNKS]

        def chunk_loaded_at(name):
            n = CHUNK_NO[name]
            return chunk_loaded[n % WSLOTS], 16 * sum(DMAS_OF[m] for m in range(n % WSLOTS, n + 1, WSLOTS))

        e13_src = [a["w_e1"][0].rearrange("e (p k) n -> p e k n", k=KD), a["w_e3"][0].rearrange("e (p k) n -> p e k n", k=KD)]
        e2_src = a["w_e2"][0].rearrange("e (j p) n -> p e j n", p=128)
        LOADS = 3

        xp, xs = a["x_prompt"][0], a["x_sample"][0]
        block = ctx.enter_context(nc.Block())

        @block.sync
        def _(sp):
            st = Steps(sp, None)
            stored = []

            def store(dst, src):
                stored.append(st.mark(sp.dma_start(dst, src), s["stored"], 16))

            def load_chunk(n):
                if n >= WSLOTS:
                    sp.wait_ge(s["psum_full"], UNIT_NO[LAST_USE[CHUNKS[n - WSLOTS][0]]] + 1)
                for dst, src in chunk_source(CHUNKS[n][0]):
                    sp.dma_start(dst, src).then_inc(chunk_loaded[n % WSLOTS], 16)

            for t, (f, n) in enumerate(TILES):
                src = xp[f:f + n, :] if t < 2 else xs
                sp.dma_start(X[0:n, t, :], src).then_inc(s["x_loaded"], 16)
            sp.dma_start(cst[:], a["consts"]).then_inc(s["const_loaded"], 16)
            sp.dma_start(grow[:], a["g_attn"][0].partition_broadcast(128)).then_inc(s["gains_loaded"], 16)
            for n, name in enumerate(("ssm_a_re", "ssm_a_im")):
                sp.dma_start(s5raw[:, n, :], a[name][0].rearrange("(q g) p -> q (g p)", g=2)).then_inc(s["s5_loaded"], 16)
            for n, name in enumerate(("cache_ssm_re", "cache_ssm_im")):
                sp.dma_start(s5raw[:, 2 + n, :], a[name][0][0].rearrange("(q g) p -> q (g p)", g=2)).then_inc(s["s5_loaded"], 16)
            sp.dma_start(dtraw[:], a["ssm_log_dt"][0].rearrange("(q g) -> q g", g=2)).then_inc(s["s5_loaded"], 16)
            load_chunk(0)
            load_chunk(1)
            load_chunk(2)
            for n in range(2):
                sp.dma_start(mem[:, n, :], a["mem_prompt"][0][128 * n:128 * n + 128, :]).then_inc(s["mem_loaded"], 16)
            sp.dma_start(memT[:, 0:4, :].rearrange("p k n -> p (k n)"),
                         a["g_mem"][0].partition_broadcast(128)).then_inc(s["mem_loaded"], 16)
            for n, name in enumerate(("ssm_b_re", "ssm_b_im")):
                for g2 in range(2):
                    sp.dma_start(braw[64 * g2:64 * g2 + 64, n], a[name][0].rearrange("(q g) p c -> g p q c", g=2)[g2])\
                        .then_inc(s["params_loaded"], 16)
            for n, name in enumerate(("ssm_c_re", "ssm_c_im")):
                sp.dma_start(craw[:, n], a[name][0].rearrange("(t g) c p -> (g c) t p", g=8)).then_inc(s["params_loaded"], 16)
            sp.dma_start(dskip[:], a["ssm_d"][0].rearrange("(t p) -> p t", p=128),
                         allow_slow_non_contiguous=True).then_inc(s["params_loaded"], 16)
            for dst, name in ((g_ql, "g_qlat"), (g_kv, "g_kvlat"), (g_qn, "g_qn"), (g_kn, "g_kn"), (g_mq, "g_mqn"), (g_mk, "g_mkn")):
                sp.dma_start(dst, a[name][0].partition_broadcast(128)).then_inc(s["gains_loaded"], 16)
            for n in range(2):
                r = slice(128 * n, 128 * n + 128)
                sp.dma_start(ckv[:, 2 + n, 0:KVL], a["cache_mla_ckv"][0][0][r, :]).then_inc(s["cache_loaded"], 16)
                sp.dma_start(ckv[:, 2 + n, KVL:], a["cache_mla_kpe"][0][0][r, :]).then_inc(s["cache_loaded"], 16)
                sp.dma_start(mk[:, 1, n, :], a["cache_mem_k"][0][0][r].rearrange("t h d -> t (h d)")).then_inc(s["cache_loaded"], 16)
                sp.dma_start(mv[:, 1, n, :], a["cache_mem_v"][0][0][r].rearrange("t h d -> t (h d)")).then_inc(s["cache_loaded"], 16)
            for n in range(3, CHUNK_NO["ukv"]):
                load_chunk(n)
            for t, (f, n) in enumerate(TILES):
                sp.wait_ge(s["ck_ready"], t + 1)
                j = KEY_OF_TILE[t]
                store(o["ckv_p"][f:f + n, :] if t < 2 else o["ckv_s"], ckv[0:n, j, 0:KVL])
                store(o["kpe_p"][f:f + n, :] if t < 2 else o["kpe_s"], ckv[0:n, j, KVL:])
            for t in range(2):
                sp.wait_ge(s["mk_ready"], t + 1)
                store(o["mem_k"][128 * t:128 * t + 128, :], mk[:, 0, t, :])
                store(o["mem_v"][128 * t:128 * t + 128, :], mv[:, 0, t, :])
            for f, n in FILLS:
                sp.dma_start(scratch["y"][f:f + n, :], X[0:n, 0, :]).then_inc(s["y_filled"], 16)
            for n in range(CHUNK_NO["ukv"], CHUNK_NO["gateA0"]):
                load_chunk(n)
            sp.wait_ge(s["h_ready"], NT)
            sp.dma_start(grow[:], a["g_ffn"][0].partition_broadcast(128)).then_inc(s["gffn_loaded"], 16)
            sp.wait_ge(s["finals_out"], 1)
            for n, name in enumerate(("sre_p", "sim_p", "sre_s", "sim_s")):
                store(o[name], finrow[:, n, :])
            for n in range(CHUNK_NO["gateA0"], len(CHUNKS)):
                load_chunk(n)

            sp.wait_ge(s["y_filled"], 16 * len(FILLS))
            sp.wait_ge(s["psum_full"], UNIT_NO["wout", 2, NT - 1] + 1)
            st.after(stored[-1])
            sp.dma_start(wr[:, :, 0:NG], a["w_rg"][0].rearrange("(p k) n -> p k n", k=KD)).then_inc(s["router_loaded"], 16)
            sp.dma_start(wr[:, :, NG:], a["w_re"][0].rearrange("(p k) n -> p k n", k=KD)).then_inc(s["router_loaded"], 16)
            sp.dma_start(brow[:, 0:NG], a["b_rg"][0].partition_broadcast(128)).then_inc(s["router_loaded"], 16)
            sp.dma_start(brow[:, NG:], a["b_re"][0].rearrange("g e -> (g e)").partition_broadcast(128)).then_inc(s["router_loaded"], 16)

            def load_expert(u, e):
                for n in range(2):
                    sp.dma_start(E13[u][:, n, :, :], e13_src[n][:, e, :, :]).then_inc(expert_loaded[u], 16)
                sp.dma_start(E2[u][:], e2_src[:, e, :, :]).then_inc(expert_loaded[u], 16)

            for u in range(4):
                load_expert(u, u)
            for t, (f, n) in enumerate(TILES):
                sp.wait_ge(s["h2_ready"], t + 1)
                sp.dma_start(scratch["h2"][f:f + n, :], h2[0:n, t, :]).then_inc(s["h2_stored"], 16)

            def store_rows(u, e):
                sp.wait_ge(s["y_act"], e + 1)
                sp.wait_ge(s["y_dve"], e + 1)
                sp.dma_start(scratch["y"][bass.ts(e, B), :], yb[:, u % 2, :]).then_inc(s[f"y_stored{u % 2}"], 16)

            with sp.Fori(0, NE // 4 - 1) as i:
                for u in range(4):
                    e = i * 4 + u
                    sp.wait_ge(s["y_mm"], e + 1)
                    for n in range(2):
                        sp.dma_start(E13[u][:, n, :, :], e13_src[n][:, bass.ds(e + 4, 1), :, :].rearrange("p e k n -> p (e k) n"))\
                            .then_inc(expert_loaded[u], 16)
                    sp.dma_start(E2[u][:], e2_src[:, bass.ds(e + 4, 1), :, :].rearrange("p e k n -> p (e k) n"))\
                        .then_inc(expert_loaded[u], 16)
                    store_rows(u, e)
            for u in range(4):
                store_rows(u, NE - 4 + u)

            sp.wait_ge(s["idx_ready"], 1)
            blocks = sp.value_load(ovi[0:1, NOV:NOV + 1], min_val=0, max_val=NOV)
            with sp.Fori(0, NOV) as i:
                with sp.If(i < blocks):
                    e = sp.value_load(ovi[0:1, bass.ds(i, 1)], min_val=0, max_val=NE - 1)
                    sp.wait_ge(s["ov_y_mm"], i)
                    for n in range(2):
                        sp.dma_start(E13[0][:, n, :, :], e13_src[n][:, bass.ds(e, 1), :, :].rearrange("p e k n -> p (e k) n"))\
                            .then_inc(s["ov_w"], 16)
                    sp.dma_start(E2[0][:], e2_src[:, bass.ds(e, 1), :, :].rearrange("p e k n -> p (e k) n")).then_inc(s["ov_w"], 16)
                    sp.wait_ge(s["ov_y_act"], i + 1)
                    sp.wait_ge(s["ov_y_dve"], i + 1)
                    sp.dma_start(scratch["y"][bass.ds(i * B + NE * B, B), :], yb[:, 0, :]).then_inc(s["ov_stored"], 16)
            for t, (f, n) in enumerate(TILES):
                sp.wait_ge(s["out_ready"], t + 1)
                store(o["y_p"][f:f + n, :] if t < 2 else o["y_s"], X[0:n, t, :])
            st.after(stored[-1])

        @block.tensor
        def _(pe):
            mm = nc.tensor.matmul

            def begin(key):
                n = UNIT_NO[key]
                if n >= RING:
                    pe.wait_ge(*emptied_at(n - RING))
                return bank(key)

            def end(ins):
                ins.then_inc(s["psum_full"], 1)

            def use(name):
                sem_, value = chunk_loaded_at(name)
                pe.wait_ge(sem_, value)
                return chunk_view(name)

            def emptied(key):
                pe.wait_ge(*emptied_at(UNIT_NO[key]))

            pe.wait_ge(s["const_loaded"], 16)
            pe.wait_ge(s["s5_raw_ready"], 1)
            out = begin("par")
            for n in range(5):
                ins = nc.tensor.transpose(out[:, GP * n:GP * n + GP], s5raw[:, n, :], ident[0:GP, 0:GP])
            end(ins)

            for t, (f, n) in enumerate(TILES):
                pe.wait_ge(s["h_ready"], t + 1)
                for g in range(2):
                    out = begin(("xT", t, g))
                    for k in range(4):
                        ins = nc.tensor.transpose(out[:, k * n:k * n + n], Hn[0:n, t, 4 * g + k::KD], ident[0:n, 0:n])
                    end(ins)

            def feature_major(key, w, cols, rhs, kt):
                out = begin(key)
                for k in range(kt):
                    ins = mm(out[:, 0:TOK], w[:, k, cols:cols + 128], rhs[:, k, :], start=(k == 0), stop=(k == kt - 1))
                end(ins)

            def token_major(key, w, c0, cols, lhs, f, n, kt):
                out = begin(key)
                for k in range(kt):
                    ins = mm(out[0:n, 0:cols], lhs[:, k, f:f + n], w[:, k, c0:c0 + cols], start=(k == 0), stop=(k == kt - 1))
                end(ins)

            emptied(("xT", NT - 1, 1))
            for m in range(4):
                w = use(f"u{m // 2}")
                feature_major(("u", m), w, 128 * (m % 2), hT, KD)
            for name in ("ql", "kv", "qm0", "qm1"):
                w = use(name)
                for t, (f, n) in enumerate(TILES):
                    token_major((name, t), w, 0, CHUNKS[CHUNK_NO[name]][2], hT, f, n, KD)

            for t in range(2):
                pe.wait_ge(s["mem_ready"], t + 1)
                for g in range(2):
                    out = begin(("memT", t, g))
                    for k in range(4):
                        ins = nc.tensor.transpose(out[:, 128 * k:128 * k + 128], mem[:, t, 4 * g + k::KD], ident)
                    end(ins)
            emptied(("memT", 1, 1))
            for name in ("mk0", "mk1", "mv0", "mv1"):
                w = use(name)
                for t in range(2):
                    token_major((name, t), w, 0, 256, memT, 128 * t, 128, KD)

            for n in range(4):
                pe.wait_ge(s["s5_padded"], n + 1)
                out = begin(("s5T", n))
                for t in range(4):
                    src = (bpad[:, n, 4 * t:4 * t + 4].rearrange("p q g c -> p (q g c)") if n < 2
                           else cpad[:, n - 2, t].rearrange("p g s -> p (g s)"))
                    ins = nc.tensor.transpose(out[:, 128 * t:128 * t + 128], src, ident)
                end(ins)

            def s5_y(q):
                t, r = q // 4, 32 * (q % 4)
                pe.wait_ge(s["h_state"], q + 1)
                if q % 4 == 0 and t > 0:
                    pe.wait_ge(s["y_skipped"], t)
                for c in range(2):
                    ins = mm(PS[r:r + 32, YB, 0:TOK], wC[:, c, t, r:r + 32], hS[:, q % 2, c, :], start=(c == 0), stop=(c == 1))
                ins.then_inc(s["y_full"], 1)

            def s5_turn(q):
                t, r = q // 4, 32 * (q % 4)
                if q == 0:
                    emptied(("s5T", 3))
                else:
                    pe.wait_ge(s["bu_free"], q)
                for c in range(2):
                    ins = mm(PS[:, BU + c, 0:TOK], wB[r:r + 32, c, t, :], uT[r:r + 32, t, :], start=True, stop=True)
                ins.then_inc(s["bu_full"], 1)
                if q > 0:
                    s5_y(q - 1)

            turns = S5Turns(s5_turn, S5_EVERY)

            for src in range(2):
                for kt in range(2):
                    if src == 0:
                        pe.wait_ge(s["mk_ready"], kt + 1)
                    else:
                        pe.wait_ge(s["cache_loaded"], 16 * 8)
                    out = begin(("mkT", src, kt))
                    for h in range(MH):
                        ins = nc.tensor.transpose(out[:, 128 * h:128 * h + 128], mk[:, src, kt, MD * h:MD * h + MD], ident)
                    end(ins)
                    turns.beat()
            for t, (f, n) in enumerate(TILES):
                pe.wait_ge(s["qm_ready"], t + 1)
                out = begin(("qmT", t))
                for h in range(MH):
                    ins = nc.tensor.transpose(out[:, n * h:n * h + n], qmem[0:n, t, MD * h:MD * h + MD], ident[0:n, 0:n])
                end(ins)
                turns.beat()

            def attention(kind, units):
                mem_ = kind == "mem"
                for step, m in attention_order(units):
                    out = begin((kind, step, m))
                    if step == "OT":
                        n = TILES[m][1]
                        emptied((kind, "O", max(k for k, x in enumerate(units) if x[1] == m)))
                        for j in range(4):
                            ins = nc.tensor.transpose(out[:, n * j:n * j + n], O[0:n, m, 128 * j:128 * j + 128], ident[0:n, 0:n])
                        end(ins)
                        continue
                    _, t, h0, nh = units[m]
                    f, n = TILES[t]
                    kb = key_blocks(units[m])
                    nk = sum(kb)
                    if step == "S":
                        for h in range(nh):
                            if mem_:
                                lhs, rhs = qmT[:, h0 + h, f:f + n], mkT[:, t // 2, h0 + h, :]
                            else:
                                k0 = 0 if t < 2 else 256
                                lhs, rhs = qT[0:QK, h0 + h, f:f + n], kT[0:QK, h0 + h, k0:k0 + nk]
                            ins = mm(out[0:n, nk * h:nk * h + nk], lhs, rhs, start=True, stop=True)
                        end(ins)
                        turns.beat()
                    elif step == "PT":
                        emptied((kind, "S", m))
                        at = 0
                        for h in range(nh):
                            for b, rows_ in enumerate(kb):
                                src = P[0:n, m % 2, nk * h + 128 * b:nk * h + 128 * b + rows_]
                                ins = nc.tensor.transpose(out[0:rows_, n * at:n * at + n], src, ident[0:n, 0:n])
                                at += 1
                        end(ins)
                    else:
                        emptied((kind, "PT", m))
                        dv = MD if mem_ else VH
                        for h in range(nh):
                            for b, rows_ in enumerate(kb):
                                at = h * len(kb) + b
                                if mem_:
                                    rhs = mv[0:rows_, t // 2, b, MD * (h0 + h):MD * (h0 + h) + MD]
                                else:
                                    rhs = V[0:rows_, (0 if t < 2 else 2) + b, VH * (h0 + h):VH * (h0 + h) + VH]
                                ins = mm(out[0:n, dv * h:dv * h + dv], PT[0:rows_, m % 2, n * at:n * at + n], rhs,
                                         start=(b == 0), stop=(b == len(kb) - 1))
                        end(ins)

            emptied(("qmT", NT - 1))
            attention("mem", MEM_UNITS)

            for t, (f, n) in enumerate(TILES):
                pe.wait_ge(s["ql_ready"], t + 1)
                out = begin(("qlT", t))
                for k in range(3):
                    ins = nc.tensor.transpose(out[:, n * k:n * k + n], qlat[0:n, t, 128 * k:128 * k + 128], ident[0:n, 0:n])
                end(ins)
                turns.beat()
            for j, (f, n) in enumerate(KEYS):
                if j in (2, 3):
                    pe.wait_ge(s["cache_loaded"], 16 * 8)
                else:
                    pe.wait_ge(s["ck_ready"], KEY_OF_TILE.index(j) + 1)
                out = begin(("ckT", j))
                for k in range(2):
                    ins = nc.tensor.transpose(out[:, n * k:n * k + n], ckv[0:n, j, 128 * k:128 * k + 128], ident[0:n, 0:n])
                end(ins)
                turns.beat()
            emptied(("ckT", 4))
            for m in range(len(KQ_UNITS) + KQ_LAG):
                if m < len(KQ_UNITS):
                    what, j, half = KQ_UNITS[m]
                    if what == "k":
                        f, n = KEYS[j]
                        token_major(("kq", m), use("ukv"), 512 * half, 512, ckT, f, n, 2)
                    else:
                        f, n = TILES[j]
                        token_major(("kq", m), use("uq"), 384 * half, 384, qlT, f, n, 3)
                if m >= KQ_LAG:
                    m2 = m - KQ_LAG
                    what, j, half = KQ_UNITS[m2]
                    n = KEYS[j][1] if what == "k" else TILES[j][1]
                    pe.wait_ge(s["kq_ready"], m2 + 1)
                    out = begin(("kqT", m2))
                    for h in range(4):
                        ins = nc.tensor.transpose(out[0:QK, n * h:n * h + n], KQ[0:n, m2 % KQ_BUFS, h, :], ident[0:n, 0:n])
                    end(ins)
                turns.beat()
            emptied(("kqT", len(KQ_UNITS) - 1))
            attention("mla", MLA_UNITS)

            emptied(("mla", "OT", NT - 1))
            for br, oT in (("C", oTmem), ("B", oTmla)):
                for g, (d0, nd) in enumerate(DGROUPS):
                    for d in range(d0, d0 + nd):
                        feature_major((f"gate{br}", d), use(f"gate{br}{g}"), 128 * (d - d0), hT, KD)
                        feature_major((f"out{br}", d), use(f"out{br}{g}"), 128 * (d - d0), oT, 4)
                        turns.beat()
            turns.finish()
            s5_y(GP - 1)
            pe.wait_ge(s["finals_copied"], GP)
            pe.wait_ge(s["bu_free"], GP)
            for n in range(4):
                ins = nc.tensor.transpose(PS[0:GP, BU, 128 * n:128 * n + 128], finals[:, n // 2, n % 2, :], ident)
            ins.then_inc(s["finals_full"], 1)
            pe.wait_ge(s["z_ready"], 4)
            for g, (d0, nd) in enumerate(DGROUPS):
                for d in range(d0, d0 + nd):
                    w = use(f"glu{g}")
                    feature_major(("glug", d), w, 128 * (nd + d - d0), uT, 4)
                    feature_major(("gluv", d), w, 128 * (d - d0), uT, 4)
                    feature_major(("gateA", d), use(f"gateA{g}"), 128 * (d - d0), hT, KD)
            pe.wait_ge(s["merged"], KD)
            for g, (d0, nd) in enumerate(DGROUPS):
                for t, (f, n) in enumerate(TILES):
                    token_major(("wout", g, t), use(f"wout{g}"), 0, 128 * nd, mergedT, f, n, KD)

            for t, (f, n) in enumerate(TILES):
                pe.wait_ge(s["h2_ready"], t + 1)
                for g in range(2):
                    out = begin(("h2T", t, g))
                    for k in range(4):
                        ins = nc.tensor.transpose(out[:, k * n:k * n + n], h2[0:n, t, 4 * g + k::KD], ident[0:n, 0:n])
                    end(ins)
            emptied(("h2T", NT - 1, 1))
            pe.wait_ge(s["router_loaded"], 64)
            for t, (f, n) in enumerate(TILES):
                token_major(("route", t), wr, 0, NG + NE, h2T, f, n, KD)
            pe.wait_ge(s["onehot_ready"], 1)
            out = begin("rank")
            for t in range(NT):
                for t2 in range(t):
                    mm(out[:, NE * t:NE * t + NE], const("ones"), Ek[:, 2, t2, :], start=(t2 == 0), stop=False)
                mm(out[:, NE * t:NE * t + NE], const("upper"), Ek[:, 2, t, :], start=(t == 0), stop=True)
            for t in range(NT):
                ins = mm(out[:, NE * NT:NE * NT + NE], const("ones"), Ek[:, 2, t, :], start=(t == 0), stop=(t == NT - 1))
            end(ins)
            pe.wait_ge(s["tables_in"], 1)
            out = begin("table")
            for k in range(2):
                for t in range(NT):
                    ins = mm(out[0:B, 0:NBLK], ohs[:, k, t, :], ohb[:, k, t, :], start=(k + t == 0), stop=(k * NT + t == 2 * NT - 1))
            end(ins)
            pe.wait_ge(s["emptied_dve"], sum(1 for _, w in UNITS if w == "dve"))
            pe.wait_ge(s["emptied_act"], sum(1 for _, w in UNITS if w == "act"))

            def x_transposes(par, e, first):
                pe.wait_ge(s[f"gathered{par}"], 8 * (e - par) + 16)
                if not first:
                    pe.wait_ge(s["xt_ready"], e - 1)
                pe.sem_inc(s["pe_passed"], 1)
                for k in range(KD):
                    ins = nc.tensor.transpose(PS[:, par, B * k:B * k + B], xg[:, par, k::KD], ident[0:B, 0:B])
                ins.then_inc(s["xt_full"], 1)

            def up(slot, par, e, first, turn):
                pe.wait_ge(expert_loaded[slot], 16 * LOADS * (turn + 1))
                pe.wait_ge(s["xt_ready"], e + 1)
                if not first:
                    pe.wait_ge(s["hid_ready"], e - 1)
                up_products(slot, par).then_inc(s["ab_full"], 1)

            def up_products(slot, par):
                for w in range(2):
                    for j in range(2):
                        for k in range(KD):
                            ins = mm(PS[:, 2 + par, B * (2 * w + j):B * (2 * w + j) + B], E13[slot][:, w, k, 128 * j:128 * j + 128],
                                     xT[:, par, k, :], start=(k == 0), stop=(k == KD - 1))
                return ins

            def down(slot, par, e, first):
                pe.wait_ge(s["hid_ready"], e + 1)
                if not first:
                    pe.wait_ge(s["y_act"], e - 1)
                    pe.wait_ge(s["y_dve"], e - 1)
                down_products(slot, par).then_inc(s["y_mm"], 1)

            def down_products(slot, par):
                for c in range(2):
                    for j in range(2):
                        ins = mm(PS[0:B, 4 + 2 * par + c, :], hid[:, par, j, :], E2[slot][:, j, 512 * c:512 * c + 512],
                                 start=(j == 0), stop=(j == 1))
                return ins

            x_transposes(0, 0, True)
            for e in range(4):
                up(e, e % 2, e, e < 2, 0)
                x_transposes((e + 1) % 2, e + 1, e + 1 < 2)
                if e > 0:
                    down(e - 1, (e - 1) % 2, e - 1, e - 1 < 2)
            with pe.Fori(1, NE // 4) as i:
                for u in range(4):
                    e = i * 4 + u
                    up(u, u % 2, e, False, i)
                    x_transposes((u + 1) % 2, e + 1, False)
                    down((u - 1) % 4, (u - 1) % 2, e - 1, False)
            down(3, 1, NE - 1, False)

            pe.wait_ge(s["idx_ready"], 1)
            blocks = pe.value_load(ovi[0:1, NOV:NOV + 1], min_val=0, max_val=NOV)
            with pe.Fori(0, NOV) as i:
                with pe.If(i < blocks):
                    pe.wait_ge(s["ov_gathered"], 16 * i + 16)
                    pe.sem_inc(s["pe_passed"], 1)
                    for k in range(KD):
                        ins = nc.tensor.transpose(PS[:, 0, B * k:B * k + B], xg[:, 1, k::KD], ident[0:B, 0:B])
                    ins.then_inc(s["ov_xt_full"], 1)
                    pe.wait_ge(s["ov_xt_ready"], i + 1)
                    pe.wait_ge(s["ov_w"], 16 * LOADS * i + 16 * LOADS)
                    up_products(0, 0).then_inc(s["ov_ab"], 1)
                    pe.wait_ge(s["ov_hid"], i + 1)
                    down_products(0, 0).then_inc(s["ov_y_mm"], 1)

        @block.scalar
        def _(act):
            st = Steps(act, s["act_step"])
            fn = nc.scalar.activation
            junk_at = [None] * 4

            def full(key):
                act.wait_ge(s["psum_full"], UNIT_NO[key] + 1)
                return bank(key)

            def empty(dst, src, func=ACT.Copy, **kw):
                return st.mark(fn(dst, src, func, **kw), s["emptied_act"])

            def sumsq(key, srcs, *after):
                n = norm_rows(key)
                st.after(*after)
                for h, src in enumerate(srcs):
                    w = src.free_size()
                    parts = [h % 4] if w <= 256 else [0, 1, 2, 3]
                    for m in {junk_at[q] for q in parts if junk_at[q]}:
                        st.after(m)
                    q = parts[0]
                    ins = fn(junk[0:n, 256 * q:256 * q + w], src, ACT.Square, accum_out=sums[0:n, NORM_NO[key], h:h + 1])
                    m = st.mark(ins, s["sums_ready"] if h == len(srcs) - 1 else None)
                    for q in parts:
                        junk_at[q] = m

            act.wait_ge(s["x_loaded"], 16 * NT)
            for t, (f, n) in enumerate(TILES):
                sumsq(("x", t), [X[0:n, t, :]])
            act.wait_ge(s["s5_loaded"], 16 * 5)
            fn(s5raw[:, 4, :].rearrange("q (g p) -> q g p", g=2), dtraw[:, :, None].broadcast_to([GP, 2, ST]),
               ACT.Exp).then_inc(s["s5_raw_ready"], 1)
            empty(s5par[:].rearrange("p n q -> p (n q)"), full("par")[:, 0:5 * GP])
            for t, (f, n) in enumerate(TILES):
                for g in range(2):
                    empty(hT[:, 4 * g:4 * g + 4, f:f + n], full(("xT", t, g))[:, 0:4 * n].rearrange("p (k n) -> p k n", k=4))
            act.wait_ge(s["mem_loaded"], 16 * 3)
            for t in range(2):
                sumsq(("m", t), [mem[:, t, :]])
            act.wait_ge(s["s5_scaled"], 1)
            fn(s5tmp[:, 2, :], s5tmp[:, 0, :], ACT.Exp).then_inc(s["s5_mag_ready"], 1)
            for m in range(4):
                empty(uT[:, m, :], full(("u", m))[:, 0:TOK])
            act.wait_ge(s["s5_reduced"], 1)
            fn(s5tmp[:, 5, :], s5tmp[:, 4, :], ACT.Sin).then_inc(s["s5_sin_ready"], 1)
            fn(s5tmp[:, 6, :], s5tmp[:, 4, :], ACT.Sin, scale=0.5).then_inc(s["s5_sin_ready"], 1)
            copied = [empty(qlat[0:n, t, :], full(("ql", t))[0:n, 0:QL]) for t, (f, n) in enumerate(TILES)]
            for t, (f, n) in enumerate(TILES):
                sumsq(("ql", t), [qlat[0:n, t, :]], copied[t])
            copied = [empty(ckv[0:n, KEY_OF_TILE[t], :], full(("kv", t))[0:n, 0:KVL + ROPE]) for t, (f, n) in enumerate(TILES)]
            for t, (f, n) in enumerate(TILES):
                sumsq(("ck", t), [ckv[0:n, KEY_OF_TILE[t], 0:KVL]], copied[t])
            for c in range(2):
                copied = [empty(qmem[0:n, t, 256 * c:256 * c + 256], full((f"qm{c}", t))[0:n, 0:256]) for t, (f, n) in enumerate(TILES)]
            for t, (f, n) in enumerate(TILES):
                sumsq(("qm", t), [qmem[0:n, t, MD * h:MD * h + MD] for h in range(MH)], copied[t])
            act.wait_ge(s["mem_ready"], 2)
            for t in range(2):
                for g in range(2):
                    empty(memT[:, 4 * g:4 * g + 4, 128 * t:128 * t + 128],
                          full(("memT", t, g)).rearrange("p (k n) -> p k n", k=4))
            for name, dst in (("mk", mk), ("mv", mv)):
                for c in range(2):
                    copied = [empty(dst[:, 0, t, 256 * c:256 * c + 256], full((f"{name}{c}", t))[:, 0:256]) for t in range(2)]
            for t in range(2):
                sumsq(("mk", t), [mk[:, 0, t, MD * h:MD * h + MD] for h in range(MH)], copied[t])
            for n in range(4):
                dst = wB[:, n] if n < 2 else wC[:, n - 2]
                empty(dst.rearrange("p t s -> p (t s)"), full(("s5T", n)))
            for src in range(2):
                for kt in range(2):
                    empty(mkT[:, src, :, 128 * kt:128 * kt + 128], full(("mkT", src, kt)).rearrange("p (h n) -> p h n", h=MH))
            for t, (f, n) in enumerate(TILES):
                empty(qmT[:, :, f:f + n], full(("qmT", t))[:, 0:MH * n].rearrange("p (h n) -> p h n", h=MH))

            def attention(kind, units, unit0, oT):
                for step, m in attention_order(units):
                    if step == "OT":
                        f, n = TILES[m]
                        empty(oT[:, :, f:f + n], full((kind, "OT", m))[:, 0:4 * n].rearrange("p (j n) -> p j n", j=4))
                        continue
                    _, t, h0, nh = units[m]
                    n = TILES[t][1]
                    kb = key_blocks(units[m])
                    nk = sum(kb)
                    if step == "S":
                        src = full((kind, "S", m))
                        act.wait_ge(s["scores_max"], unit0 + m + 1)
                        w = (unit0 + m) % 4
                        scale = 1.0 if kind == "mla" and t < 2 else SCALE_MEM if kind == "mem" else SCALE_MLA
                        for h in range(nh):
                            ins = fn(P[0:n, m % 2, nk * h:nk * h + nk], src[0:n, nk * h:nk * h + nk], ACT.Exp,
                                     bias=soft[0:n, w, 0, h:h + 1], scale=scale, accum_out=soft[0:n, w, 1, h:h + 1])
                            st.mark(ins, s["emptied_act"] if h == nh - 1 else None)
                    elif step == "PT":
                        src = full((kind, "PT", m))
                        if kb[-1] == 128:
                            empty(PT[:, m % 2, 0:n * nh * len(kb)], src[:, 0:n * nh * len(kb)])
                        else:
                            whole = n * (len(kb) - 1)
                            st.mark(fn(PT[:, m % 2, 0:whole], src[:, 0:whole], ACT.Copy))
                            empty(PT[0:kb[-1], m % 2, whole:whole + n], src[0:kb[-1], whole:whole + n])

            attention("mem", MEM_UNITS, 0, oTmem)
            act.wait_ge(s["stored"], 16 * 10)
            for t, (f, n) in enumerate(TILES):
                empty(qlT[:, :, f:f + n], full(("qlT", t))[:, 0:3 * n].rearrange("p (k n) -> p k n", k=3))
            for j, (f, n) in enumerate(KEYS):
                empty(ckT[:, :, f:f + n], full(("ckT", j))[:, 0:2 * n].rearrange("p (k n) -> p k n", k=2))
            for m in range(len(KQ_UNITS) + KQ_LAG):
                if m < len(KQ_UNITS):
                    what, j, half = KQ_UNITS[m]
                    src = full(("kq", m))
                    dst = KQ[:, m % KQ_BUFS]
                    if what == "k":
                        n = KEYS[j][1]
                        view = src[0:n, :].rearrange("p (h d) -> p h d", h=4)
                        m1 = st.mark(fn(dst[0:n, :, 0:NOPE], view[:, :, 0:NOPE], ACT.Copy))
                        m2 = st.mark(fn(dst[0:n, :, NOPE:], ckv[0:n, j, None, KVL:].broadcast_to([n, 4, ROPE]), ACT.Copy))
                        empty(V[0:n, j, 256 * half:256 * half + 256].rearrange("p (h d) -> p h d", h=4), view[:, :, NOPE:])
                        sumsq(("kq", m), [dst[0:n, h, :] for h in range(4)], m1, m2)
                    else:
                        n = TILES[j][1]
                        m1 = empty(dst[0:n].rearrange("p h d -> p (h d)"), src[0:n, 0:4 * QK])
                        sumsq(("kq", m), [dst[0:n, h, :] for h in range(4)], m1)
                if m >= KQ_LAG:
                    what, j, half = KQ_UNITS[m - KQ_LAG]
                    f, n = KEYS[j] if what == "k" else TILES[j]
                    dst = kT if what == "k" else qT
                    empty(dst[0:QK, 4 * half:4 * half + 4, f:f + n],
                          full(("kqT", m - KQ_LAG))[0:QK, 0:4 * n].rearrange("p (h n) -> p h n", h=4))
            attention("mla", MLA_UNITS, len(MEM_UNITS), oTmla)
            for b, br in enumerate(("C", "B")):
                for d in range(KD):
                    src = full((f"gate{br}", d))
                    if b or d >= 2:
                        act.wait_ge(*emptied_at(UNIT_NO[(f"out{br}", d - 2) if d >= 2 else ("outC", KD - 2 + d)]))
                    empty(sig[:, d % 2, :], src[:, 0:TOK], ACT.Tanh, scale=0.5)
            act.wait_ge(s["finals_full"], 1)
            st.mark(fn(finrow[:].rearrange("q n p -> q (n p)"), PS[0:GP, BU, :], ACT.Copy), s["finals_out"])
            for t in range(4):
                act.wait_ge(s["y_skipped"], t + 1)
                fn(gelu[:, t, :], uT[:, t, :], ACT.Square).then_inc(s["y_square"], 1)
            for t in range(4):
                act.wait_ge(s["y_inner"], t + 1)
                fn(gelu[:, t, :], gelu[:, t, :], ACT.Tanh, scale=math.sqrt(2 / math.pi)).then_inc(s["y_tanh"], 1)
            for d in range(KD):
                src = full(("glug", d))
                act.wait_ge(*emptied_at(UNIT_NO[("gluv", d - 2) if d >= 2 else ("outB", KD - 2 + d)]))
                if d >= 2:
                    act.wait_ge(s["merged"], d - 1)
                empty(gsig[:, d % 2, :], src[:, 0:TOK], ACT.Tanh, scale=0.5)
                empty(sig[:, d % 2, :], full(("gateA", d))[:, 0:TOK], ACT.Tanh, scale=0.5)
            for t, (f, n) in enumerate(TILES):
                act.wait_ge(*emptied_at(UNIT_NO["wout", 2, t]))
                sumsq(("f", t), [X[0:n, t, :]])
            for t, (f, n) in enumerate(TILES):
                for g in range(2):
                    empty(h2T[:, 4 * g:4 * g + 4, f:f + n], full(("h2T", t, g))[:, 0:4 * n].rearrange("p (k n) -> p k n", k=4))
            act.wait_ge(s["logits_in"], 1)
            fn(ex4[:, 1], ex4[:, 0], ACT.Exp).then_inc(s["logits_exp"], 1)
            act.wait_ge(s["logits_in"], 2)
            fn(rs[:, 5, :], rs[:, 4, :], ACT.Exp).then_inc(s["logits_exp"], 1)
            def x_copy(par, e, first):
                act.wait_ge(s["xt_full"], e + 1)
                if not first:
                    act.wait_ge(s["ab_full"], e - 1)
                fn(xT[:, par].rearrange("p k n -> p (k n)"), PS[:, par, 0:KD * B], ACT.Copy).then_inc(s["xt_ready"], 1)

            def gate(par, e, first):
                act.wait_ge(s["ab_full"], e + 1)
                if not first:
                    act.wait_ge(s["hid_ready"], e - 1)
                fn(tg[:, par].rearrange("p j n -> p (j n)"), PS[:, 2 + par, 0:2 * B], ACT.Tanh, scale=0.5)\
                    .then_inc(s["tanh_ready"], 1)

            def y_copy(par, e, first):
                act.wait_ge(s["y_mm"], e + 1)
                if not first:
                    act.wait_ge(s[f"y_stored{par}"], 8 * (e - par))
                fn(yb[:, par, 0:512], PS[0:B, 4 + 2 * par, :], ACT.Copy).then_inc(s["y_act"], 1)

            x_copy(0, 0, True)
            for e in range(4):
                gate(e % 2, e, e < 2)
                x_copy((e + 1) % 2, e + 1, e + 1 < 2)
                if e > 0:
                    y_copy((e - 1) % 2, e - 1, e - 1 < 2)
            with act.Fori(1, NE // 4) as i:
                for u in range(4):
                    e = i * 4 + u
                    gate(u % 2, e, False)
                    x_copy((u + 1) % 2, e + 1, False)
                    y_copy((u - 1) % 2, e - 1, False)
            y_copy(1, NE - 1, False)
            act.wait_ge(s["idx_ready"], 1)
            blocks = act.value_load(ovi[0:1, NOV:NOV + 1], min_val=0, max_val=NOV)
            with act.Fori(0, NOV) as i:
                with act.If(i < blocks):
                    act.wait_ge(s["ov_xt_full"], i + 1)
                    fn(xT[:, 0].rearrange("p k n -> p (k n)"), PS[:, 0, 0:KD * B], ACT.Copy).then_inc(s["ov_xt_ready"], 1)
                    act.wait_ge(s["ov_ab"], i + 1)
                    fn(tg[:, 0].rearrange("p j n -> p (j n)"), PS[:, 2, 0:2 * B], ACT.Tanh, scale=0.5).then_inc(s["ov_tanh"], 1)
                    act.wait_ge(s["y_stored0"], 8 * NE)
                    act.wait_ge(s["ov_stored"], i * 16)
                    act.wait_ge(s["ov_y_mm"], i + 1)
                    fn(yb[:, 0, 0:512], PS[0:B, 4, :], ACT.Copy).then_inc(s["ov_y_act"], 1)

        @block.vector
        def _(dve):
            st = Steps(dve, s["dve_step"])
            V_ = nc.vector

            def full(key):
                dve.wait_ge(s["psum_full"], UNIT_NO[key] + 1)
                return bank(key)

            def link(ins, sem_=None):
                st.after(st.mark(ins, sem_))

            def norm(key):
                dve.wait_ge(s["rstd_ready"], NORM_NO[key] + 1)
                return rstd[0:norm_rows(key), NORM_NO[key], 0:NORM_HEADS[key[0]]]

            def scaled_rows(dst, src, r, gain, ready):
                V_.scalar_tensor_tensor(dst, src, r, gain, ALU.mult, ALU.mult).then_inc(ready, 1)

            def scaled_heads(rows_, key, heads, gain, ready):
                n = norm_rows(key)
                d = gain.shape[1]
                r = norm(key)
                link(V_.tensor_tensor(rows_, rows_, r[:, :, None].broadcast_to([n, heads, d]), ALU.mult))
                return V_.tensor_tensor(rows_, rows_, gain[0:n, None, :].broadcast_to([n, heads, d]), ALU.mult)

            dve.wait_ge(s["gains_loaded"], 16 * 7)
            for t, (f, n) in enumerate(TILES):
                scaled_rows(Hn[0:n, t, :], X[0:n, t, :], norm(("x", t)), grow[0:n, :], s["h_ready"])
            gmem = memT[:, 0:4, :].rearrange("p k n -> p (k n)")
            dve.wait_ge(s["mem_loaded"], 16 * 3)
            for t in range(2):
                scaled_rows(mem[:, t, :], mem[:, t, :], norm(("m", t)), gmem, s["mem_ready"])
            dve.wait_ge(s["s5_den"], 1)
            V_.reciprocal(s5tmp[:, 11, :], s5tmp[:, 10, :]).then_inc(s["s5_rden"], 1)
            for t, (f, n) in enumerate(TILES):
                scaled_rows(qlat[0:n, t, :], qlat[0:n, t, :], norm(("ql", t)), g_ql[0:n], s["ql_ready"])
            for t, (f, n) in enumerate(TILES):
                c = ckv[0:n, KEY_OF_TILE[t], 0:KVL]
                scaled_rows(c, c, norm(("ck", t)), g_kv[0:n], s["ck_ready"])
            for t, (f, n) in enumerate(TILES):
                scaled_heads(qmem[0:n, t].rearrange("p (h d) -> p h d", h=MH), ("qm", t), MH, g_mq, None).then_inc(s["qm_ready"], 1)
            for t in range(2):
                scaled_heads(mk[:, 0, t].rearrange("p (h d) -> p h d", h=MH), ("mk", t), MH, g_mk, None).then_inc(s["mk_ready"], 1)

            def s5_turn(q):
                def win(x):
                    return x.rearrange("p (w j) -> p w j", j=WIN)

                cb = cosT[:, q, None, :].broadcast_to([128, NWIN, WIN])
                sb_ = sinT[:, q, None, :].broadcast_to([128, NWIN, WIN])
                if q == 0:
                    dve.wait_ge(s["s5_tables"], 1)
                dve.wait_ge(s["bu_full"], q + 1)
                re, im = PS[:, BU, 0:TOK], PS[:, BU + 1, 0:TOK]
                m1 = st.mark(V_.tensor_tensor(win(rotA[:, 0]), win(re), cb, ALU.mult))
                m2 = st.mark(V_.tensor_tensor(win(rotB[:, 0]), win(im), sb_, ALU.mult))
                m3 = st.mark(V_.tensor_tensor(win(rotA[:, 1]), win(im), cb, ALU.mult))
                m4 = st.mark(V_.tensor_tensor(win(rotB[:, 1]), win(re), sb_, ALU.mult), s["bu_free"])
                st.after(m2)
                m5 = st.mark(V_.tensor_tensor(rotA[:, 0], rotA[:, 0], rotB[:, 0], ALU.add))
                st.after(m4, m3)
                m6 = st.mark(V_.tensor_tensor(rotA[:, 1], rotA[:, 1], rotB[:, 1], ALU.subtract))
                mag = s5tmp[:, 2, q:q + 1].broadcast_to([128, WIN])

                def scan(w, c, initial):
                    return st.mark(V_.tensor_tensor_scan(rotB[:, c, WIN * w:WIN * w + WIN], mag, rotA[:, c, WIN * w:WIN * w + WIN],
                                                         initial, ALU.mult, ALU.add))

                st.after(m6)
                last = [scan(0, 0, 0.0), scan(0, 1, 0.0)]
                sample = [scan(NWIN - 1, c, s5par[:, 2 + c, q:q + 1]) for c in range(2)]
                for w in range(1, NWIN - 1):
                    end = slice(WIN * w - 1, WIN * w)
                    c64, s64, n64 = cosT[:, q, WIN - 1:WIN], sinT[:, q, WIN - 1:WIN], s5tmp[:, 8, q:q + 1]
                    cr = carry[:, q % 2, w - 1]
                    st.after(last[1])
                    m7 = st.mark(V_.tensor_scalar(cr[:, 0:2], rotB[:, :, end].rearrange("p c o -> p (c o)"), c64, None, ALU.mult))
                    st.after(m7)
                    st.mark(V_.scalar_tensor_tensor(cr[:, 2:3], rotB[:, 1, end], n64, cr[:, 0:1], ALU.mult, ALU.add))
                    m8 = st.mark(V_.scalar_tensor_tensor(cr[:, 3:4], rotB[:, 0, end], s64, cr[:, 1:2], ALU.mult, ALU.add))
                    st.after(m8)
                    last = [scan(w, c, cr[:, 2 + c:3 + c]) for c in range(2)]
                st.after(last[1])
                dst = hS[:, q % 2]
                m1 = st.mark(V_.tensor_tensor(win(rotA[:, 0]), win(rotB[:, 0]), cb, ALU.mult))
                m2 = st.mark(V_.tensor_tensor(win(rotC[:, 0]), win(rotB[:, 1]), sb_, ALU.mult))
                m3 = st.mark(V_.tensor_tensor(win(rotA[:, 1]), win(rotB[:, 1]), cb, ALU.mult))
                m4 = st.mark(V_.tensor_tensor(win(rotC[:, 1]), win(rotB[:, 0]), sb_, ALU.mult))
                if q >= 2:
                    dve.wait_ge(s["y_full"], q - 1)
                st.after(m2)
                m5 = st.mark(V_.tensor_tensor(dst[:, 0], rotA[:, 0], rotC[:, 0], ALU.subtract))
                st.after(m4)
                m6 = st.mark(V_.tensor_tensor(dst[:, 1], rotA[:, 1], rotC[:, 1], ALU.add), s["h_state"])
                st.after(m6)
                st.mark(V_.tensor_copy(finals[:, :, :, q].rearrange("p s c -> p c s"), dst[:, :, SEQ - 1:TOK:DEC]), s["finals_copied"])
                if q % 4 == 0 and q > 0:
                    y_skip(q // 4 - 1)

            def y_skip(t):
                dve.wait_ge(s["y_full"], 4 * t + 4)
                V_.scalar_tensor_tensor(uT[:, t, :], uT[:, t, :], dskip[:, t:t + 1], PS[:, YB, 0:TOK], ALU.mult, ALU.add)\
                    .then_inc(s["y_skipped"], 1)

            dve.wait_ge(s["params_loaded"], 16 * 7)
            turns = S5Turns(s5_turn, S5_EVERY)

            def attention(kind, units, unit0):
                for step, m in attention_order(units):
                    if step not in ("S", "O"):
                        continue
                    _, t, h0, nh = units[m]
                    n = TILES[t][1]
                    nk = sum(key_blocks(units[m]))
                    w = soft[0:n, (unit0 + m) % 4]
                    if step == "S":
                        src = full((kind, "S", m))[0:n, 0:nh * nk]
                        heads = src.rearrange("p (h k) -> p h k", h=nh)
                        if kind == "mla" and t < 2:
                            mask = const(f"mask{t}")[0:n, None, :].broadcast_to([n, nh, nk])
                            link(V_.scalar_tensor_tensor(heads, heads, SCALE_MLA, mask, ALU.mult, ALU.add))
                            V_.tensor_reduce(w[:, 0, 0:nh], heads, AX.X, ALU.max, negate=True).then_inc(s["scores_max"], 1)
                        else:
                            link(V_.tensor_reduce(w[:, 0, 0:nh], heads, AX.X, ALU.max, negate=True))
                            V_.tensor_scalar(w[:, 0, 0:nh], w[:, 0, 0:nh], SCALE_MEM if kind == "mem" else SCALE_MLA, None, ALU.mult)\
                                .then_inc(s["scores_max"], 1)
                        turns.beat()
                    else:
                        dv = MD if kind == "mem" else VH
                        src = full((kind, "O", m))[0:n, 0:nh * dv].rearrange("p (h d) -> p h d", h=nh)
                        link(V_.reciprocal(w[:, 2, 0:nh], w[:, 1, 0:nh]))
                        st.mark(V_.tensor_tensor(O[0:n, t, dv * h0:dv * (h0 + nh)].rearrange("p (h d) -> p h d", h=nh), src,
                                                 w[:, 2, 0:nh, None].broadcast_to([n, nh, dv]), ALU.mult), s["emptied_dve"])

            for _ in range(4 + NT):
                turns.beat()
            attention("mem", MEM_UNITS, 0)
            for _ in range(NT + len(KEYS)):
                turns.beat()
            for m in range(len(KQ_UNITS) + KQ_LAG):
                if m < len(KQ_UNITS):
                    what, j, half = KQ_UNITS[m]
                    n = KEYS[j][1] if what == "k" else TILES[j][1]
                    where = POS_OF_KEY[j if what == "k" else KEY_OF_TILE[j]]
                    x = KQ[0:n, m % KQ_BUFS]
                    link(scaled_heads(x, ("kq", m), 4, g_kn if what == "k" else g_qn, None))
                    r = x[:, :, NOPE:]
                    hr = ROPE // 2
                    a_, b_ = ropet[0:n, m % 2, 0], ropet[0:n, m % 2, 1]
                    cos_, sin_ = rope[0:n, where, 0, None, :], rope[0:n, where, 1, None, :]
                    st.mark(V_.tensor_tensor(a_, r, cos_.broadcast_to([n, 4, ROPE]), ALU.mult))
                    st.mark(V_.tensor_tensor(b_[:, :, 0:hr], r[:, :, hr:], sin_[:, :, 0:hr].broadcast_to([n, 4, hr]), ALU.mult))
                    link(V_.tensor_tensor(b_[:, :, hr:], r[:, :, 0:hr], sin_[:, :, hr:].broadcast_to([n, 4, hr]), ALU.mult))
                    V_.tensor_tensor(r, a_, b_, ALU.add).then_inc(s["kq_ready"], 1)
                turns.beat()
            attention("mla", MLA_UNITS, len(MEM_UNITS))

            for b, br in enumerate(("C", "B")):
                for d in range(KD):
                    src = full((f"out{br}", d))[:, 0:TOK]
                    dve.wait_ge(*emptied_at(UNIT_NO[f"gate{br}", d]))
                    dst = mtmp[:, d % 2, :] if b else mergedT[:, d, :]
                    link(V_.scalar_tensor_tensor(dst, sig[:, d % 2, :], 1.0, src, ALU.add, ALU.mult), s["emptied_dve"])
                    if b:
                        st.mark(V_.tensor_tensor(mergedT[:, d, :], mergedT[:, d, :], dst, ALU.add))
                    turns.beat()
            turns.finish()
            y_skip(3)
            for t in range(4):
                dve.wait_ge(s["y_square"], t + 1)
                link(V_.tensor_scalar(gelu[:, t, :], gelu[:, t, :], 0.044715, 1.0, ALU.mult, ALU.add))
                V_.tensor_tensor(gelu[:, t, :], gelu[:, t, :], uT[:, t, :], ALU.mult).then_inc(s["y_inner"], 1)
            for t in range(4):
                dve.wait_ge(s["y_tanh"], t + 1)
                link(V_.tensor_scalar(gelu[:, t, :], gelu[:, t, :], 0.5, 0.5, ALU.mult, ALU.add))
                V_.tensor_tensor(uT[:, t, :], gelu[:, t, :], uT[:, t, :], ALU.mult).then_inc(s["z_ready"], 1)
            for d in range(KD):
                src = full(("gluv", d))[:, 0:TOK]
                dve.wait_ge(*emptied_at(UNIT_NO["glug", d]))
                m = mtmp[:, d % 2, :]
                link(V_.scalar_tensor_tensor(m, gsig[:, d % 2, :], 1.0, src, ALU.add, ALU.mult), s["emptied_dve"])
                dve.wait_ge(*emptied_at(UNIT_NO["gateA", d]))
                link(V_.scalar_tensor_tensor(m, sig[:, d % 2, :], 1.0, m, ALU.add, ALU.mult))
                V_.scalar_tensor_tensor(mergedT[:, d, :], m, 0.5, mergedT[:, d, :], ALU.mult, ALU.add).then_inc(s["merged"], 1)
            for g, (d0, nd) in enumerate(DGROUPS):
                for t, (f, n) in enumerate(TILES):
                    src = full(("wout", g, t))[0:n, 0:128 * nd]
                    x = X[0:n, t, 128 * d0:128 * (d0 + nd)]
                    st.mark(V_.scalar_tensor_tensor(x, src, 0.5, x, ALU.mult, ALU.add), s["emptied_dve"])
            dve.wait_ge(s["gffn_loaded"], 16)
            for t, (f, n) in enumerate(TILES):
                scaled_rows(h2[0:n, t, :], X[0:n, t, :], norm(("f", t)), grow[0:n, :], s["h2_ready"])

            link(V_.memset(lg[:], NEG))
            dve.wait_ge(s["router_loaded"], 16 * 4)
            for t, (f, n) in enumerate(TILES):
                src = full(("route", t))
                st.mark(V_.tensor_tensor(lg[0:n, t, 0:NG], src[0:n, 0:NG], brow[0:n, 0:NG], ALU.add))
                link(V_.tensor_tensor(lg[0:n, t, 8:40], src[0:n, NG:NG + NE], brow[0:n, NG:], ALU.add), s["emptied_dve"])
            for t in range(NT):
                st.mark(V_.max(r8[:, 0, t, :], lg[:, t, 0:8]))
            st.after((s["dve_step"], st.count[s["dve_step"]]))
            for t in range(NT):
                st.mark(V_.max_index(i8[:, 0, t, :], r8[:, 0, t, :], lg[:, t, 0:8]))
            V_.tensor_tensor(ex4[:, 0], lg[:, :, 0:NG], r8[:, 0, :, 0:1].broadcast_to([128, NT, NG]), ALU.subtract)\
                .then_inc(s["logits_in"], 1)
            st.after((s["dve_step"], st.count[s["dve_step"]]))
            link(V_.tensor_copy(rs[:, 0, :], i8[:, 0, :, 0]))
            link(V_.tensor_tensor(ex4[:, 2], const("iotae")[:, None, 0:NG].broadcast_to([128, NT, NG]),
                                  rs[:, 0, :, None].broadcast_to([128, NT, NG]), ALU.is_equal))
            link(V_.tensor_tensor(prod[:], lg[:, :, 8:40].rearrange("p t (g e) -> p t e g", g=NG),
                                  ex4[:, 2, :, None, :].broadcast_to([128, NT, EPG, NG]), ALU.mult))
            link(V_.tensor_reduce(r8[:, 1], prod[:], AX.X, ALU.add))
            for t in range(NT):
                st.mark(V_.max(r8[:, 2, t, :], r8[:, 1, t, :]))
            st.after((s["dve_step"], st.count[s["dve_step"]]))
            for t in range(NT):
                st.mark(V_.max_index(i8[:, 1, t, :], r8[:, 2, t, :], r8[:, 1, t, :]))
            V_.tensor_tensor(rs[:, 4, :], r8[:, 2, :, 1], r8[:, 2, :, 0], ALU.subtract).then_inc(s["logits_in"], 1)
            st.after((s["dve_step"], st.count[s["dve_step"]]))
            for k in range(2):
                st.mark(V_.tensor_copy(rs[:, 1 + k, :], i8[:, 1, :, k]))
            st.after((s["dve_step"], st.count[s["dve_step"]]))
            iotae = const("iotae")[:, None, :].broadcast_to([128, NT, NE])

            def spread(x, m):
                return x[:, :, None].broadcast_to([128, NT, m])

            def row(x):
                return x[:, None, :].broadcast_to([128, NT, NE])

            for k in range(2):
                link(V_.scalar_tensor_tensor(rs[:, 1 + k, :], rs[:, 0, :], float(EPG), rs[:, 1 + k, :], ALU.mult, ALU.add))
                link(V_.tensor_tensor(Ek[:, k], iotae, spread(rs[:, 1 + k, :], NE), ALU.is_equal))
                link(V_.tensor_tensor(Ek[:, k], Ek[:, k], spread(const("valid"), NE), ALU.mult))
            V_.tensor_tensor(Ek[:, 2], Ek[:, 0], Ek[:, 1], ALU.add).then_inc(s["onehot_ready"], 1)
            dve.wait_ge(s["logits_exp"], 2)
            link(V_.tensor_reduce(rs[:, 8, :], ex4[:, 1], AX.X, ALU.add))
            link(V_.reciprocal(rs[:, 9, :], rs[:, 8, :]))
            link(V_.tensor_scalar(rs[:, 10, :], rs[:, 5, :], 1.0, None, ALU.add))
            link(V_.reciprocal(rs[:, 11, :], rs[:, 10, :]))
            link(V_.scalar_tensor_tensor(rs[:, 6, :], rs[:, 11, :], 0.5, rs[:, 9, :], ALU.mult, ALU.mult))
            link(V_.tensor_tensor(rs[:, 7, :], rs[:, 6, :], rs[:, 5, :], ALU.mult))
            src = full("rank")
            R, J, BK, T1 = rk[:, 0], rk[:, 1], rk[:, 2], rk[:, 3]
            n_, nb, incl, excl = cnt[:, 0], cnt[:, 1], cnt[:, 2], cnt[:, 3]
            st.mark(V_.tensor_copy(R.rearrange("p t e -> p (t e)"), src[:, 0:NT * NE]))
            link(V_.tensor_copy(n_, src[:, NT * NE:NT * NE + NE]), s["emptied_dve"])
            link(V_.tensor_scalar(J, R, float(B), None, ALU.is_ge))
            link(V_.tensor_scalar(nb, n_, float(B), None, ALU.is_gt))
            for j in range(2, NJ + 1):
                link(V_.scalar_tensor_tensor(J, R, float(B * j), J, ALU.is_ge, ALU.add))
                link(V_.scalar_tensor_tensor(nb, n_, float(B * j), nb, ALU.is_gt, ALU.add))
            link(V_.tensor_tensor_scan(incl, const("ones")[:, 0:NE], nb, 0.0, ALU.mult, ALU.add))
            link(V_.tensor_tensor(excl, incl, nb, ALU.subtract))
            link(V_.scalar_tensor_tensor(R, J, -float(B), R, ALU.mult, ALU.add))
            link(V_.tensor_tensor(cnt[:, 4], excl, const("iotae"), ALU.subtract))
            link(V_.tensor_scalar(cnt[:, 4], cnt[:, 4], float(NE - 1), None, ALU.add))
            link(V_.tensor_tensor(BK, J, row(cnt[:, 4]), ALU.add))
            link(V_.tensor_scalar(T1, J, 0.5, None, ALU.is_gt))
            link(V_.tensor_tensor(BK, BK, T1, ALU.mult))
            link(V_.tensor_tensor(BK, BK, iotae, ALU.add))
            for k in range(2):
                link(V_.tensor_tensor(tp[:, 2 * k], Ek[:, k], R, ALU.mult))
                link(V_.tensor_reduce(rs[:, 12 + k, :], tp[:, 2 * k], AX.X, ALU.add))
                link(V_.tensor_tensor(tp[:, 2 * k + 1], Ek[:, k], BK, ALU.mult))
                link(V_.tensor_reduce(rs[:, 14 + k, :], tp[:, 2 * k + 1], AX.X, ALU.add))
                link(V_.scalar_tensor_tensor(rs[:, 16 + k, :], rs[:, 14 + k, :], float(B), rs[:, 12 + k, :], ALU.mult, ALU.add))
                link(V_.tensor_copy(pos[:, k, :], rs[:, 16 + k, :]))
                link(V_.tensor_tensor(ohs[:, k], const("iotab")[:, None, :].broadcast_to([128, NT, B]),
                                      spread(rs[:, 12 + k, :], B), ALU.is_equal))
                link(V_.tensor_tensor(ohb[:, 2 + k], const("iotablk")[:, None, :].broadcast_to([128, NT, NBLK]),
                                      spread(rs[:, 14 + k, :], NBLK), ALU.is_equal))
                ins = V_.tensor_tensor(ohb[:, k], ohb[:, 2 + k], spread(const("tokid"), NBLK), ALU.mult)
                if k == 0:
                    link(ins)
                else:
                    ins.then_inc(s["tables_in"], 1)
            link(V_.tensor_tensor(ovcmp[:], incl[0:1, None, :].broadcast_to([1, NOV, NE]),
                                  const("iotablk")[0:1, 0:NOV, None].broadcast_to([1, NOV, NE]), ALU.is_le))
            link(V_.tensor_reduce(ovf[:, 0, :], ovcmp[:], AX.X, ALU.add))
            link(V_.tensor_scalar(ovf[:, 1, :], ovf[:, 0, :], float(NE - 1), None, ALU.min))
            link(V_.tensor_copy(ovi[:, 0:NOV], ovf[:, 1, :]))
            link(V_.tensor_copy(ovi[:, NOV:], incl[0:1, NE - 1:NE]))
            link(V_.tensor_copy(idx[:], full("table")[0:B, 0:NBLK]), s["emptied_dve"])
            V_.tensor_copy(rs[0:1, 20, 0:1], rs[0:1, 16, 0:1]).then_inc(s["idx_ready"], 1)

            def hidden(par, e, first):
                dve.wait_ge(s["tanh_ready"], e + 1)
                if not first:
                    dve.wait_ge(s["y_mm"], e - 1)
                hidden_products(par, s["dve_moe"], e, s["hid_ready"])

            def hidden_products(par, half, e, ready):
                x1 = PS[:, 2 + par, 0:2 * B]
                x3 = PS[:, 2 + par, 2 * B:4 * B]
                u_ = ug[:, par].rearrange("p j n -> p (j n)")
                V_.scalar_tensor_tensor(u_, tg[:, par].rearrange("p j n -> p (j n)"), 1.0, x1, ALU.add, ALU.mult).then_inc(half, 1)
                dve.wait_ge(half, e + 1)
                V_.tensor_tensor(hid[:, par].rearrange("p j n -> p (j n)"), u_, x3, ALU.mult).then_inc(ready, 1)

            def y_copy(par, e, first):
                dve.wait_ge(s["y_mm"], e + 1)
                if not first:
                    dve.wait_ge(s[f"y_stored{par}"], 8 * (e - par))
                V_.tensor_copy(yb[:, par, 512:], PS[0:B, 5 + 2 * par, :]).then_inc(s["y_dve"], 1)

            for e in range(4):
                hidden(e % 2, e, e < 2)
                if e > 0:
                    y_copy((e - 1) % 2, e - 1, e - 1 < 2)
            with dve.Fori(1, NE // 4) as i:
                for u in range(4):
                    e = i * 4 + u
                    hidden(u % 2, e, False)
                    y_copy((u - 1) % 2, e - 1, False)
            y_copy(1, NE - 1, False)
            blocks = dve.value_load(ovi[0:1, NOV:NOV + 1], min_val=0, max_val=NOV)
            with dve.Fori(0, NOV) as i:
                with dve.If(i < blocks):
                    dve.wait_ge(s["ov_tanh"], i + 1)
                    hidden_products(0, s["ov_half"], i, s["ov_hid"])
                    dve.wait_ge(s["y_stored0"], 8 * NE)
                    dve.wait_ge(s["ov_stored"], i * 16)
                    dve.wait_ge(s["ov_y_mm"], i + 1)
                    V_.tensor_copy(yb[:, 0, 512:], PS[0:B, 5, :]).then_inc(s["ov_y_dve"], 1)
            for t, (f, n) in enumerate(TILES):
                dve.wait_ge(s[f"rows_gathered{t}"], 32)
                link(V_.scalar_tensor_tensor(X[0:n, t, :], rows[0:n, 0, t, :], rs[0:n, 6, t:t + 1], X[0:n, t, :], ALU.mult, ALU.add))
                V_.scalar_tensor_tensor(X[0:n, t, :], rows[0:n, 1, t, :], rs[0:n, 7, t:t + 1], X[0:n, t, :], ALU.mult, ALU.add)\
                    .then_inc(s["out_ready"], 1)

        @block.gpsimd
        def _(pool):
            st = Steps(pool, s["pool_step"])
            g_ = nc.gpsimd

            def link(ins, sem_=None):
                st.after(st.mark(ins, sem_))

            def norms(first, last):
                for n in range(first, last):
                    key = NORMS[n]
                    rows_, heads = norm_rows(key), NORM_HEADS[key[0]]
                    pool.wait_ge(s["sums_ready"], n + 1)
                    link(g_.tensor_scalar(means[0:rows_, n, 0:heads], sums[0:rows_, n, 0:heads], 1.0 / NORM_WIDTH[key[0]], EPS, ALU.mult, ALU.add))
                    g_.tensor_tensor(rstd[0:rows_, n, 0:heads], means[0:rows_, n, 0:heads], const("half")[0:rows_, 0:heads], ALU.pow)\
                        .then_inc(s["rstd_ready"], 1)

            pool.wait_ge(s["const_loaded"], 16)
            norms(0, NORM_NO["m", 0])

            are, aim, dt = s5par[:, 0, :], s5par[:, 1, :], s5par[:, 4, :]
            tmp = [s5tmp[:, n, :] for n in range(24)]
            pool.wait_ge(*emptied_at(UNIT_NO["par"]))
            tt, ts = g_.tensor_tensor, g_.tensor_scalar
            link(tt(tmp[0], are, dt, ALU.mult), s["s5_scaled"])
            link(tt(tmp[1], aim, dt, ALU.mult))
            two_pi = 2 * math.pi
            link(ts(tmp[3], tmp[1], 1.0 / two_pi, None, ALU.mult))
            link(ts(tmp[3], tmp[3], 12582912.0, None, ALU.add))
            link(ts(tmp[3], tmp[3], 12582912.0, None, ALU.subtract))
            c1 = 6.28125
            c2 = float(np.float32(np.round((two_pi - c1) * 2 ** 21) / 2 ** 21))
            c3 = two_pi - c1 - c2
            src = tmp[1]
            for c in (c1, c2, c3):
                link(ts(tmp[9], tmp[3], c, None, ALU.mult))
                link(tt(tmp[4], src, tmp[9], ALU.subtract))
                src = tmp[4]
            link(ts(tmp[4], tmp[4], 3.141592, -3.141592, ALU.min, ALU.max), s["s5_reduced"])
            link(tt(tmp[9], are, are, ALU.mult))
            link(tt(tmp[10], aim, aim, ALU.mult))
            link(tt(tmp[10], tmp[9], tmp[10], ALU.add), s["s5_den"])
            norms(NORM_NO["m", 0], NORMS_BEFORE_S5)
            pool.wait_ge(s["s5_sin_ready"], 2)
            link(tt(tmp[7], tmp[6], tmp[6], ALU.mult))
            link(ts(tmp[7], tmp[7], -2.0, 1.0, ALU.mult, ALU.add))
            pool.wait_ge(s["s5_mag_ready"], 1)
            link(tt(tmp[14], tmp[2], tmp[7], ALU.mult))
            link(tt(tmp[15], tmp[2], tmp[5], ALU.mult))
            link(ts(tmp[16], tmp[14], -1.0, None, ALU.add))
            pool.wait_ge(s["s5_rden"], 1)
            for out, x, y, op in ((12, are, aim, ALU.add), (13, None, None, ALU.subtract)):
                if out == 12:
                    link(tt(tmp[17], tmp[16], are, ALU.mult))
                    link(tt(tmp[18], tmp[15], aim, ALU.mult))
                else:
                    link(tt(tmp[17], tmp[15], are, ALU.mult))
                    link(tt(tmp[18], tmp[16], aim, ALU.mult))
                link(tt(tmp[17], tmp[17], tmp[18], op))
                link(tt(tmp[out], tmp[17], tmp[11], ALU.mult))
            pool.wait_ge(s["psum_full"], UNIT_NO["xT", NT - 1, 1] + 1)
            pool.wait_ge(s["params_loaded"], 16 * 7)
            fre, fim = (x[:, :, None].broadcast_to([128, GP, CH]) for x in (tmp[12], tmp[13]))
            br, bi = braw[:, 0], braw[:, 1]
            for c, (p0, p1, op) in enumerate((((fre, br), (fim, bi), ALU.subtract), ((fre, bi), (fim, br), ALU.add))):
                st.mark(tt(btmp[:, 2 * c], p0[0], p0[1], ALU.mult))
                link(tt(btmp[:, 2 * c + 1], p1[0], p1[1], ALU.mult))
                link(tt(bbar[:, c], btmp[:, 2 * c], btmp[:, 2 * c + 1], op))
                st.mark(ts(bpad[:, c, :, 0, :], bbar[:, c], const("sel_b")[:, 0:1], None, ALU.mult))
                st.mark(ts(bpad[:, c, :, 1, :], bbar[:, c], const("sel_b")[:, 1:2], None, ALU.mult), s["s5_padded"])
            for c in range(2):
                st.mark(ts(cpad[:, c, :, 0, :], craw[:, c], const("sel_c")[:, 2 * c:2 * c + 1], None, ALU.mult))
                st.mark(ts(cpad[:, c, :, 1, :], craw[:, c], const("sel_c")[:, 2 * c + 1:2 * c + 2], None, ALU.mult), s["s5_padded"])
            st.mark(g_.tensor_copy(cosT[:, :, 0], tmp[7]))
            link(g_.tensor_copy(sinT[:, :, 0], tmp[5]))
            flat = btmp[:].rearrange("p n q c -> p (n q c)")
            n = 1
            while n < WIN:
                t1 = flat[:, 0:GP * n].rearrange("p (q j) -> p q j", q=GP)
                t2 = flat[:, 512:512 + GP * n].rearrange("p (q j) -> p q j", q=GP)
                cn, sn = (x[:, :, n - 1:n].broadcast_to([128, GP, n]) for x in (cosT, sinT))
                c0, s0 = cosT[:, :, 0:n], sinT[:, :, 0:n]
                st.mark(tt(t1, c0, cn, ALU.mult))
                link(tt(t2, s0, sn, ALU.mult))
                link(tt(cosT[:, :, n:2 * n], t1, t2, ALU.subtract))
                st.mark(tt(t1, s0, cn, ALU.mult))
                link(tt(t2, c0, sn, ALU.mult))
                link(tt(sinT[:, :, n:2 * n], t1, t2, ALU.add))
                n *= 2
            link(ts(tmp[8], sinT[:, :, WIN - 1], -1.0, None, ALU.mult), s["s5_tables"])
            norms(NORMS_BEFORE_S5, len(NORMS))

            pool.wait_ge(s["h2_stored"], 16 * NT)
            pool.wait_ge(s["idx_ready"], 1)
            for e in range(NE + 1):
                if e >= 2:
                    pool.wait_ge(s["xt_full"], e - 1)
                g_.indirect_dma_start(xg[:, e % 2, :], None, scratch["h2"], bass.IndirectOffsetOnAxis(ap=idx[:, e:e + 1], axis=0))\
                    .then_inc(s[f"gathered{e % 2}"], 16)
            blocks = pool.value_load(ovi[0:1, NOV:NOV + 1], min_val=0, max_val=NOV)
            pool.wait_ge(s["xt_full"], NE)
            with pool.Fori(0, NOV) as i:
                with pool.If(i < blocks):
                    pool.wait_ge(s["ov_xt_full"], i)
                    g_.tensor_copy(idx_ov[:, 0:1], idx[:, bass.ds(i + NE, 1)]).then_inc(s["ov_idx"], 1)
                    pool.wait_ge(s["ov_idx"], i + 1)
                    pool.sem_inc(s["pool_passed"], 1)
                    g_.indirect_dma_start(xg[:, 1, :], None, scratch["h2"], bass.IndirectOffsetOnAxis(ap=idx_ov[:, 0:1], axis=0))\
                        .then_inc(s["ov_gathered"], 16)
            pool.wait_ge(s["y_filled"], 16 * len(FILLS))
            pool.wait_ge(s["y_stored0"], 8 * NE)
            pool.wait_ge(s["y_stored1"], 8 * NE)
            pool.wait_ge(s["ov_stored"], blocks * 16)
            pool.sem_inc(s["pool_passed"], 1)
            for t, (f, n) in enumerate(TILES):
                for k in range(2):
                    g_.indirect_dma_start(rows[0:n, k, t, :], None, scratch["y"], bass.IndirectOffsetOnAxis(ap=pos[0:n, k, t:t + 1], axis=0))\
                        .then_inc(s[f"rows_gathered{t}"], 16)


NAMES = ["x_prompt", "x_sample", "cache_mla_ckv", "cache_mla_kpe", "cache_ssm_re", "cache_ssm_im", "cache_mem_k",
         "cache_mem_v", "mem_prompt", "g_attn", "w_in", "ssm_a_re", "ssm_a_im", "ssm_log_dt", "ssm_b_re", "ssm_b_im",
         "ssm_c_re", "ssm_c_im", "ssm_d", "w_glu", "g_qlat", "w_uq", "g_kvlat", "w_ukv", "g_qn", "g_kn", "w_o_mla",
         "g_mem", "w_mem_kv", "g_mqn", "g_mkn", "w_o_mem", "w_out", "g_ffn", "w_rg", "b_rg", "w_re", "b_re", "w_e1",
         "w_e3", "w_e2"]
OUTPUTS = [("y_p", (SEQ, D), (1, SEQ, D)), ("y_s", (DEC, D), (1, DEC, D)),
           ("ckv_p", (SEQ, KVL), (1, 1, SEQ, KVL)), ("kpe_p", (SEQ, ROPE), (1, 1, SEQ, ROPE)),
           ("sre_p", (GP, 128), (1, 1, G, ST)), ("sim_p", (GP, 128), (1, 1, G, ST)),
           ("mem_k", (MEMT, MH * MD), (1, 1, MEMT, MH, MD)), ("mem_v", (MEMT, MH * MD), (1, 1, MEMT, MH, MD)),
           ("ckv_s", (DEC, KVL), (1, 1, DEC, KVL)), ("kpe_s", (DEC, ROPE), (1, 1, DEC, ROPE)),
           ("sre_s", (GP, 128), (1, 1, G, ST)), ("sim_s", (GP, 128), (1, 1, G, ST))]


def kernel(**inputs):
    import concourse.bacc as bacc
    from concourse.bass_utils import run_bass_kernel_spmd

    nc = bacc.Bacc("TRN2", target_bir_lowering=False, num_devices=1)
    arrays = {f"in_{name}": np.ascontiguousarray(inputs[name]) for name in NAMES}
    arrays["in_consts"] = constants()
    a = {name[3:]: nc.dram_tensor(name, x.shape, mybir.dt.from_np(x.dtype), kind="ExternalInput").ap() for name, x in arrays.items()}
    o = {name: nc.dram_tensor(f"out_{name}", shape, F32, kind="ExternalOutput").ap() for name, shape, _ in OUTPUTS}
    scratch = {"h2": nc.dram_tensor("h2_rows", (TOK, D), F32, kind="Internal").ap(),
               "y": nc.dram_tensor("expert_rows", (NBLK * B, D), F32, kind="Internal").ap()}
    build(nc, a, o, scratch)
    r = run_bass_kernel_spmd(nc, [arrays], core_ids=[0])
    return tuple(np.asarray(r.results[0][f"out_{name}"]).reshape(shape) for name, _, shape in OUTPUTS)
```

```python
import math
from contextlib import ExitStack

import numpy as np

import concourse.bass as bass
from concourse import mybir

F32 = mybir.dt.float32
U32 = mybir.dt.uint32
I32 = mybir.dt.int32
ALU = mybir.AluOpType
ACT = mybir.ActivationFunctionType
AX = mybir.AxisListType

D = 1024
KD = D // 128
SEQ, DEC, PAST, MEMT = 256, 64, 256, 256
TOK = SEQ + DEC
TILES = [(0, 128), (128, 128), (256, 64)]
NT = len(TILES)
G, CH, ST = 32, 16, 64
GP = G // 2
WIN, NWIN = 64, TOK // 64
H, NOPE, ROPE, QK, VH = 8, 64, 32, 96, 64
QL, KVL = 384, 256
MH, MD = 4, 128
EPS = 1e-6
SCALE_MLA = 1.0 / math.sqrt(QK)
SCALE_MEM = 1.0 / math.sqrt(MD)
NEG = -1e30
NG, EPG = 4, 8
NE, FF = NG * EPG, 256
B = 64
NJ = (TOK - 1) // B
NOV = (2 * TOK - NE) // B
NBLK = NE + NOV
FILLS = [(f, min(128, NBLK * B - f)) for f in range(NE * B, NBLK * B, 128)]

KEYS = [(0, 128), (128, 128), (256, 128), (384, 128), (512, 64)]
KEY_OF_TILE = [0, 1, 4]
POS_OF_KEY = [0, 1, 0, 1, 2]

C_U, C_QL, C_KV, C_QM, C_GATE = 0, 512, 896, 1184, 1696
DGROUPS = [(0, 3), (3, 3), (6, 2)]
BRANCH_C, BRANCH_B, BRANCH_A = 2, 1, 0


def layout(parts):
    at, out = 0, {}
    for name, n in parts:
        out[name] = (at, at + n)
        at += n
    return out, at


CONST, NCONST = layout([("ident", 128), ("upper", 128), ("ones", 128), ("rope", 3 * 2 * ROPE),
                        ("mask0", 128), ("mask1", 256), ("iotab", B), ("iotablk", NBLK), ("iotae", NE),
                        ("sel_b", 2), ("sel_c", 4), ("valid", NT), ("tokid", NT), ("half", 8)])


def constants():
    c = np.zeros((128, NCONST), np.float32)

    def put(name, value):
        a, b = CONST[name]
        c[:, a:b] = np.asarray(value, np.float32).reshape(128, b - a)

    p = np.arange(128)
    put("ident", np.eye(128))
    put("upper", p[:, None] < p[None, :])
    put("ones", np.ones((128, 128)))
    inv = (10000.0 ** (-np.arange(ROPE // 2, dtype=np.float32) / (ROPE // 2))).astype(np.float32)
    rope = np.zeros((128, 3, 2, ROPE), np.float32)
    for n in range(3):
        ang = (p + 128 * n).astype(np.float32)[:, None] * inv[None, :]
        rope[:, n, 0] = np.concatenate([np.cos(ang), np.cos(ang)], 1)
        rope[:, n, 1] = np.concatenate([-np.sin(ang), np.sin(ang)], 1)
    put("rope", rope)
    chunk = p[:, None] // 64
    put("mask0", np.where(p[None, :] // 64 <= chunk, 0, NEG))
    put("mask1", np.where(np.arange(256)[None, :] // 64 <= 2 + chunk, 0, NEG))
    put("iotab", np.tile(np.arange(B), (128, 1)))
    put("iotablk", np.tile(np.arange(NBLK), (128, 1)))
    put("iotae", np.tile(np.arange(NE), (128, 1)))
    put("sel_b", np.stack([p // ST == 0, p // ST == 1], 1))
    even = (p // CH) % 2 == 0
    put("sel_c", np.stack([even, ~even, -1.0 * even, -1.0 * ~even], 1))
    put("valid", np.stack([p < n for _, n in TILES], 1))
    put("tokid", np.stack([np.where(p < n, p + f, 0) for f, n in TILES], 1))
    put("half", np.full((128, 8), -0.5))
    return c


CHUNKS = [("u0", KD, 256), ("u1", KD, 256), ("ql", KD, QL), ("kv", KD, KVL + ROPE), ("qm0", KD, 256),
          ("qm1", KD, 256), ("mk0", KD, 256), ("mk1", KD, 256), ("mv0", KD, 256), ("mv1", KD, 256)]
SLOT_OF = [n % 3 for n in range(len(CHUNKS))]


def over_d(name, kt, per_tile, slots):
    CHUNKS.extend((f"{name}{g}", kt, per_tile * nd) for g, (d0, nd) in enumerate(DGROUPS))
    SLOT_OF.extend(slots)


over_d("gateC", KD, 128, (1, 2, 0))
CHUNKS += [("ukv", 2, H * (NOPE + VH)), ("uq", 3, H * QK)]
SLOT_OF += [1, 2]
over_d("outC", 4, 128, (0, 0, 0))
over_d("gateB", KD, 128, (1, 2, 0))
over_d("gateA", KD, 128, (1, 2, 0))
over_d("outB", 4, 128, (1, 2, 0))
over_d("glu", 4, 256, (1, 2, 0))
over_d("wout", KD, 128, (1, 2, 0))
CHUNK_NO = {c[0]: n for n, c in enumerate(CHUNKS)}
WSLOTS, WSLOT = 3, 3072
FORMER = [max((m for m in range(n) if SLOT_OF[m] == SLOT_OF[n]), default=None) for n in range(len(CHUNKS))]

MEM_UNITS = [("mem", t, h, 2) for t in range(NT) for h in (0, 2)]
MLA_UNITS = ([("mla", 0, h, 4) for h in (0, 4)] + [("mla", 1, h, 2) for h in (0, 2, 4, 6)]
             + [("mla", 2, h, 1) for h in range(H)])
KQ_UNITS = [("k", j, half) for j in range(5) for half in (0, 1)] + [("q", t, half) for t in range(NT) for half in (0, 1)]
KQ_LAG, KQ_BUFS = 2, 4
RING = 5


def key_blocks(unit):
    kind, t = unit[0], unit[1]
    if kind == "mem":
        return [128, 128]
    return [[128], [128, 128], [128, 128, 64]][t]


def attention_order(units):
    for n in range(len(units) + 2):
        if n < len(units):
            yield "S", n
        if 1 <= n <= len(units):
            yield "PT", n - 1
        if n >= 2:
            yield "O", n - 2
            if n - 1 == len(units) or units[n - 1][1] != units[n - 2][1]:
                yield "OT", units[n - 2][1]


def middle():
    out, fills, turns = [], [], iter(range(GP))
    beats = 0

    def beat():
        nonlocal beats
        if beats % S5_EVERY == 0:
            out.extend(("turn", q) for q in [next(turns, None)] if q is not None)
        beats += 1

    def fill(n=1):
        for _ in range(n):
            if fills:
                out.append(fills.pop(0))

    def attention(kind, units, order_fill):
        for step, m in attention_order(units):
            out.append((kind, step, m))
            if step == "S":
                beat()
                fill(order_fill)

    fills = [("gateC", d) for d in range(KD)]
    for src in range(2):
        for kt in range(2):
            out.append(("mkT", src, kt))
            beat()
    for t in range(NT):
        out.append(("qmT", t))
        beat()
        if t < 2:
            fill()
    attention("mem", MEM_UNITS, 1)
    fill(KD)
    fills = [("outC", d) for d in range(KD)]
    for t in range(NT):
        out.append(("qlT", t))
        beat()
    for j in range(len(KEYS)):
        out.append(("ckT", j))
        beat()
    for n in range(len(KQ_UNITS) + KQ_LAG):
        if n < len(KQ_UNITS):
            out.append(("kq", n))
        if n % 2 == 1:
            fill()
        if n >= KQ_LAG:
            out.append(("kqT", n - KQ_LAG))
        beat()
    fill(KD)
    fills = [("gateB", d) for d in range(KD)] + [("gateA", d) for d in range(KD)]
    attention("mla", MLA_UNITS, 1)
    fill(KD)
    for d in range(KD):
        out.append(("outB", d))
        beat()
    out.extend(("turn", q) for q in turns)
    return out


S5_EVERY = 4
MIDDLE = middle()


def emptier(unit):
    if unit[0] in ("mem", "mla"):
        return {"S": "act", "PT": "act", "O": "dve", "OT": "act"}[unit[1]]
    return "dve" if unit[0].startswith("out") else "act"


def units_in_order():
    out = [("par", "act")]
    out += [(("xT", t, g), "act") for t in range(NT) for g in range(2)]
    out += [(("u", m), "act") for m in range(4)]
    out += [((c, t), "act") for c in ("ql", "kv", "qm0", "qm1") for t in range(NT)]
    out += [(("memT", t, g), "act") for t in range(2) for g in range(2)]
    out += [((c, t), "act") for c in ("mk0", "mk1", "mv0", "mv1") for t in range(2)]
    out += [(("s5T", n), "act") for n in range(4)]
    out += [(step, emptier(step)) for step in MIDDLE if step[0] != "turn"]
    for d in range(KD):
        out += [(("glug", d), "act"), (("gluv", d), "dve")]
    for t in range(NT + 1):
        if t < NT:
            out += [(("wout", g, t), "dve") for g in range(3)]
        if t > 0:
            out += [(("h2T", t - 1, g), "act") for g in range(2)] + [(("route", t - 1), "dve")]
    out += [("rank", "dve"), ("table", "dve")]
    return out


UNITS = units_in_order()
UNIT_NO = {k: n for n, (k, _) in enumerate(UNITS)}


def last_use():
    out = {f"u{n}": ("u", 2 * n + 1) for n in range(2)}
    out |= {c: (c, NT - 1) for c in ("ql", "kv", "qm0", "qm1")}
    out |= {c: (c, 1) for c in ("mk0", "mk1", "mv0", "mv1")}
    out |= {"ukv": ("kq", 9), "uq": ("kq", len(KQ_UNITS) - 1)}
    for g, (d0, nd) in enumerate(DGROUPS):
        for br in "CB":
            out |= {f"gate{br}{g}": (f"gate{br}", d0 + nd - 1), f"out{br}{g}": (f"out{br}", d0 + nd - 1)}
        out |= {f"glu{g}": ("gluv", d0 + nd - 1), f"gateA{g}": ("gateA", d0 + nd - 1), f"wout{g}": ("wout", g, NT - 1)}
    return out


LAST_USE = last_use()

NORMS = ([("x", t) for t in range(NT)] + [("m", t) for t in range(2)] + [("ql", t) for t in range(NT)]
         + [("ck", t) for t in range(NT)] + [("qm", t) for t in range(NT)] + [("mk", t) for t in range(2)]
         + [("kq", n) for n in range(len(KQ_UNITS))] + [("f", t) for t in range(NT)])
NORM_NO = {k: n for n, k in enumerate(NORMS)}
NORM_WIDTH = {"x": D, "m": D, "ql": QL, "ck": KVL, "qm": MD, "mk": MD, "kq": QK, "f": D}
NORM_HEADS = {"x": 1, "m": 1, "ql": 1, "ck": 1, "qm": MH, "mk": MH, "kq": 4, "f": 1}
NORMS_BEFORE_S5 = NORM_NO["ql", 0]


def norm_rows(key):
    kind, n = key
    if kind == "m" or kind == "mk":
        return 128
    if kind == "kq":
        what, j, _ = KQ_UNITS[n]
        return KEYS[j][1] if what == "k" else TILES[j][1]
    return TILES[n][1]


class Steps:

    def __init__(self, eng, own):
        self.eng, self.own, self.count = eng, own, {}

    def mark(self, ins, sem=None, by=1):
        sem = self.own if sem is None else sem
        ins.then_inc(sem, by)
        self.count[sem] = self.count.get(sem, 0) + by
        return sem, self.count[sem]

    def after(self, *marks):
        for sem, n in marks:
            self.eng.wait_ge(sem, n)


def build(nc, a, o, scratch):
    ctx = ExitStack()
    with ctx:
        def sem(name):
            return ctx.enter_context(nc.semaphore(name))

        def alloc(stack, name, shape, dt=F32):
            return stack.enter_context(nc.sbuf_tensor(name, shape, dt))

        def width(shape):
            return 4 * int(np.prod(shape[1:]))

        def overlay(stack, *groups):
            out, sizes = {}, [sum(width(s) for _, s in g) for g in groups]
            for n, group in enumerate(groups):
                own = stack if n == len(groups) - 1 else ExitStack()
                for name, shape in group:
                    if name in out:
                        alloc(own, f"{name}_again", shape)
                    else:
                        out[name] = alloc(own, name, shape)
                if n == len(groups) - 1:
                    if sizes[n] < max(sizes):
                        alloc(own, f"pad_{group[0][0]}", [128, (max(sizes) - sizes[n]) // 4])
                else:
                    own.close()
            return out

        v = overlay(ctx, [("X0", [128, NT, D])], [("qT", [128, H, TOK])], [("X", [128, NT, D])])
        X0, qT, X = v["X0"], v["qT"], v["X"]
        cst = alloc(ctx, "cst", [128, NCONST])
        sums = alloc(ctx, "sums", [128, len(NORMS), 4])
        rstd = alloc(ctx, "rstd", [128, len(NORMS), 4])
        means = alloc(ctx, "means", [128, len(NORMS), 4])
        grow = alloc(ctx, "grow", [128, D])
        junk = ctx.enter_context(nc.sbuf_tensor("junk", [128, D], mybir.dt.bfloat16))
        pre = ExitStack()
        hT = alloc(pre, "hT", [128, KD, TOK])
        uT = alloc(pre, "uT", [128, 4, TOK])
        oTmem = alloc(pre, "oTmem", [128, 4, TOK])
        oTmla = alloc(pre, "oTmla", [128, 4, TOK])
        v = overlay(pre, [("qlat", [128, NT, QL]), ("ckv", [128, 5, KVL + ROPE])], [("gateA", [128, KD, TOK])])
        qlat, ckv, gateA = v["qlat"], v["ckv"], v["gateA"]
        gsmall = alloc(pre, "gsmall", [128, QL + KVL + 2 * QK + 2 * MD])
        s5par = alloc(pre, "s5par", [128, 5, GP])
        s5tmp = alloc(pre, "s5tmp", [128, 24, GP])
        cosT = alloc(pre, "cosT", [128, GP, WIN])
        sinT = alloc(pre, "sinT", [128, GP, WIN])
        wB = alloc(pre, "wB", [128, 2, 4, 128])
        wC = alloc(pre, "wC", [128, 2, 4, 128])
        dskip = alloc(pre, "dskip", [128, 4])
        rotA = alloc(pre, "rotA", [128, 2, TOK])
        rotB = alloc(pre, "rotB", [128, 2, TOK])
        rotC = alloc(pre, "rotC", [128, 2, TOK])
        hS = alloc(pre, "hS", [128, 2, 2, TOK])
        carry = alloc(pre, "carry", [128, 2, 3, 4])
        finals = alloc(pre, "finals", [128, 2, 2, GP])
        soft = alloc(pre, "soft", [128, 4, 3, 4])
        v = overlay(pre, [("Hn", [128, NT, D])],
                    [("bbar", [128, 2, GP, CH]), ("btmp", [128, 4, GP, CH])],
                    [("KQ", [128, KQ_BUFS, 4, QK]), ("ropet", [128, 2, 2, 4, ROPE])],
                    [("gateB", [128, KD, TOK]), ("mtmp", [128, 2, TOK])])
        Hn, bbar, btmp, KQ, ropet, gateB, mtmp = (v[k] for k in ("Hn", "bbar", "btmp", "KQ", "ropet", "gateB", "mtmp"))
        v = overlay(pre, [("s5raw", [GP, 5, 128]), ("dtraw", [GP, 2]), ("braw", [128, 2, GP, CH]),
                          ("bpad", [128, 2, GP, 2, CH]), ("craw", [128, 2, 4, ST]), ("cpad", [128, 2, 4, 2, ST])],
                    [("P", [128, 2, 512]), ("PT", [128, 2, 512]), ("O", [128, NT, 512])])
        s5raw, dtraw, braw, bpad, craw, cpad = (v[k] for k in ("s5raw", "dtraw", "braw", "bpad", "craw", "cpad"))
        P, PT, O = v["P"], v["PT"], v["O"]
        kv = [("mk", [128, 2, 2, 512]), ("mv", [128, 2, 2, 512]), ("qmem", [128, NT, MH * MD])]
        v = overlay(pre, kv + [("mem", [128, 2, D]), ("memT", [128, KD, MEMT])],
                    kv + [("mkT", [128, 2, MH, MEMT]), ("qmT", [128, MH, TOK])],
                    [("ckT", [128, 2, 576]), ("qlT", [128, 3, TOK]), ("V", [128, 5, 512]),
                     ("kT", [128, H, 576])],
                    [("gelu", [128, 4, TOK]), ("finrow", [GP, 4, 128]), ("gsig", [128, 2, TOK])])
        mem, memT, mk, mv, qmem, mkT, qmT = (v[k] for k in ("mem", "memT", "mk", "mv", "qmem", "mkT", "qmT"))
        ckT, qlT, V, kT = (v[k] for k in ("ckT", "qlT", "V", "kT"))
        gelu, finrow, gsig = (v[k] for k in ("gelu", "finrow", "gsig"))
        mergedT = alloc(pre, "mergedT", [128, KD, TOK])
        W = [alloc(pre, f"W{i}", [128, WSLOT]) for i in range(WSLOTS)]
        pre.close()
        moe = ExitStack()
        ctx.enter_context(moe)
        h2 = alloc(moe, "h2", [128, NT, D])
        h2T = alloc(moe, "h2T", [128, KD, TOK])
        wr = alloc(moe, "wr", [128, KD, NG + NE])
        brow = alloc(moe, "brow", [128, NG + NE])
        lg = alloc(moe, "lg", [128, NT, 40])
        E13 = [alloc(moe, f"E13_{i}", [128, 2, KD, FF]) for i in range(4)]
        E2 = [alloc(moe, f"E2_{i}", [128, 2, D]) for i in range(4)]
        xg = alloc(moe, "xg", [B, 2, D])
        xT = alloc(moe, "xT", [128, 2, KD, B])
        tg = alloc(moe, "tg", [128, 2, 2, B])
        ug = alloc(moe, "ug", [128, 2, 2, B])
        hid = alloc(moe, "hid", [128, 2, 2, B])
        yb = alloc(moe, "yb", [B, 2, D])
        r8 = alloc(moe, "r8", [128, 4, NT, 8])
        i8 = alloc(moe, "i8", [128, 2, NT, 8], U32)
        rs = alloc(moe, "rs", [128, 24, NT])
        ex4 = alloc(moe, "ex4", [128, 3, NT, NG])
        prod = alloc(moe, "prod", [128, NT, EPG, NG])
        Ek = alloc(moe, "Ek", [128, 3, NT, NE])
        rk = alloc(moe, "rk", [128, 8, NT, NE])
        cnt = alloc(moe, "cnt", [128, 6, NE])
        tp = alloc(moe, "tp", [128, 4, NT, NE])
        ohs = alloc(moe, "ohs", [128, 2, NT, B])
        ohb = alloc(moe, "ohb", [128, 4, NT, NBLK])
        idx = alloc(moe, "idx", [B, NBLK], U32)
        idx_ov = alloc(moe, "idx_ov", [B, 2], U32)
        pos = alloc(moe, "pos", [128, 2, NT], U32)
        ovcmp = alloc(moe, "ovcmp", [1, NOV, NE])
        ovf = alloc(moe, "ovf", [1, 2, NOV])
        ovi = alloc(moe, "ovi", [1, NOV + 1], I32)
        rows = alloc(moe, "rows", [128, 2, NT, D])
        PS = ctx.enter_context(nc.psum_tensor("PS", [128, 8, 512], F32))
        BU, YB = 5, 7

        def const(name, rows_=128):
            x, y = CONST[name]
            return cst[0:rows_, x:y]

        ident = const("ident")
        rope = const("rope").rearrange("p (n c d) -> p n c d", n=3, c=2)
        g_ql = gsmall[:, 0:QL]
        g_kv = gsmall[:, QL:QL + KVL]
        o1 = QL + KVL
        g_qn, g_kn = gsmall[:, o1:o1 + QK], gsmall[:, o1 + QK:o1 + 2 * QK]
        g_mq, g_mk = gsmall[:, o1 + 2 * QK:o1 + 2 * QK + MD], gsmall[:, o1 + 2 * QK + MD:]

        names = """x_loaded params_loaded const_loaded gains_loaded mem_loaded s5_loaded cache_loaded
            gffn_loaded router_loaded psum_full emptied_act emptied_dve sums_ready rstd_ready h_ready mem_ready
            s5_raw_ready s5_scaled s5_mag_ready s5_reduced s5_sin_ready s5_den s5_rden s5_tables s5_padded
            bu_full bu_free h_state y_full y_skipped y_square y_inner y_tanh z_ready finals_copied finals_full
            finals_out ql_ready ck_ready qm_ready mk_ready scores_max kq_ready merged h2_ready
            logits_in logits_exp onehot_ready tables_in idx_ready gathered0 gathered1 xt_full xt_ready
            ab_full tanh_ready hid_ready y_mm y_act y_dve y_filled y_stored0 y_stored1 h2_stored ov_idx ov_gathered ov_xt_full ov_xt_ready
            ov_ab ov_tanh ov_hid ov_y_mm ov_y_act ov_y_dve ov_stored ov_w rows_gathered0 rows_gathered1 rows_gathered2 out_ready
            stored pe_passed pool_passed act_step dve_step pool_step dve_moe ov_half""".split()
        s = {n: sem(n) for n in names}
        chunk_loaded = [sem(f"chunk_loaded{i}") for i in range(WSLOTS)]
        expert_loaded = [sem(f"expert_loaded{i}") for i in range(4)]

        def bank(key):
            return PS[:, UNIT_NO[key] % RING, :]

        def emptied_at(n):
            who = UNITS[n][1]
            return s["emptied_" + who], sum(1 for _, w in UNITS[:n + 1] if w == who)

        def chunk(name, kt, cols):
            return W[SLOT_OF[CHUNK_NO[name]]][:, 0:kt * cols].rearrange("p (k n) -> p k n", k=kt)

        def chunk_view(name):
            _, kt, cols = CHUNKS[CHUNK_NO[name]]
            return chunk(name, kt, cols)

        def chunk_source(name):
            w_in = a["w_in"][0].rearrange("(p k) n -> p k n", k=KD)
            w_mem = a["w_mem_kv"][0].rearrange("(p k) n -> p k n", k=KD)
            dst = chunk_view(name)
            cols = CHUNKS[CHUNK_NO[name]][2]
            first = {"u0": C_U, "u1": C_U + 256, "ql": C_QL, "kv": C_KV, "qm0": C_QM, "qm1": C_QM + 256}
            if name in first:
                return [(dst, w_in[:, :, first[name]:first[name] + cols])]
            if name[:2] in ("mk", "mv"):
                c = (512 if name[1] == "v" else 0) + 256 * int(name[2])
                return [(dst, w_mem[:, :, c:c + cols])]
            if name == "ukv":
                return [(dst, a["w_ukv"][0].rearrange("(k p) n -> p k n", p=128))]
            if name == "uq":
                return [(dst, a["w_uq"][0].rearrange("(k p) n -> p k n", p=128))]
            d0, nd = DGROUPS[int(name[-1])]
            if name.startswith("gate"):
                c = C_GATE + D * {"A": BRANCH_A, "B": BRANCH_B, "C": BRANCH_C}[name[4]] + 128 * d0
                return [(dst, w_in[:, :, c:c + cols])]
            if name.startswith("out"):
                w = a["w_o_mem"] if name[3] == "C" else a["w_o_mla"]
                return [(dst, w[0].rearrange("(k p) n -> p k n", p=128)[:, :, 128 * d0:128 * d0 + cols])]
            if name.startswith("glu"):
                w = a["w_glu"][0].rearrange("(k p) n -> p k n", p=128)
                n = 128 * nd
                return [(dst[:, :, 0:n], w[:, :, 128 * d0:128 * d0 + n]),
                        (dst[:, :, n:2 * n], w[:, :, D + 128 * d0:D + 128 * d0 + n])]
            w = a["w_out"][0].rearrange("(k p) n -> p k n", p=128)
            return [(dst, w[:, :, 128 * d0:128 * d0 + cols])]

        DMAS_OF = [len(chunk_source(c[0])) for c in CHUNKS]

        def chunk_loaded_at(name):
            n = CHUNK_NO[name]
            return chunk_loaded[SLOT_OF[n]], 16 * sum(DMAS_OF[m] for m in range(n + 1) if SLOT_OF[m] == SLOT_OF[n])

        e13_src = [a["w_e1"][0].rearrange("e (p k) n -> p e k n", k=KD), a["w_e3"][0].rearrange("e (p k) n -> p e k n", k=KD)]
        e2_src = a["w_e2"][0].rearrange("e (j p) n -> p e j n", p=128)
        LOADS = 3

        xp, xs = a["x_prompt"][0], a["x_sample"][0]
        block = ctx.enter_context(nc.Block())

        @block.sync
        def _(sp):
            st = Steps(sp, None)
            stored = []

            def store(dst, src):
                stored.append(st.mark(sp.dma_start(dst, src), s["stored"], 16))

            def load_chunk(n):
                if FORMER[n] is not None:
                    sp.wait_ge(s["psum_full"], UNIT_NO[LAST_USE[CHUNKS[FORMER[n]][0]]] + 1)
                for dst, src in chunk_source(CHUNKS[n][0]):
                    sp.dma_start(dst, src).then_inc(chunk_loaded[SLOT_OF[n]], 16)

            for t, (f, n) in enumerate(TILES):
                src = xp[f:f + n, :] if t < 2 else xs
                sp.dma_start(X0[0:n, t, :], src).then_inc(s["x_loaded"], 16)
            sp.dma_start(cst[:], a["consts"]).then_inc(s["const_loaded"], 16)
            sp.dma_start(grow[:], a["g_attn"][0].partition_broadcast(128)).then_inc(s["gains_loaded"], 16)
            for n, name in enumerate(("ssm_a_re", "ssm_a_im")):
                sp.dma_start(s5raw[:, n, :], a[name][0].rearrange("(q g) p -> q (g p)", g=2)).then_inc(s["s5_loaded"], 16)
            for n, name in enumerate(("cache_ssm_re", "cache_ssm_im")):
                sp.dma_start(s5raw[:, 2 + n, :], a[name][0][0].rearrange("(q g) p -> q (g p)", g=2)).then_inc(s["s5_loaded"], 16)
            sp.dma_start(dtraw[:], a["ssm_log_dt"][0].rearrange("(q g) -> q g", g=2)).then_inc(s["s5_loaded"], 16)
            load_chunk(0)
            load_chunk(1)
            load_chunk(2)
            for n in range(2):
                sp.dma_start(mem[:, n, :], a["mem_prompt"][0][128 * n:128 * n + 128, :]).then_inc(s["mem_loaded"], 16)
            sp.dma_start(memT[:, 0:4, :].rearrange("p k n -> p (k n)"),
                         a["g_mem"][0].partition_broadcast(128)).then_inc(s["mem_loaded"], 16)
            for n, name in enumerate(("ssm_b_re", "ssm_b_im")):
                for g2 in range(2):
                    sp.dma_start(braw[64 * g2:64 * g2 + 64, n], a[name][0].rearrange("(q g) p c -> g p q c", g=2)[g2])\
                        .then_inc(s["params_loaded"], 16)
            for n, name in enumerate(("ssm_c_re", "ssm_c_im")):
                sp.dma_start(craw[:, n], a[name][0].rearrange("(t g) c p -> (g c) t p", g=8)).then_inc(s["params_loaded"], 16)
            sp.dma_start(dskip[:], a["ssm_d"][0].rearrange("(t p) -> p t", p=128),
                         allow_slow_non_contiguous=True).then_inc(s["params_loaded"], 16)
            for dst, name in ((g_ql, "g_qlat"), (g_kv, "g_kvlat"), (g_qn, "g_qn"), (g_kn, "g_kn"), (g_mq, "g_mqn"), (g_mk, "g_mkn")):
                sp.dma_start(dst, a[name][0].partition_broadcast(128)).then_inc(s["gains_loaded"], 16)
            for n in range(2):
                r = slice(128 * n, 128 * n + 128)
                sp.dma_start(ckv[:, 2 + n, 0:KVL], a["cache_mla_ckv"][0][0][r, :]).then_inc(s["cache_loaded"], 16)
                sp.dma_start(ckv[:, 2 + n, KVL:], a["cache_mla_kpe"][0][0][r, :]).then_inc(s["cache_loaded"], 16)
                sp.dma_start(mk[:, 1, n, :], a["cache_mem_k"][0][0][r].rearrange("t h d -> t (h d)")).then_inc(s["cache_loaded"], 16)
                sp.dma_start(mv[:, 1, n, :], a["cache_mem_v"][0][0][r].rearrange("t h d -> t (h d)")).then_inc(s["cache_loaded"], 16)
            sp.wait_ge(s["x_loaded"], 16 * NT)
            for f, n in FILLS:
                sp.dma_start(scratch["y"][f:f + n, :], X0[0:n, 0, :]).then_inc(s["y_filled"], 16)
            for n in range(3, CHUNK_NO["mv1"] + 1):
                load_chunk(n)
            for t, (f, n) in enumerate(TILES):
                sp.wait_ge(s["ck_ready"], t + 1)
                j = KEY_OF_TILE[t]
                store(o["ckv_p"][f:f + n, :] if t < 2 else o["ckv_s"], ckv[0:n, j, 0:KVL])
                store(o["kpe_p"][f:f + n, :] if t < 2 else o["kpe_s"], ckv[0:n, j, KVL:])
            for t in range(2):
                sp.wait_ge(s["mk_ready"], t + 1)
                store(o["mem_k"][128 * t:128 * t + 128, :], mk[:, 0, t, :])
                store(o["mem_v"][128 * t:128 * t + 128, :], mv[:, 0, t, :])
            for n in range(CHUNK_NO["gateC0"], CHUNK_NO["glu0"]):
                load_chunk(n)
            sp.wait_ge(s["psum_full"], UNIT_NO["mla", "S", len(MLA_UNITS) - 1] + 1)
            for t, (f, n) in enumerate(TILES):
                sp.dma_start(X[0:n, t, :], xp[f:f + n, :] if t < 2 else xs).then_inc(s["x_loaded"], 16)
            sp.wait_ge(s["h_ready"], NT)
            sp.dma_start(grow[:], a["g_ffn"][0].partition_broadcast(128)).then_inc(s["gffn_loaded"], 16)
            sp.wait_ge(s["finals_out"], 1)
            for n, name in enumerate(("sre_p", "sim_p", "sre_s", "sim_s")):
                store(o[name], finrow[:, n, :])
            for n in range(CHUNK_NO["glu0"], len(CHUNKS)):
                load_chunk(n)

            sp.wait_ge(s["y_filled"], 16 * len(FILLS))
            sp.wait_ge(s["merged"], KD)
            st.after(stored[-1])
            sp.dma_start(wr[:, :, 0:NG], a["w_rg"][0].rearrange("(p k) n -> p k n", k=KD)).then_inc(s["router_loaded"], 16)
            sp.dma_start(wr[:, :, NG:], a["w_re"][0].rearrange("(p k) n -> p k n", k=KD)).then_inc(s["router_loaded"], 16)
            sp.dma_start(brow[:, 0:NG], a["b_rg"][0].partition_broadcast(128)).then_inc(s["router_loaded"], 16)
            sp.dma_start(brow[:, NG:], a["b_re"][0].rearrange("g e -> (g e)").partition_broadcast(128)).then_inc(s["router_loaded"], 16)

            def load_expert(u, e):
                for n in range(2):
                    sp.dma_start(E13[u][:, n, :, :], e13_src[n][:, e, :, :]).then_inc(expert_loaded[u], 16)
                sp.dma_start(E2[u][:], e2_src[:, e, :, :]).then_inc(expert_loaded[u], 16)

            for u in range(4):
                load_expert(u, u)
            for t, (f, n) in enumerate(TILES):
                sp.wait_ge(s["h2_ready"], t + 1)
                sp.dma_start(scratch["h2"][f:f + n, :], h2[0:n, t, :]).then_inc(s["h2_stored"], 16)

            def store_rows(u, e):
                sp.wait_ge(s["y_act"], e + 1)
                sp.wait_ge(s["y_dve"], e + 1)
                sp.dma_start(scratch["y"][bass.ts(e, B), :], yb[:, u % 2, :]).then_inc(s[f"y_stored{u % 2}"], 16)

            with sp.Fori(0, NE // 4 - 1) as i:
                for u in range(4):
                    e = i * 4 + u
                    sp.wait_ge(s["y_mm"], e + 1)
                    for n in range(2):
                        sp.dma_start(E13[u][:, n, :, :], e13_src[n][:, bass.ds(e + 4, 1), :, :].rearrange("p e k n -> p (e k) n"))\
                            .then_inc(expert_loaded[u], 16)
                    sp.dma_start(E2[u][:], e2_src[:, bass.ds(e + 4, 1), :, :].rearrange("p e k n -> p (e k) n"))\
                        .then_inc(expert_loaded[u], 16)
                    store_rows(u, e)
            for u in range(4):
                store_rows(u, NE - 4 + u)

            sp.wait_ge(s["idx_ready"], 1)
            blocks = sp.value_load(ovi[0:1, NOV:NOV + 1], min_val=0, max_val=NOV)
            with sp.Fori(0, NOV) as i:
                with sp.If(i < blocks):
                    e = sp.value_load(ovi[0:1, bass.ds(i, 1)], min_val=0, max_val=NE - 1)
                    sp.wait_ge(s["ov_y_mm"], i)
                    for n in range(2):
                        sp.dma_start(E13[0][:, n, :, :], e13_src[n][:, bass.ds(e, 1), :, :].rearrange("p e k n -> p (e k) n"))\
                            .then_inc(s["ov_w"], 16)
                    sp.dma_start(E2[0][:], e2_src[:, bass.ds(e, 1), :, :].rearrange("p e k n -> p (e k) n")).then_inc(s["ov_w"], 16)
                    sp.wait_ge(s["ov_y_act"], i + 1)
                    sp.wait_ge(s["ov_y_dve"], i + 1)
                    sp.dma_start(scratch["y"][bass.ds(i * B + NE * B, B), :], yb[:, 0, :]).then_inc(s["ov_stored"], 16)
            for t, (f, n) in enumerate(TILES):
                sp.wait_ge(s["out_ready"], t + 1)
                store(o["y_p"][f:f + n, :] if t < 2 else o["y_s"], X[0:n, t, :])
            st.after(stored[-1])

        @block.tensor
        def _(pe):
            mm = nc.tensor.matmul

            def begin(key):
                n = UNIT_NO[key]
                if n >= RING:
                    pe.wait_ge(*emptied_at(n - RING))
                return bank(key)

            def end(ins):
                ins.then_inc(s["psum_full"], 1)

            def use(name):
                sem_, value = chunk_loaded_at(name)
                pe.wait_ge(sem_, value)
                return chunk_view(name)

            def emptied(key):
                pe.wait_ge(*emptied_at(UNIT_NO[key]))

            pe.wait_ge(s["const_loaded"], 16)
            pe.wait_ge(s["s5_raw_ready"], 1)
            out = begin("par")
            for n in range(5):
                ins = nc.tensor.transpose(out[:, GP * n:GP * n + GP], s5raw[:, n, :], ident[0:GP, 0:GP])
            end(ins)

            for t, (f, n) in enumerate(TILES):
                pe.wait_ge(s["h_ready"], t + 1)
                for g in range(2):
                    out = begin(("xT", t, g))
                    for k in range(4):
                        ins = nc.tensor.transpose(out[:, k * n:k * n + n], Hn[0:n, t, 4 * g + k::KD], ident[0:n, 0:n])
                    end(ins)

            def feature_major(key, w, cols, rhs, kt):
                out = begin(key)
                for k in range(kt):
                    ins = mm(out[:, 0:TOK], w[:, k, cols:cols + 128], rhs[:, k, :], start=(k == 0), stop=(k == kt - 1))
                end(ins)

            def token_major(key, w, c0, cols, lhs, f, n, kt):
                out = begin(key)
                for k in range(kt):
                    ins = mm(out[0:n, 0:cols], lhs[:, k, f:f + n], w[:, k, c0:c0 + cols], start=(k == 0), stop=(k == kt - 1))
                end(ins)

            emptied(("xT", NT - 1, 1))
            for m in range(4):
                w = use(f"u{m // 2}")
                feature_major(("u", m), w, 128 * (m % 2), hT, KD)
            for name in ("ql", "kv", "qm0", "qm1"):
                w = use(name)
                for t, (f, n) in enumerate(TILES):
                    token_major((name, t), w, 0, CHUNKS[CHUNK_NO[name]][2], hT, f, n, KD)

            for t in range(2):
                pe.wait_ge(s["mem_ready"], t + 1)
                for g in range(2):
                    out = begin(("memT", t, g))
                    for k in range(4):
                        ins = nc.tensor.transpose(out[:, 128 * k:128 * k + 128], mem[:, t, 4 * g + k::KD], ident)
                    end(ins)
            emptied(("memT", 1, 1))
            for name in ("mk0", "mk1", "mv0", "mv1"):
                w = use(name)
                for t in range(2):
                    token_major((name, t), w, 0, 256, memT, 128 * t, 128, KD)

            for n in range(4):
                pe.wait_ge(s["s5_padded"], n + 1)
                out = begin(("s5T", n))
                for t in range(4):
                    src = (bpad[:, n, 4 * t:4 * t + 4].rearrange("p q g c -> p (q g c)") if n < 2
                           else cpad[:, n - 2, t].rearrange("p g s -> p (g s)"))
                    ins = nc.tensor.transpose(out[:, 128 * t:128 * t + 128], src, ident)
                end(ins)

            def s5_y(q):
                t, r = q // 4, 32 * (q % 4)
                pe.wait_ge(s["h_state"], q + 1)
                if q % 4 == 0 and t > 0:
                    pe.wait_ge(s["y_skipped"], t)
                for c in range(2):
                    ins = mm(PS[r:r + 32, YB, 0:TOK], wC[:, c, t, r:r + 32], hS[:, q % 2, c, :], start=(c == 0), stop=(c == 1))
                ins.then_inc(s["y_full"], 1)

            def s5_turn(q):
                t, r = q // 4, 32 * (q % 4)
                if q == 0:
                    emptied(("s5T", 3))
                else:
                    pe.wait_ge(s["bu_free"], q)
                for c in range(2):
                    ins = mm(PS[:, BU + c, 0:TOK], wB[r:r + 32, c, t, :], uT[r:r + 32, t, :], start=True, stop=True)
                ins.then_inc(s["bu_full"], 1)
                if q > 0:
                    s5_y(q - 1)

            def memory_keys(src, kt):
                if src == 0:
                    pe.wait_ge(s["mk_ready"], kt + 1)
                else:
                    pe.wait_ge(s["cache_loaded"], 16 * 8)
                out = begin(("mkT", src, kt))
                for h in range(MH):
                    ins = nc.tensor.transpose(out[:, 128 * h:128 * h + 128], mk[:, src, kt, MD * h:MD * h + MD], ident)
                end(ins)

            def memory_queries(t):
                f, n = TILES[t]
                pe.wait_ge(s["qm_ready"], t + 1)
                out = begin(("qmT", t))
                for h in range(MH):
                    ins = nc.tensor.transpose(out[:, n * h:n * h + n], qmem[0:n, t, MD * h:MD * h + MD], ident[0:n, 0:n])
                end(ins)

            def attention(kind, units, step, m):
                    mem_ = kind == "mem"
                    if (step, m) == ("S", 0):
                        emptied(("qmT", NT - 1) if mem_ else ("kqT", len(KQ_UNITS) - 1))
                    out = begin((kind, step, m))
                    if step == "OT":
                        n = TILES[m][1]
                        emptied((kind, "O", max(k for k, x in enumerate(units) if x[1] == m)))
                        for j in range(4):
                            ins = nc.tensor.transpose(out[:, n * j:n * j + n], O[0:n, m, 128 * j:128 * j + 128], ident[0:n, 0:n])
                        end(ins)
                        return
                    _, t, h0, nh = units[m]
                    f, n = TILES[t]
                    kb = key_blocks(units[m])
                    nk = sum(kb)
                    if step == "S":
                        for h in range(nh):
                            if mem_:
                                lhs, rhs = qmT[:, h0 + h, f:f + n], mkT[:, t // 2, h0 + h, :]
                            else:
                                k0 = 0 if t < 2 else 256
                                lhs, rhs = qT[0:QK, h0 + h, f:f + n], kT[0:QK, h0 + h, k0:k0 + nk]
                            ins = mm(out[0:n, nk * h:nk * h + nk], lhs, rhs, start=True, stop=True)
                        end(ins)
                    elif step == "PT":
                        emptied((kind, "S", m))
                        at = 0
                        for h in range(nh):
                            for b, rows_ in enumerate(kb):
                                src = P[0:n, m % 2, nk * h + 128 * b:nk * h + 128 * b + rows_]
                                ins = nc.tensor.transpose(out[0:rows_, n * at:n * at + n], src, ident[0:n, 0:n])
                                at += 1
                        end(ins)
                    else:
                        emptied((kind, "PT", m))
                        dv = MD if mem_ else VH
                        for h in range(nh):
                            for b, rows_ in enumerate(kb):
                                at = h * len(kb) + b
                                if mem_:
                                    rhs = mv[0:rows_, t // 2, b, MD * (h0 + h):MD * (h0 + h) + MD]
                                else:
                                    rhs = V[0:rows_, (0 if t < 2 else 2) + b, VH * (h0 + h):VH * (h0 + h) + VH]
                                ins = mm(out[0:n, dv * h:dv * h + dv], PT[0:rows_, m % 2, n * at:n * at + n], rhs,
                                         start=(b == 0), stop=(b == len(kb) - 1))
                        end(ins)

            def query_latents(t):
                f, n = TILES[t]
                pe.wait_ge(s["ql_ready"], t + 1)
                out = begin(("qlT", t))
                for k in range(3):
                    ins = nc.tensor.transpose(out[:, n * k:n * k + n], qlat[0:n, t, 128 * k:128 * k + 128], ident[0:n, 0:n])
                end(ins)

            def key_latents(j):
                f, n = KEYS[j]
                if j in (2, 3):
                    pe.wait_ge(s["cache_loaded"], 16 * 8)
                else:
                    pe.wait_ge(s["ck_ready"], KEY_OF_TILE.index(j) + 1)
                out = begin(("ckT", j))
                for k in range(2):
                    ins = nc.tensor.transpose(out[:, n * k:n * k + n], ckv[0:n, j, 128 * k:128 * k + 128], ident[0:n, 0:n])
                end(ins)

            def latents_up(m):
                what, j, half = KQ_UNITS[m]
                if m == 0:
                    emptied(("ckT", 4))
                if what == "k":
                    f, n = KEYS[j]
                    token_major(("kq", m), use("ukv"), 512 * half, 512, ckT, f, n, 2)
                else:
                    f, n = TILES[j]
                    token_major(("kq", m), use("uq"), 384 * half, 384, qlT, f, n, 3)

            def heads_transposed(m):
                what, j, half = KQ_UNITS[m]
                n = KEYS[j][1] if what == "k" else TILES[j][1]
                pe.wait_ge(s["kq_ready"], m + 1)
                out = begin(("kqT", m))
                for h in range(4):
                    ins = nc.tensor.transpose(out[0:QK, n * h:n * h + n], KQ[0:n, m % KQ_BUFS, h, :], ident[0:n, 0:n])
                end(ins)

            def branch(kind, d):
                g = min(d // 3, 2)
                col = 128 * (d - DGROUPS[g][0])
                if kind.startswith("gate"):
                    feature_major((kind, d), use(f"{kind}{g}"), col, hT, KD)
                else:
                    if d == 0:
                        emptied(("mem" if kind == "outC" else "mla", "OT", NT - 1))
                    feature_major((kind, d), use(f"{kind}{g}"), col, oTmem if kind == "outC" else oTmla, 4)

            run = {"turn": s5_turn, "mkT": memory_keys, "qmT": memory_queries, "qlT": query_latents, "ckT": key_latents,
                   "kq": latents_up, "kqT": heads_transposed}
            for kind, *which in MIDDLE:
                if kind in ("mem", "mla"):
                    attention(kind, MEM_UNITS if kind == "mem" else MLA_UNITS, *which)
                elif kind in run:
                    run[kind](*which)
                else:
                    branch(kind, *which)
            s5_y(GP - 1)
            pe.wait_ge(s["finals_copied"], GP)
            pe.wait_ge(s["bu_free"], GP)
            for n in range(4):
                ins = nc.tensor.transpose(PS[0:GP, BU, 128 * n:128 * n + 128], finals[:, n // 2, n % 2, :], ident)
            ins.then_inc(s["finals_full"], 1)
            pe.wait_ge(s["z_ready"], 4)
            for g, (d0, nd) in enumerate(DGROUPS):
                for d in range(d0, d0 + nd):
                    w = use(f"glu{g}")
                    feature_major(("glug", d), w, 128 * (nd + d - d0), uT, 4)
                    feature_major(("gluv", d), w, 128 * (d - d0), uT, 4)
            pe.wait_ge(s["merged"], KD)

            def route(t):
                f, n = TILES[t]
                pe.wait_ge(s["h2_ready"], t + 1)
                for g in range(2):
                    out = begin(("h2T", t, g))
                    for k in range(4):
                        ins = nc.tensor.transpose(out[:, k * n:k * n + n], h2[0:n, t, 4 * g + k::KD], ident[0:n, 0:n])
                    end(ins)
                emptied(("h2T", t, 1))
                if t == 0:
                    pe.wait_ge(s["router_loaded"], 64)
                token_major(("route", t), wr, 0, NG + NE, h2T, f, n, KD)

            for t, (f, n) in enumerate(TILES):
                for g, (d0, nd) in enumerate(DGROUPS):
                    token_major(("wout", g, t), use(f"wout{g}"), 0, 128 * nd, mergedT, f, n, KD)
                if t > 0:
                    route(t - 1)
            route(NT - 1)
            pe.wait_ge(s["onehot_ready"], 1)
            out = begin("rank")
            for t in range(NT):
                for t2 in range(t):
                    mm(out[:, NE * t:NE * t + NE], const("ones"), Ek[:, 2, t2, :], start=(t2 == 0), stop=False)
                mm(out[:, NE * t:NE * t + NE], const("upper"), Ek[:, 2, t, :], start=(t == 0), stop=True)
            for t in range(NT):
                ins = mm(out[:, NE * NT:NE * NT + NE], const("ones"), Ek[:, 2, t, :], start=(t == 0), stop=(t == NT - 1))
            end(ins)
            pe.wait_ge(s["tables_in"], 1)
            out = begin("table")
            for k in range(2):
                for t in range(NT):
                    ins = mm(out[0:B, 0:NBLK], ohs[:, k, t, :], ohb[:, k, t, :], start=(k + t == 0), stop=(k * NT + t == 2 * NT - 1))
            end(ins)
            pe.wait_ge(s["emptied_dve"], sum(1 for _, w in UNITS if w == "dve"))
            pe.wait_ge(s["emptied_act"], sum(1 for _, w in UNITS if w == "act"))

            def x_transposes(par, e, first):
                pe.wait_ge(s[f"gathered{par}"], 8 * (e - par) + 16)
                if not first:
                    pe.wait_ge(s["xt_ready"], e - 1)
                pe.sem_inc(s["pe_passed"], 1)
                for k in range(KD):
                    ins = nc.tensor.transpose(PS[:, par, B * k:B * k + B], xg[:, par, k::KD], ident[0:B, 0:B])
                ins.then_inc(s["xt_full"], 1)

            def up(slot, par, e, first, turn):
                pe.wait_ge(expert_loaded[slot], 16 * LOADS * (turn + 1))
                pe.wait_ge(s["xt_ready"], e + 1)
                if not first:
                    pe.wait_ge(s["hid_ready"], e - 1)
                up_products(slot, par).then_inc(s["ab_full"], 1)

            def up_products(slot, par):
                for w in range(2):
                    for j in range(2):
                        for k in range(KD):
                            ins = mm(PS[:, 2 + par, B * (2 * w + j):B * (2 * w + j) + B], E13[slot][:, w, k, 128 * j:128 * j + 128],
                                     xT[:, par, k, :], start=(k == 0), stop=(k == KD - 1))
                return ins

            def down(slot, par, e, first):
                pe.wait_ge(s["hid_ready"], e + 1)
                if not first:
                    pe.wait_ge(s["y_act"], e - 1)
                    pe.wait_ge(s["y_dve"], e - 1)
                down_products(slot, par).then_inc(s["y_mm"], 1)

            def down_products(slot, par):
                for c in range(2):
                    for j in range(2):
                        ins = mm(PS[0:B, 4 + 2 * par + c, :], hid[:, par, j, :], E2[slot][:, j, 512 * c:512 * c + 512],
                                 start=(j == 0), stop=(j == 1))
                return ins

            x_transposes(0, 0, True)
            for e in range(4):
                up(e, e % 2, e, e < 2, 0)
                x_transposes((e + 1) % 2, e + 1, e + 1 < 2)
                if e > 0:
                    down(e - 1, (e - 1) % 2, e - 1, e - 1 < 2)
            with pe.Fori(1, NE // 4) as i:
                for u in range(4):
                    e = i * 4 + u
                    up(u, u % 2, e, False, i)
                    x_transposes((u + 1) % 2, e + 1, False)
                    down((u - 1) % 4, (u - 1) % 2, e - 1, False)
            down(3, 1, NE - 1, False)

            pe.wait_ge(s["xt_ready"], NE + 1)
            pe.wait_ge(s["y_act"], NE)
            pe.wait_ge(s["y_dve"], NE)
            pe.wait_ge(s["idx_ready"], 1)
            blocks = pe.value_load(ovi[0:1, NOV:NOV + 1], min_val=0, max_val=NOV)
            with pe.Fori(0, NOV) as i:
                with pe.If(i < blocks):
                    pe.wait_ge(s["ov_gathered"], 16 * i + 16)
                    pe.sem_inc(s["pe_passed"], 1)
                    for k in range(KD):
                        ins = nc.tensor.transpose(PS[:, 0, B * k:B * k + B], xg[:, 1, k::KD], ident[0:B, 0:B])
                    ins.then_inc(s["ov_xt_full"], 1)
                    pe.wait_ge(s["ov_xt_ready"], i + 1)
                    pe.wait_ge(s["ov_w"], 16 * LOADS * i + 16 * LOADS)
                    up_products(0, 0).then_inc(s["ov_ab"], 1)
                    pe.wait_ge(s["ov_hid"], i + 1)
                    down_products(0, 0).then_inc(s["ov_y_mm"], 1)

        @block.scalar
        def _(act):
            st = Steps(act, s["act_step"])
            fn = nc.scalar.activation
            junk_at = [None] * 4

            def full(key):
                act.wait_ge(s["psum_full"], UNIT_NO[key] + 1)
                return bank(key)

            def empty(dst, src, func=ACT.Copy, **kw):
                return st.mark(fn(dst, src, func, **kw), s["emptied_act"])

            def sumsq(key, srcs, *after):
                n = norm_rows(key)
                st.after(*after)
                for h, src in enumerate(srcs):
                    w = src.free_size()
                    parts = [h % 4] if w <= 256 else [0, 1, 2, 3]
                    for m in {junk_at[q] for q in parts if junk_at[q]}:
                        st.after(m)
                    q = parts[0]
                    ins = fn(junk[0:n, 256 * q:256 * q + w], src, ACT.Square, accum_out=sums[0:n, NORM_NO[key], h:h + 1])
                    m = st.mark(ins, s["sums_ready"] if h == len(srcs) - 1 else None)
                    for q in parts:
                        junk_at[q] = m

            act.wait_ge(s["x_loaded"], 16 * NT)
            for t, (f, n) in enumerate(TILES):
                sumsq(("x", t), [X0[0:n, t, :]])
            act.wait_ge(s["s5_loaded"], 16 * 5)
            fn(s5raw[:, 4, :].rearrange("q (g p) -> q g p", g=2), dtraw[:, :, None].broadcast_to([GP, 2, ST]),
               ACT.Exp).then_inc(s["s5_raw_ready"], 1)
            empty(s5par[:].rearrange("p n q -> p (n q)"), full("par")[:, 0:5 * GP])
            for t, (f, n) in enumerate(TILES):
                for g in range(2):
                    empty(hT[:, 4 * g:4 * g + 4, f:f + n], full(("xT", t, g))[:, 0:4 * n].rearrange("p (k n) -> p k n", k=4))
            act.wait_ge(s["mem_loaded"], 16 * 3)
            for t in range(2):
                sumsq(("m", t), [mem[:, t, :]])
            act.wait_ge(s["s5_scaled"], 1)
            fn(s5tmp[:, 2, :], s5tmp[:, 0, :], ACT.Exp).then_inc(s["s5_mag_ready"], 1)
            for m in range(4):
                empty(uT[:, m, :], full(("u", m))[:, 0:TOK])
            act.wait_ge(s["s5_reduced"], 1)
            fn(s5tmp[:, 5, :], s5tmp[:, 4, :], ACT.Sin).then_inc(s["s5_sin_ready"], 1)
            fn(s5tmp[:, 6, :], s5tmp[:, 4, :], ACT.Sin, scale=0.5).then_inc(s["s5_sin_ready"], 1)
            copied = [empty(qlat[0:n, t, :], full(("ql", t))[0:n, 0:QL]) for t, (f, n) in enumerate(TILES)]
            for t, (f, n) in enumerate(TILES):
                sumsq(("ql", t), [qlat[0:n, t, :]], copied[t])
            copied = [empty(ckv[0:n, KEY_OF_TILE[t], :], full(("kv", t))[0:n, 0:KVL + ROPE]) for t, (f, n) in enumerate(TILES)]
            for t, (f, n) in enumerate(TILES):
                sumsq(("ck", t), [ckv[0:n, KEY_OF_TILE[t], 0:KVL]], copied[t])
            for c in range(2):
                copied = [empty(qmem[0:n, t, 256 * c:256 * c + 256], full((f"qm{c}", t))[0:n, 0:256]) for t, (f, n) in enumerate(TILES)]
            for t, (f, n) in enumerate(TILES):
                sumsq(("qm", t), [qmem[0:n, t, MD * h:MD * h + MD] for h in range(MH)], copied[t])
            act.wait_ge(s["mem_ready"], 2)
            for t in range(2):
                for g in range(2):
                    empty(memT[:, 4 * g:4 * g + 4, 128 * t:128 * t + 128],
                          full(("memT", t, g)).rearrange("p (k n) -> p k n", k=4))
            for name, dst in (("mk", mk), ("mv", mv)):
                for c in range(2):
                    copied = [empty(dst[:, 0, t, 256 * c:256 * c + 256], full((f"{name}{c}", t))[:, 0:256]) for t in range(2)]
            for t in range(2):
                sumsq(("mk", t), [mk[:, 0, t, MD * h:MD * h + MD] for h in range(MH)], copied[t])
            for n in range(4):
                dst = wB[:, n] if n < 2 else wC[:, n - 2]
                empty(dst.rearrange("p t s -> p (t s)"), full(("s5T", n)))
            def memory_keys(src, kt):
                empty(mkT[:, src, :, 128 * kt:128 * kt + 128], full(("mkT", src, kt)).rearrange("p (h n) -> p h n", h=MH))

            def memory_queries(t):
                f, n = TILES[t]
                empty(qmT[:, :, f:f + n], full(("qmT", t))[:, 0:MH * n].rearrange("p (h n) -> p h n", h=MH))

            def attention(kind, units, step, m):
                unit0, oT = (0, oTmem) if kind == "mem" else (len(MEM_UNITS), oTmla)
                if step == "OT":
                    f, n = TILES[m]
                    empty(oT[:, :, f:f + n], full((kind, "OT", m))[:, 0:4 * n].rearrange("p (j n) -> p j n", j=4))
                    return
                _, t, h0, nh = units[m]
                n = TILES[t][1]
                kb = key_blocks(units[m])
                nk = sum(kb)
                if step == "S":
                    src = full((kind, "S", m))
                    act.wait_ge(s["scores_max"], unit0 + m + 1)
                    w = (unit0 + m) % 4
                    scale = 1.0 if kind == "mla" and t < 2 else SCALE_MEM if kind == "mem" else SCALE_MLA
                    for h in range(nh):
                        ins = fn(P[0:n, m % 2, nk * h:nk * h + nk], src[0:n, nk * h:nk * h + nk], ACT.Exp,
                                 bias=soft[0:n, w, 0, h:h + 1], scale=scale, accum_out=soft[0:n, w, 1, h:h + 1])
                        st.mark(ins, s["emptied_act"] if h == nh - 1 else None)
                elif step == "PT":
                    src = full((kind, "PT", m))
                    if kb[-1] == 128:
                        empty(PT[:, m % 2, 0:n * nh * len(kb)], src[:, 0:n * nh * len(kb)])
                    else:
                        whole = n * (len(kb) - 1)
                        st.mark(fn(PT[:, m % 2, 0:whole], src[:, 0:whole], ACT.Copy))
                        empty(PT[0:kb[-1], m % 2, whole:whole + n], src[0:kb[-1], whole:whole + n])

            def query_latents(t):
                f, n = TILES[t]
                if t == 0:
                    act.wait_ge(s["stored"], 16 * 10)
                empty(qlT[:, :, f:f + n], full(("qlT", t))[:, 0:3 * n].rearrange("p (k n) -> p k n", k=3))

            def key_latents(j):
                f, n = KEYS[j]
                empty(ckT[:, :, f:f + n], full(("ckT", j))[:, 0:2 * n].rearrange("p (k n) -> p k n", k=2))

            def latents_up(m):
                what, j, half = KQ_UNITS[m]
                src = full(("kq", m))
                dst = KQ[:, m % KQ_BUFS]
                if what == "k":
                    n = KEYS[j][1]
                    view = src[0:n, :].rearrange("p (h d) -> p h d", h=4)
                    m1 = st.mark(fn(dst[0:n, :, 0:NOPE], view[:, :, 0:NOPE], ACT.Copy))
                    m2 = st.mark(fn(dst[0:n, :, NOPE:], ckv[0:n, j, None, KVL:].broadcast_to([n, 4, ROPE]), ACT.Copy))
                    empty(V[0:n, j, 256 * half:256 * half + 256].rearrange("p (h d) -> p h d", h=4), view[:, :, NOPE:])
                    sumsq(("kq", m), [dst[0:n, h, :] for h in range(4)], m1, m2)
                else:
                    n = TILES[j][1]
                    m1 = empty(dst[0:n].rearrange("p h d -> p (h d)"), src[0:n, 0:4 * QK])
                    sumsq(("kq", m), [dst[0:n, h, :] for h in range(4)], m1)

            def heads_transposed(m):
                what, j, half = KQ_UNITS[m]
                f, n = KEYS[j] if what == "k" else TILES[j]
                dst = kT if what == "k" else qT
                if (what, j, half) == ("q", 0, 0):
                    act.wait_ge(s["y_filled"], 16 * len(FILLS))
                empty(dst[0:QK, 4 * half:4 * half + 4, f:f + n],
                      full(("kqT", m))[0:QK, 0:4 * n].rearrange("p (h n) -> p h n", h=4))

            run = {"mkT": memory_keys, "qmT": memory_queries, "qlT": query_latents, "ckT": key_latents,
                   "kq": latents_up, "kqT": heads_transposed}
            for kind, *which in MIDDLE:
                if kind in ("mem", "mla"):
                    attention(kind, MEM_UNITS if kind == "mem" else MLA_UNITS, *which)
                elif kind in run:
                    run[kind](*which)
                elif kind.startswith("gate"):
                    if (kind, which[0]) == ("gateA", 0):
                        act.wait_ge(s["stored"], 16 * 10)
                    dst = {"A": gateA, "B": gateB, "C": mergedT}[kind[-1]]
                    empty(dst[:, which[0], :], full((kind, which[0]))[:, 0:TOK], ACT.Tanh, scale=0.5)
            act.wait_ge(s["finals_full"], 1)
            st.mark(fn(finrow[:].rearrange("q n p -> q (n p)"), PS[0:GP, BU, :], ACT.Copy), s["finals_out"])
            for t in range(4):
                act.wait_ge(s["y_skipped"], t + 1)
                fn(gelu[:, t, :], uT[:, t, :], ACT.Square).then_inc(s["y_square"], 1)
            for t in range(4):
                act.wait_ge(s["y_inner"], t + 1)
                fn(gelu[:, t, :], gelu[:, t, :], ACT.Tanh, scale=math.sqrt(2 / math.pi)).then_inc(s["y_tanh"], 1)
            for d in range(KD):
                src = full(("glug", d))
                if d >= 2:
                    act.wait_ge(*emptied_at(UNIT_NO["gluv", d - 2]))
                empty(gsig[:, d % 2, :], src[:, 0:TOK], ACT.Tanh, scale=0.5)
            for t, (f, n) in enumerate(TILES):
                act.wait_ge(*emptied_at(UNIT_NO["wout", 2, t]))
                sumsq(("f", t), [X[0:n, t, :]])
                for g in range(2):
                    empty(h2T[:, 4 * g:4 * g + 4, f:f + n], full(("h2T", t, g))[:, 0:4 * n].rearrange("p (k n) -> p k n", k=4))
            act.wait_ge(s["logits_in"], 1)
            fn(ex4[:, 1], ex4[:, 0], ACT.Exp).then_inc(s["logits_exp"], 1)
            act.wait_ge(s["logits_in"], 2)
            fn(rs[:, 5, :], rs[:, 4, :], ACT.Exp).then_inc(s["logits_exp"], 1)
            def x_copy(par, e, first):
                act.wait_ge(s["xt_full"], e + 1)
                if not first:
                    act.wait_ge(s["ab_full"], e - 1)
                fn(xT[:, par].rearrange("p k n -> p (k n)"), PS[:, par, 0:KD * B], ACT.Copy).then_inc(s["xt_ready"], 1)

            def gate(par, e, first):
                act.wait_ge(s["ab_full"], e + 1)
                if not first:
                    act.wait_ge(s["hid_ready"], e - 1)
                fn(tg[:, par].rearrange("p j n -> p (j n)"), PS[:, 2 + par, 0:2 * B], ACT.Tanh, scale=0.5)\
                    .then_inc(s["tanh_ready"], 1)

            def y_copy(par, e, first):
                act.wait_ge(s["y_mm"], e + 1)
                if not first:
                    act.wait_ge(s[f"y_stored{par}"], 8 * (e - par))
                fn(yb[:, par, 0:512], PS[0:B, 4 + 2 * par, :], ACT.Copy).then_inc(s["y_act"], 1)

            x_copy(0, 0, True)
            for e in range(4):
                gate(e % 2, e, e < 2)
                x_copy((e + 1) % 2, e + 1, e + 1 < 2)
                if e > 0:
                    y_copy((e - 1) % 2, e - 1, e - 1 < 2)
            with act.Fori(1, NE // 4) as i:
                for u in range(4):
                    e = i * 4 + u
                    gate(u % 2, e, False)
                    x_copy((u + 1) % 2, e + 1, False)
                    y_copy((u - 1) % 2, e - 1, False)
            y_copy(1, NE - 1, False)
            act.wait_ge(s["idx_ready"], 1)
            blocks = act.value_load(ovi[0:1, NOV:NOV + 1], min_val=0, max_val=NOV)
            with act.Fori(0, NOV) as i:
                with act.If(i < blocks):
                    act.wait_ge(s["ov_xt_full"], i + 1)
                    fn(xT[:, 0].rearrange("p k n -> p (k n)"), PS[:, 0, 0:KD * B], ACT.Copy).then_inc(s["ov_xt_ready"], 1)
                    act.wait_ge(s["ov_ab"], i + 1)
                    fn(tg[:, 0].rearrange("p j n -> p (j n)"), PS[:, 2, 0:2 * B], ACT.Tanh, scale=0.5).then_inc(s["ov_tanh"], 1)
                    act.wait_ge(s["y_stored0"], 8 * NE)
                    act.wait_ge(s["ov_stored"], i * 16)
                    act.wait_ge(s["ov_y_mm"], i + 1)
                    fn(yb[:, 0, 0:512], PS[0:B, 4, :], ACT.Copy).then_inc(s["ov_y_act"], 1)

        @block.vector
        def _(dve):
            st = Steps(dve, s["dve_step"])
            V_ = nc.vector

            def full(key):
                dve.wait_ge(s["psum_full"], UNIT_NO[key] + 1)
                return bank(key)

            def link(ins, sem_=None):
                st.after(st.mark(ins, sem_))

            def norm(key):
                dve.wait_ge(s["rstd_ready"], NORM_NO[key] + 1)
                return rstd[0:norm_rows(key), NORM_NO[key], 0:NORM_HEADS[key[0]]]

            def scaled_rows(dst, src, r, gain, ready):
                V_.scalar_tensor_tensor(dst, src, r, gain, ALU.mult, ALU.mult).then_inc(ready, 1)

            def scaled_heads(rows_, key, heads, gain, ready):
                n = norm_rows(key)
                r = norm(key)
                for h in range(heads):
                    ins = V_.scalar_tensor_tensor(rows_[:, h, :], rows_[:, h, :], r[:, h:h + 1], gain[0:n], ALU.mult, ALU.mult)
                    if h < heads - 1:
                        st.mark(ins)
                return ins

            dve.wait_ge(s["gains_loaded"], 16 * 7)
            for t, (f, n) in enumerate(TILES):
                scaled_rows(Hn[0:n, t, :], X0[0:n, t, :], norm(("x", t)), grow[0:n, :], s["h_ready"])
            gmem = memT[:, 0:4, :].rearrange("p k n -> p (k n)")
            dve.wait_ge(s["mem_loaded"], 16 * 3)
            for t in range(2):
                scaled_rows(mem[:, t, :], mem[:, t, :], norm(("m", t)), gmem, s["mem_ready"])
            dve.wait_ge(s["s5_den"], 1)
            V_.reciprocal(s5tmp[:, 11, :], s5tmp[:, 10, :]).then_inc(s["s5_rden"], 1)
            for t, (f, n) in enumerate(TILES):
                scaled_rows(qlat[0:n, t, :], qlat[0:n, t, :], norm(("ql", t)), g_ql[0:n], s["ql_ready"])
            for t, (f, n) in enumerate(TILES):
                c = ckv[0:n, KEY_OF_TILE[t], 0:KVL]
                scaled_rows(c, c, norm(("ck", t)), g_kv[0:n], s["ck_ready"])
            for t, (f, n) in enumerate(TILES):
                scaled_heads(qmem[0:n, t].rearrange("p (h d) -> p h d", h=MH), ("qm", t), MH, g_mq, None).then_inc(s["qm_ready"], 1)
            for t in range(2):
                scaled_heads(mk[:, 0, t].rearrange("p (h d) -> p h d", h=MH), ("mk", t), MH, g_mk, None).then_inc(s["mk_ready"], 1)

            def s5_turn(q):
                def win(x):
                    return x.rearrange("p (w j) -> p w j", j=WIN)

                cb = cosT[:, q, None, :].broadcast_to([128, NWIN, WIN])
                sb_ = sinT[:, q, None, :].broadcast_to([128, NWIN, WIN])
                if q == 0:
                    dve.wait_ge(s["s5_tables"], 1)
                dve.wait_ge(s["bu_full"], q + 1)
                re, im = PS[:, BU, 0:TOK], PS[:, BU + 1, 0:TOK]
                m1 = st.mark(V_.tensor_tensor(win(rotA[:, 0]), win(re), cb, ALU.mult))
                m2 = st.mark(V_.tensor_tensor(win(rotB[:, 0]), win(im), sb_, ALU.mult))
                m3 = st.mark(V_.tensor_tensor(win(rotA[:, 1]), win(im), cb, ALU.mult))
                m4 = st.mark(V_.tensor_tensor(win(rotB[:, 1]), win(re), sb_, ALU.mult), s["bu_free"])
                st.after(m2)
                m5 = st.mark(V_.tensor_tensor(rotA[:, 0], rotA[:, 0], rotB[:, 0], ALU.add))
                st.after(m4, m3)
                m6 = st.mark(V_.tensor_tensor(rotA[:, 1], rotA[:, 1], rotB[:, 1], ALU.subtract))
                mag = s5tmp[:, 2, q:q + 1].broadcast_to([128, WIN])

                def scan(w, c, initial):
                    return st.mark(V_.tensor_tensor_scan(rotB[:, c, WIN * w:WIN * w + WIN], mag, rotA[:, c, WIN * w:WIN * w + WIN],
                                                         initial, ALU.mult, ALU.add))

                st.after(m6)
                last = [scan(0, 0, 0.0), scan(0, 1, 0.0)]
                sample = [scan(NWIN - 1, c, s5par[:, 2 + c, q:q + 1]) for c in range(2)]
                for w in range(1, NWIN - 1):
                    end = slice(WIN * w - 1, WIN * w)
                    c64, s64, n64 = cosT[:, q, WIN - 1:WIN], sinT[:, q, WIN - 1:WIN], s5tmp[:, 8, q:q + 1]
                    cr = carry[:, q % 2, w - 1]
                    st.after(last[1])
                    m7 = st.mark(V_.tensor_scalar(cr[:, 0:2], rotB[:, :, end].rearrange("p c o -> p (c o)"), c64, None, ALU.mult))
                    st.after(m7)
                    st.mark(V_.scalar_tensor_tensor(cr[:, 2:3], rotB[:, 1, end], n64, cr[:, 0:1], ALU.mult, ALU.add))
                    m8 = st.mark(V_.scalar_tensor_tensor(cr[:, 3:4], rotB[:, 0, end], s64, cr[:, 1:2], ALU.mult, ALU.add))
                    st.after(m8)
                    last = [scan(w, c, cr[:, 2 + c:3 + c]) for c in range(2)]
                st.after(last[1])
                dst = hS[:, q % 2]
                m1 = st.mark(V_.tensor_tensor(win(rotA[:, 0]), win(rotB[:, 0]), cb, ALU.mult))
                m2 = st.mark(V_.tensor_tensor(win(rotC[:, 0]), win(rotB[:, 1]), sb_, ALU.mult))
                m3 = st.mark(V_.tensor_tensor(win(rotA[:, 1]), win(rotB[:, 1]), cb, ALU.mult))
                m4 = st.mark(V_.tensor_tensor(win(rotC[:, 1]), win(rotB[:, 0]), sb_, ALU.mult))
                if q >= 2:
                    dve.wait_ge(s["y_full"], q - 1)
                st.after(m2)
                m5 = st.mark(V_.tensor_tensor(dst[:, 0], rotA[:, 0], rotC[:, 0], ALU.subtract))
                st.after(m4)
                m6 = st.mark(V_.tensor_tensor(dst[:, 1], rotA[:, 1], rotC[:, 1], ALU.add), s["h_state"])
                st.after(m6)
                st.mark(V_.tensor_copy(finals[:, :, :, q].rearrange("p s c -> p c s"), dst[:, :, SEQ - 1:TOK:DEC]), s["finals_copied"])
                if q % 4 == 0 and q > 0:
                    y_skip(q // 4 - 1)

            def y_skip(t):
                dve.wait_ge(s["y_full"], 4 * t + 4)
                V_.scalar_tensor_tensor(uT[:, t, :], uT[:, t, :], dskip[:, t:t + 1], PS[:, YB, 0:TOK], ALU.mult, ALU.add)\
                    .then_inc(s["y_skipped"], 1)

            dve.wait_ge(s["params_loaded"], 16 * 7)
            def attention(kind, units, step, m):
                if step not in ("S", "O"):
                    return
                unit0 = 0 if kind == "mem" else len(MEM_UNITS)
                _, t, h0, nh = units[m]
                n = TILES[t][1]
                nk = sum(key_blocks(units[m]))
                w = soft[0:n, (unit0 + m) % 4]
                if step == "S":
                    src = full((kind, "S", m))[0:n, 0:nh * nk]
                    heads = src.rearrange("p (h k) -> p h k", h=nh)
                    if kind == "mla" and t < 2:
                        mask = const(f"mask{t}")[0:n, None, :].broadcast_to([n, nh, nk])
                        link(V_.scalar_tensor_tensor(heads, heads, SCALE_MLA, mask, ALU.mult, ALU.add))
                        V_.tensor_reduce(w[:, 0, 0:nh], heads, AX.X, ALU.max, negate=True).then_inc(s["scores_max"], 1)
                    else:
                        link(V_.tensor_reduce(w[:, 0, 0:nh], heads, AX.X, ALU.max, negate=True))
                        V_.tensor_scalar(w[:, 0, 0:nh], w[:, 0, 0:nh], SCALE_MEM if kind == "mem" else SCALE_MLA, None, ALU.mult)\
                            .then_inc(s["scores_max"], 1)
                else:
                    dv = MD if kind == "mem" else VH
                    src = full((kind, "O", m))[0:n, 0:nh * dv].rearrange("p (h d) -> p h d", h=nh)
                    link(V_.reciprocal(w[:, 2, 0:nh], w[:, 1, 0:nh]))
                    st.mark(V_.tensor_tensor(O[0:n, t, dv * h0:dv * (h0 + nh)].rearrange("p (h d) -> p h d", h=nh), src,
                                             w[:, 2, 0:nh, None].broadcast_to([n, nh, dv]), ALU.mult), s["emptied_dve"])

            def heads_up(m):
                what, j, half = KQ_UNITS[m]
                n = KEYS[j][1] if what == "k" else TILES[j][1]
                where = POS_OF_KEY[j if what == "k" else KEY_OF_TILE[j]]
                x = KQ[0:n, m % KQ_BUFS]
                link(scaled_heads(x, ("kq", m), 4, g_kn if what == "k" else g_qn, None))
                r = x[:, :, NOPE:]
                hr = ROPE // 2
                a_, b_ = ropet[0:n, m % 2, 0], ropet[0:n, m % 2, 1]
                cos_, sin_ = rope[0:n, where, 0, None, :], rope[0:n, where, 1, None, :]
                st.mark(V_.tensor_tensor(a_, r, cos_.broadcast_to([n, 4, ROPE]), ALU.mult))
                st.mark(V_.tensor_tensor(b_[:, :, 0:hr], r[:, :, hr:], sin_[:, :, 0:hr].broadcast_to([n, 4, hr]), ALU.mult))
                link(V_.tensor_tensor(b_[:, :, hr:], r[:, :, 0:hr], sin_[:, :, hr:].broadcast_to([n, 4, hr]), ALU.mult))
                V_.tensor_tensor(r, a_, b_, ALU.add).then_inc(s["kq_ready"], 1)

            def gated(kind, d):
                src = full((kind, d))[:, 0:TOK]
                if kind == "outC":
                    dve.wait_ge(*emptied_at(UNIT_NO["gateC", d]))
                    link(V_.scalar_tensor_tensor(mergedT[:, d, :], mergedT[:, d, :], 1.0, src, ALU.add, ALU.mult), s["emptied_dve"])
                else:
                    dve.wait_ge(*emptied_at(UNIT_NO["gateB", d]))
                    m = mtmp[:, d % 2, :]
                    link(V_.scalar_tensor_tensor(m, gateB[:, d, :], 1.0, src, ALU.add, ALU.mult), s["emptied_dve"])
                    st.mark(V_.tensor_tensor(mergedT[:, d, :], mergedT[:, d, :], m, ALU.add))

            for kind, *which in MIDDLE:
                if kind in ("mem", "mla"):
                    attention(kind, MEM_UNITS if kind == "mem" else MLA_UNITS, *which)
                elif kind == "turn":
                    s5_turn(*which)
                elif kind == "kq":
                    heads_up(*which)
                elif kind.startswith("out"):
                    gated(kind, *which)
            y_skip(3)
            for t in range(4):
                dve.wait_ge(s["y_square"], t + 1)
                link(V_.tensor_scalar(gelu[:, t, :], gelu[:, t, :], 0.044715, 1.0, ALU.mult, ALU.add))
                V_.tensor_tensor(gelu[:, t, :], gelu[:, t, :], uT[:, t, :], ALU.mult).then_inc(s["y_inner"], 1)
            for t in range(4):
                dve.wait_ge(s["y_tanh"], t + 1)
                link(V_.tensor_scalar(gelu[:, t, :], gelu[:, t, :], 0.5, 0.5, ALU.mult, ALU.add))
                V_.tensor_tensor(uT[:, t, :], gelu[:, t, :], uT[:, t, :], ALU.mult).then_inc(s["z_ready"], 1)
            for d in range(KD):
                src = full(("gluv", d))[:, 0:TOK]
                dve.wait_ge(*emptied_at(UNIT_NO["glug", d]))
                m = mtmp[:, d % 2, :]
                link(V_.scalar_tensor_tensor(m, gsig[:, d % 2, :], 1.0, src, ALU.add, ALU.mult), s["emptied_dve"])
                if d == 0:
                    dve.wait_ge(*emptied_at(UNIT_NO["gateA", KD - 1]))
                link(V_.scalar_tensor_tensor(m, gateA[:, d, :], 1.0, m, ALU.add, ALU.mult))
                V_.scalar_tensor_tensor(mergedT[:, d, :], m, 0.5, mergedT[:, d, :], ALU.mult, ALU.add).then_inc(s["merged"], 1)
            dve.wait_ge(s["x_loaded"], 16 * 2 * NT)
            dve.wait_ge(s["gffn_loaded"], 16)
            link(V_.memset(lg[:], NEG))
            for t in range(NT + 1):
                if t < NT:
                    n = TILES[t][1]
                    for g, (d0, nd) in enumerate(DGROUPS):
                        src = full(("wout", g, t))[0:n, 0:128 * nd]
                        x = X[0:n, t, 128 * d0:128 * (d0 + nd)]
                        st.mark(V_.scalar_tensor_tensor(x, src, 0.5, x, ALU.mult, ALU.add), s["emptied_dve"])
                        if g == 0 and t > 0:
                            n1 = TILES[t - 1][1]
                            scaled_rows(h2[0:n1, t - 1, :], X[0:n1, t - 1, :], norm(("f", t - 1)), grow[0:n1, :], s["h2_ready"])
                else:
                    n1 = TILES[t - 1][1]
                    scaled_rows(h2[0:n1, t - 1, :], X[0:n1, t - 1, :], norm(("f", t - 1)), grow[0:n1, :], s["h2_ready"])
                if t > 0:
                    n1 = TILES[t - 1][1]
                    if t == 1:
                        dve.wait_ge(s["router_loaded"], 16 * 4)
                    src = full(("route", t - 1))
                    st.mark(V_.tensor_tensor(lg[0:n1, t - 1, 0:NG], src[0:n1, 0:NG], brow[0:n1, 0:NG], ALU.add))
                    st.mark(V_.tensor_tensor(lg[0:n1, t - 1, 8:40], src[0:n1, NG:NG + NE], brow[0:n1, NG:], ALU.add), s["emptied_dve"])

            st.after((s["emptied_dve"], st.count[s["emptied_dve"]]))
            for t in range(NT):
                st.mark(V_.max(r8[:, 0, t, :], lg[:, t, 0:8]))
            st.after((s["dve_step"], st.count[s["dve_step"]]))
            for t in range(NT):
                st.mark(V_.max_index(i8[:, 0, t, :], r8[:, 0, t, :], lg[:, t, 0:8]))
            V_.tensor_tensor(ex4[:, 0], lg[:, :, 0:NG], r8[:, 0, :, 0:1].broadcast_to([128, NT, NG]), ALU.subtract)\
                .then_inc(s["logits_in"], 1)
            st.after((s["dve_step"], st.count[s["dve_step"]]))
            link(V_.tensor_copy(rs[:, 0, :], i8[:, 0, :, 0]))
            link(V_.tensor_tensor(ex4[:, 2], const("iotae")[:, None, 0:NG].broadcast_to([128, NT, NG]),
                                  rs[:, 0, :, None].broadcast_to([128, NT, NG]), ALU.is_equal))
            link(V_.tensor_tensor(prod[:], lg[:, :, 8:40].rearrange("p t (g e) -> p t e g", g=NG),
                                  ex4[:, 2, :, None, :].broadcast_to([128, NT, EPG, NG]), ALU.mult))
            link(V_.tensor_reduce(r8[:, 1], prod[:], AX.X, ALU.add))
            for t in range(NT):
                st.mark(V_.max(r8[:, 2, t, :], r8[:, 1, t, :]))
            st.after((s["dve_step"], st.count[s["dve_step"]]))
            for t in range(NT):
                st.mark(V_.max_index(i8[:, 1, t, :], r8[:, 2, t, :], r8[:, 1, t, :]))
            V_.tensor_tensor(rs[:, 4, :], r8[:, 2, :, 1], r8[:, 2, :, 0], ALU.subtract).then_inc(s["logits_in"], 1)
            st.after((s["dve_step"], st.count[s["dve_step"]]))
            for k in range(2):
                st.mark(V_.tensor_copy(rs[:, 1 + k, :], i8[:, 1, :, k]))
            st.after((s["dve_step"], st.count[s["dve_step"]]))
            iotae = const("iotae")[:, None, :].broadcast_to([128, NT, NE])

            def spread(x, m):
                return x[:, :, None].broadcast_to([128, NT, m])

            def row(x):
                return x[:, None, :].broadcast_to([128, NT, NE])

            for k in range(2):
                link(V_.scalar_tensor_tensor(rs[:, 1 + k, :], rs[:, 0, :], float(EPG), rs[:, 1 + k, :], ALU.mult, ALU.add))
                link(V_.tensor_tensor(Ek[:, k], iotae, spread(rs[:, 1 + k, :], NE), ALU.is_equal))
                link(V_.tensor_tensor(Ek[:, k], Ek[:, k], spread(const("valid"), NE), ALU.mult))
            V_.tensor_tensor(Ek[:, 2], Ek[:, 0], Ek[:, 1], ALU.add).then_inc(s["onehot_ready"], 1)
            dve.wait_ge(s["logits_exp"], 2)
            link(V_.tensor_reduce(rs[:, 8, :], ex4[:, 1], AX.X, ALU.add))
            link(V_.reciprocal(rs[:, 9, :], rs[:, 8, :]))
            link(V_.tensor_scalar(rs[:, 10, :], rs[:, 5, :], 1.0, None, ALU.add))
            link(V_.reciprocal(rs[:, 11, :], rs[:, 10, :]))
            link(V_.scalar_tensor_tensor(rs[:, 6, :], rs[:, 11, :], 0.5, rs[:, 9, :], ALU.mult, ALU.mult))
            link(V_.tensor_tensor(rs[:, 7, :], rs[:, 6, :], rs[:, 5, :], ALU.mult))
            src = full("rank")
            R, J, BK, T1 = rk[:, 0], rk[:, 1], rk[:, 2], rk[:, 3]
            n_, nb, incl, excl = cnt[:, 0], cnt[:, 1], cnt[:, 2], cnt[:, 3]
            st.mark(V_.tensor_copy(R.rearrange("p t e -> p (t e)"), src[:, 0:NT * NE]))
            link(V_.tensor_copy(n_, src[:, NT * NE:NT * NE + NE]), s["emptied_dve"])
            link(V_.tensor_scalar(J, R, float(B), None, ALU.is_ge))
            link(V_.tensor_scalar(nb, n_, float(B), None, ALU.is_gt))
            for j in range(2, NJ + 1):
                link(V_.scalar_tensor_tensor(J, R, float(B * j), J, ALU.is_ge, ALU.add))
                link(V_.scalar_tensor_tensor(nb, n_, float(B * j), nb, ALU.is_gt, ALU.add))
            link(V_.tensor_tensor_scan(incl, const("ones")[:, 0:NE], nb, 0.0, ALU.mult, ALU.add))
            link(V_.tensor_tensor(excl, incl, nb, ALU.subtract))
            link(V_.scalar_tensor_tensor(R, J, -float(B), R, ALU.mult, ALU.add))
            link(V_.tensor_tensor(cnt[:, 4], excl, const("iotae"), ALU.subtract))
            link(V_.tensor_scalar(cnt[:, 4], cnt[:, 4], float(NE - 1), None, ALU.add))
            link(V_.tensor_tensor(BK, J, row(cnt[:, 4]), ALU.add))
            link(V_.tensor_scalar(T1, J, 0.5, None, ALU.is_gt))
            link(V_.tensor_tensor(BK, BK, T1, ALU.mult))
            link(V_.tensor_tensor(BK, BK, iotae, ALU.add))
            for k in range(2):
                link(V_.tensor_tensor(tp[:, 2 * k], Ek[:, k], R, ALU.mult))
                link(V_.tensor_reduce(rs[:, 12 + k, :], tp[:, 2 * k], AX.X, ALU.add))
                link(V_.tensor_tensor(tp[:, 2 * k + 1], Ek[:, k], BK, ALU.mult))
                link(V_.tensor_reduce(rs[:, 14 + k, :], tp[:, 2 * k + 1], AX.X, ALU.add))
                link(V_.scalar_tensor_tensor(rs[:, 16 + k, :], rs[:, 14 + k, :], float(B), rs[:, 12 + k, :], ALU.mult, ALU.add))
                link(V_.tensor_copy(pos[:, k, :], rs[:, 16 + k, :]))
                link(V_.tensor_tensor(ohs[:, k], const("iotab")[:, None, :].broadcast_to([128, NT, B]),
                                      spread(rs[:, 12 + k, :], B), ALU.is_equal))
                link(V_.tensor_tensor(ohb[:, 2 + k], const("iotablk")[:, None, :].broadcast_to([128, NT, NBLK]),
                                      spread(rs[:, 14 + k, :], NBLK), ALU.is_equal))
                ins = V_.tensor_tensor(ohb[:, k], ohb[:, 2 + k], spread(const("tokid"), NBLK), ALU.mult)
                if k == 0:
                    link(ins)
                else:
                    ins.then_inc(s["tables_in"], 1)
            link(V_.tensor_tensor(ovcmp[:], incl[0:1, None, :].broadcast_to([1, NOV, NE]),
                                  const("iotablk")[0:1, 0:NOV, None].broadcast_to([1, NOV, NE]), ALU.is_le))
            link(V_.tensor_reduce(ovf[:, 0, :], ovcmp[:], AX.X, ALU.add))
            link(V_.tensor_scalar(ovf[:, 1, :], ovf[:, 0, :], float(NE - 1), None, ALU.min))
            link(V_.tensor_copy(ovi[:, 0:NOV], ovf[:, 1, :]))
            link(V_.tensor_copy(ovi[:, NOV:], incl[0:1, NE - 1:NE]))
            link(V_.tensor_copy(idx[:], full("table")[0:B, 0:NBLK]), s["emptied_dve"])
            V_.tensor_copy(rs[0:1, 20, 0:1], rs[0:1, 16, 0:1]).then_inc(s["idx_ready"], 1)

            def hidden(par, e, first):
                dve.wait_ge(s["tanh_ready"], e + 1)
                if not first:
                    dve.wait_ge(s["y_mm"], e - 1)
                hidden_products(par, s["dve_moe"], e, s["hid_ready"])

            def hidden_products(par, half, e, ready):
                x1 = PS[:, 2 + par, 0:2 * B]
                x3 = PS[:, 2 + par, 2 * B:4 * B]
                u_ = ug[:, par].rearrange("p j n -> p (j n)")
                V_.scalar_tensor_tensor(u_, tg[:, par].rearrange("p j n -> p (j n)"), 1.0, x1, ALU.add, ALU.mult).then_inc(half, 1)
                dve.wait_ge(half, e + 1)
                V_.tensor_tensor(hid[:, par].rearrange("p j n -> p (j n)"), u_, x3, ALU.mult).then_inc(ready, 1)

            def y_copy(par, e, first):
                dve.wait_ge(s["y_mm"], e + 1)
                if not first:
                    dve.wait_ge(s[f"y_stored{par}"], 8 * (e - par))
                V_.tensor_copy(yb[:, par, 512:], PS[0:B, 5 + 2 * par, :]).then_inc(s["y_dve"], 1)

            for e in range(4):
                hidden(e % 2, e, e < 2)
                if e > 0:
                    y_copy((e - 1) % 2, e - 1, e - 1 < 2)
            with dve.Fori(1, NE // 4) as i:
                for u in range(4):
                    e = i * 4 + u
                    hidden(u % 2, e, False)
                    y_copy((u - 1) % 2, e - 1, False)
            y_copy(1, NE - 1, False)
            blocks = dve.value_load(ovi[0:1, NOV:NOV + 1], min_val=0, max_val=NOV)
            with dve.Fori(0, NOV) as i:
                with dve.If(i < blocks):
                    dve.wait_ge(s["ov_tanh"], i + 1)
                    hidden_products(0, s["ov_half"], i, s["ov_hid"])
                    dve.wait_ge(s["y_stored0"], 8 * NE)
                    dve.wait_ge(s["ov_stored"], i * 16)
                    dve.wait_ge(s["ov_y_mm"], i + 1)
                    V_.tensor_copy(yb[:, 0, 512:], PS[0:B, 5, :]).then_inc(s["ov_y_dve"], 1)
            for t, (f, n) in enumerate(TILES):
                dve.wait_ge(s[f"rows_gathered{t}"], 32)
                link(V_.scalar_tensor_tensor(X[0:n, t, :], rows[0:n, 0, t, :], rs[0:n, 6, t:t + 1], X[0:n, t, :], ALU.mult, ALU.add))
                V_.scalar_tensor_tensor(X[0:n, t, :], rows[0:n, 1, t, :], rs[0:n, 7, t:t + 1], X[0:n, t, :], ALU.mult, ALU.add)\
                    .then_inc(s["out_ready"], 1)

        @block.gpsimd
        def _(pool):
            st = Steps(pool, s["pool_step"])
            g_ = nc.gpsimd

            def link(ins, sem_=None):
                st.after(st.mark(ins, sem_))

            def norms(first, last):
                for n in range(first, last):
                    key = NORMS[n]
                    rows_, heads = norm_rows(key), NORM_HEADS[key[0]]
                    pool.wait_ge(s["sums_ready"], n + 1)
                    link(g_.tensor_scalar(means[0:rows_, n, 0:heads], sums[0:rows_, n, 0:heads], 1.0 / NORM_WIDTH[key[0]], EPS, ALU.mult, ALU.add))
                    g_.tensor_tensor(rstd[0:rows_, n, 0:heads], means[0:rows_, n, 0:heads], const("half")[0:rows_, 0:heads], ALU.pow)\
                        .then_inc(s["rstd_ready"], 1)

            pool.wait_ge(s["const_loaded"], 16)
            norms(0, NORM_NO["m", 0])

            are, aim, dt = s5par[:, 0, :], s5par[:, 1, :], s5par[:, 4, :]
            tmp = [s5tmp[:, n, :] for n in range(24)]
            pool.wait_ge(*emptied_at(UNIT_NO["par"]))
            tt, ts = g_.tensor_tensor, g_.tensor_scalar
            link(tt(tmp[0], are, dt, ALU.mult), s["s5_scaled"])
            link(tt(tmp[1], aim, dt, ALU.mult))
            two_pi = 2 * math.pi
            link(ts(tmp[3], tmp[1], 1.0 / two_pi, None, ALU.mult))
            link(ts(tmp[3], tmp[3], 12582912.0, None, ALU.add))
            link(ts(tmp[3], tmp[3], 12582912.0, None, ALU.subtract))
            c1 = 6.28125
            c2 = float(np.float32(np.round((two_pi - c1) * 2 ** 21) / 2 ** 21))
            c3 = two_pi - c1 - c2
            src = tmp[1]
            for c in (c1, c2, c3):
                link(ts(tmp[9], tmp[3], c, None, ALU.mult))
                link(tt(tmp[4], src, tmp[9], ALU.subtract))
                src = tmp[4]
            link(ts(tmp[4], tmp[4], 3.141592, -3.141592, ALU.min, ALU.max), s["s5_reduced"])
            link(tt(tmp[9], are, are, ALU.mult))
            link(tt(tmp[10], aim, aim, ALU.mult))
            link(tt(tmp[10], tmp[9], tmp[10], ALU.add), s["s5_den"])
            norms(NORM_NO["m", 0], NORMS_BEFORE_S5)
            pool.wait_ge(s["s5_sin_ready"], 2)
            link(tt(tmp[7], tmp[6], tmp[6], ALU.mult))
            link(ts(tmp[7], tmp[7], -2.0, 1.0, ALU.mult, ALU.add))
            pool.wait_ge(s["s5_mag_ready"], 1)
            link(tt(tmp[14], tmp[2], tmp[7], ALU.mult))
            link(tt(tmp[15], tmp[2], tmp[5], ALU.mult))
            link(ts(tmp[16], tmp[14], -1.0, None, ALU.add))
            pool.wait_ge(s["s5_rden"], 1)
            for out, x, y, op in ((12, are, aim, ALU.add), (13, None, None, ALU.subtract)):
                if out == 12:
                    link(tt(tmp[17], tmp[16], are, ALU.mult))
                    link(tt(tmp[18], tmp[15], aim, ALU.mult))
                else:
                    link(tt(tmp[17], tmp[15], are, ALU.mult))
                    link(tt(tmp[18], tmp[16], aim, ALU.mult))
                link(tt(tmp[17], tmp[17], tmp[18], op))
                link(tt(tmp[out], tmp[17], tmp[11], ALU.mult))
            pool.wait_ge(s["psum_full"], UNIT_NO["xT", NT - 1, 1] + 1)
            pool.wait_ge(s["params_loaded"], 16 * 7)
            fre, fim = (x[:, :, None].broadcast_to([128, GP, CH]) for x in (tmp[12], tmp[13]))
            br, bi = braw[:, 0], braw[:, 1]
            for c, (p0, p1, op) in enumerate((((fre, br), (fim, bi), ALU.subtract), ((fre, bi), (fim, br), ALU.add))):
                st.mark(tt(btmp[:, 2 * c], p0[0], p0[1], ALU.mult))
                link(tt(btmp[:, 2 * c + 1], p1[0], p1[1], ALU.mult))
                link(tt(bbar[:, c], btmp[:, 2 * c], btmp[:, 2 * c + 1], op))
                st.mark(ts(bpad[:, c, :, 0, :], bbar[:, c], const("sel_b")[:, 0:1], None, ALU.mult))
                st.mark(ts(bpad[:, c, :, 1, :], bbar[:, c], const("sel_b")[:, 1:2], None, ALU.mult), s["s5_padded"])
            for c in range(2):
                st.mark(ts(cpad[:, c, :, 0, :], craw[:, c], const("sel_c")[:, 2 * c:2 * c + 1], None, ALU.mult))
                st.mark(ts(cpad[:, c, :, 1, :], craw[:, c], const("sel_c")[:, 2 * c + 1:2 * c + 2], None, ALU.mult), s["s5_padded"])
            st.mark(g_.tensor_copy(cosT[:, :, 0], tmp[7]))
            link(g_.tensor_copy(sinT[:, :, 0], tmp[5]))
            flat = btmp[:].rearrange("p n q c -> p (n q c)")
            n = 1
            while n < WIN:
                t1 = flat[:, 0:GP * n].rearrange("p (q j) -> p q j", q=GP)
                t2 = flat[:, 512:512 + GP * n].rearrange("p (q j) -> p q j", q=GP)
                cn, sn = (x[:, :, n - 1:n].broadcast_to([128, GP, n]) for x in (cosT, sinT))
                c0, s0 = cosT[:, :, 0:n], sinT[:, :, 0:n]
                st.mark(tt(t1, c0, cn, ALU.mult))
                link(tt(t2, s0, sn, ALU.mult))
                link(tt(cosT[:, :, n:2 * n], t1, t2, ALU.subtract))
                st.mark(tt(t1, s0, cn, ALU.mult))
                link(tt(t2, c0, sn, ALU.mult))
                link(tt(sinT[:, :, n:2 * n], t1, t2, ALU.add))
                n *= 2
            link(ts(tmp[8], sinT[:, :, WIN - 1], -1.0, None, ALU.mult), s["s5_tables"])
            norms(NORMS_BEFORE_S5, len(NORMS))

            pool.wait_ge(s["h2_stored"], 16 * NT)
            pool.wait_ge(s["idx_ready"], 1)
            for e in range(NE + 1):
                if e >= 2:
                    pool.wait_ge(s["xt_full"], e - 1)
                g_.indirect_dma_start(xg[:, e % 2, :], None, scratch["h2"], bass.IndirectOffsetOnAxis(ap=idx[:, e:e + 1], axis=0))\
                    .then_inc(s[f"gathered{e % 2}"], 16)
            blocks = pool.value_load(ovi[0:1, NOV:NOV + 1], min_val=0, max_val=NOV)
            pool.wait_ge(s["xt_full"], NE)
            with pool.Fori(0, NOV) as i:
                with pool.If(i < blocks):
                    pool.wait_ge(s["ov_xt_full"], i)
                    g_.tensor_copy(idx_ov[:, 0:1], idx[:, bass.ds(i + NE, 1)]).then_inc(s["ov_idx"], 1)
                    pool.wait_ge(s["ov_idx"], i + 1)
                    pool.sem_inc(s["pool_passed"], 1)
                    g_.indirect_dma_start(xg[:, 1, :], None, scratch["h2"], bass.IndirectOffsetOnAxis(ap=idx_ov[:, 0:1], axis=0))\
                        .then_inc(s["ov_gathered"], 16)
            pool.wait_ge(s["y_filled"], 16 * len(FILLS))
            pool.wait_ge(s["y_stored0"], 8 * NE)
            pool.wait_ge(s["y_stored1"], 8 * NE)
            pool.wait_ge(s["ov_stored"], blocks * 16)
            pool.sem_inc(s["pool_passed"], 1)
            for t, (f, n) in enumerate(TILES):
                for k in range(2):
                    g_.indirect_dma_start(rows[0:n, k, t, :], None, scratch["y"], bass.IndirectOffsetOnAxis(ap=pos[0:n, k, t:t + 1], axis=0))\
                        .then_inc(s[f"rows_gathered{t}"], 16)


NAMES = ["x_prompt", "x_sample", "cache_mla_ckv", "cache_mla_kpe", "cache_ssm_re", "cache_ssm_im", "cache_mem_k",
         "cache_mem_v", "mem_prompt", "g_attn", "w_in", "ssm_a_re", "ssm_a_im", "ssm_log_dt", "ssm_b_re", "ssm_b_im",
         "ssm_c_re", "ssm_c_im", "ssm_d", "w_glu", "g_qlat", "w_uq", "g_kvlat", "w_ukv", "g_qn", "g_kn", "w_o_mla",
         "g_mem", "w_mem_kv", "g_mqn", "g_mkn", "w_o_mem", "w_out", "g_ffn", "w_rg", "b_rg", "w_re", "b_re", "w_e1",
         "w_e3", "w_e2"]
OUTPUTS = [("y_p", (SEQ, D), (1, SEQ, D)), ("y_s", (DEC, D), (1, DEC, D)),
           ("ckv_p", (SEQ, KVL), (1, 1, SEQ, KVL)), ("kpe_p", (SEQ, ROPE), (1, 1, SEQ, ROPE)),
           ("sre_p", (GP, 128), (1, 1, G, ST)), ("sim_p", (GP, 128), (1, 1, G, ST)),
           ("mem_k", (MEMT, MH * MD), (1, 1, MEMT, MH, MD)), ("mem_v", (MEMT, MH * MD), (1, 1, MEMT, MH, MD)),
           ("ckv_s", (DEC, KVL), (1, 1, DEC, KVL)), ("kpe_s", (DEC, ROPE), (1, 1, DEC, ROPE)),
           ("sre_s", (GP, 128), (1, 1, G, ST)), ("sim_s", (GP, 128), (1, 1, G, ST))]


def kernel(**inputs):
    import concourse.bacc as bacc
    from concourse.bass_utils import run_bass_kernel_spmd

    nc = bacc.Bacc("TRN2", target_bir_lowering=False, num_devices=1)
    arrays = {f"in_{name}": np.ascontiguousarray(inputs[name]) for name in NAMES}
    arrays["in_consts"] = constants()
    a = {name[3:]: nc.dram_tensor(name, x.shape, mybir.dt.from_np(x.dtype), kind="ExternalInput").ap() for name, x in arrays.items()}
    o = {name: nc.dram_tensor(f"out_{name}", shape, F32, kind="ExternalOutput").ap() for name, shape, _ in OUTPUTS}
    scratch = {"h2": nc.dram_tensor("h2_rows", (TOK, D), F32, kind="Internal").ap(),
               "y": nc.dram_tensor("expert_rows", (NBLK * B, D), F32, kind="Internal").ap()}
    build(nc, a, o, scratch)
    r = run_bass_kernel_spmd(nc, [arrays], core_ids=[0])
    return tuple(np.asarray(r.results[0][f"out_{name}"]).reshape(shape) for name, _, shape in OUTPUTS)
```

```python
import math
from contextlib import ExitStack

import numpy as np

import concourse.bass as bass
from concourse import mybir

F32 = mybir.dt.float32
U32 = mybir.dt.uint32
I32 = mybir.dt.int32
ALU = mybir.AluOpType
ACT = mybir.ActivationFunctionType
AX = mybir.AxisListType

D = 1024
KD = D // 128
SEQ, DEC, PAST, MEMT = 256, 64, 256, 256
TOK = SEQ + DEC
TILES = [(0, 128), (128, 128), (256, 64)]
NT = len(TILES)
G, CH, ST = 32, 16, 64
GP = G // 2
WIN, NWIN = 64, TOK // 64
H, NOPE, ROPE, QK, VH = 8, 64, 32, 96, 64
QL, KVL = 384, 256
MH, MD = 4, 128
EPS = 1e-6
SCALE_MLA = 1.0 / math.sqrt(QK)
SCALE_MEM = 1.0 / math.sqrt(MD)
NEG = -1e30
NG, EPG = 4, 8
NE, FF = NG * EPG, 256
B = 64
NJ = (TOK - 1) // B
NOV = (2 * TOK - NE) // B
NBLK = NE + NOV
FILLS = [(f, min(128, NBLK * B - f)) for f in range(NE * B, NBLK * B, 128)]

KEYS = [(0, 128), (128, 128), (256, 128), (384, 128), (512, 64)]
KEY_OF_TILE = [0, 1, 4]
POS_OF_KEY = [0, 1, 0, 1, 2]

C_U, C_QL, C_KV, C_QM, C_GATE = 0, 512, 896, 1184, 1696
DGROUPS = [(0, 3), (3, 3), (6, 2)]
OGROUPS = [(0, 6), (6, 2)]
BRANCH_C, BRANCH_B, BRANCH_A = 2, 1, 0


def layout(parts):
    at, out = 0, {}
    for name, n in parts:
        out[name] = (at, at + n)
        at += n
    return out, at


CONST, NCONST = layout([("ident", 128), ("upper", 128), ("ones", 128), ("rope", 3 * 2 * ROPE),
                        ("mask0", 128), ("mask1", 256), ("iotab", B), ("iotablk", NBLK), ("iotae", NE),
                        ("sel_b", 2), ("sel_c", 4), ("valid", NT), ("tokid", NT), ("blocks", NJ)])


def constants():
    c = np.zeros((128, NCONST), np.float32)

    def put(name, value):
        a, b = CONST[name]
        c[:, a:b] = np.asarray(value, np.float32).reshape(128, b - a)

    p = np.arange(128)
    put("ident", np.eye(128))
    put("upper", p[:, None] < p[None, :])
    put("ones", np.ones((128, 128)))
    inv = (10000.0 ** (-np.arange(ROPE // 2, dtype=np.float32) / (ROPE // 2))).astype(np.float32)
    rope = np.zeros((128, 3, 2, ROPE), np.float32)
    for n in range(3):
        ang = (p + 128 * n).astype(np.float32)[:, None] * inv[None, :]
        rope[:, n, 0] = np.concatenate([np.cos(ang), np.cos(ang)], 1)
        rope[:, n, 1] = np.concatenate([-np.sin(ang), np.sin(ang)], 1)
    put("rope", rope)
    chunk = p[:, None] // 64
    put("mask0", np.where(p[None, :] // 64 <= chunk, 0, NEG))
    put("mask1", np.where(np.arange(256)[None, :] // 64 <= 2 + chunk, 0, NEG))
    put("iotab", np.tile(np.arange(B), (128, 1)))
    put("iotablk", np.tile(np.arange(NBLK), (128, 1)))
    put("iotae", np.tile(np.arange(NE), (128, 1)))
    put("sel_b", np.stack([p // ST == 0, p // ST == 1], 1))
    even = (p // CH) % 2 == 0
    put("sel_c", np.stack([even, ~even, -1.0 * even, -1.0 * ~even], 1))
    put("valid", np.stack([p < n for _, n in TILES], 1))
    put("tokid", np.stack([np.where(p < n, p + f, 0) for f, n in TILES], 1))
    put("blocks", np.tile(B * np.arange(1, NJ + 1), (128, 1)))
    return c


CHUNKS = [("u0", KD, 256), ("u1", KD, 256), ("qm0", KD, 256), ("qm1", KD, 256), ("mk0", KD, 256),
          ("mk1", KD, 256), ("mv0", KD, 256), ("mv1", KD, 256), ("ql", KD, QL), ("kv", KD, KVL + ROPE)]
SLOT_OF = [n % 3 for n in range(len(CHUNKS))]


def groups_of(name):
    return OGROUPS if name.startswith("out") else DGROUPS


def over_d(name, kt, per_tile, slots):
    CHUNKS.extend((f"{name}{g}", kt, per_tile * nd) for g, (d0, nd) in enumerate(groups_of(name)))
    SLOT_OF.extend(slots)


over_d("gateC", KD, 128, (1, 2, 0))
CHUNKS += [("ukv", 2, H * (NOPE + VH)), ("uq", 3, H * QK)]
SLOT_OF += [1, 2]
over_d("outC", 4, 128, (0, 1))
over_d("gateB", KD, 128, (0, 2, 1))
over_d("gateA", KD, 128, (0, 2, 1))
over_d("outB", 4, 128, (0, 2))
over_d("glu", 4, 256, (1, 0, 2))
over_d("wout", KD, 128, (1, 0, 2))
CHUNK_NO = {c[0]: n for n, c in enumerate(CHUNKS)}
WSLOTS, WSLOT = 3, 3072
FORMER = [max((m for m in range(n) if SLOT_OF[m] == SLOT_OF[n]), default=None) for n in range(len(CHUNKS))]

MEM_UNITS = [("mem", t, h, 2) for t in range(NT) for h in (0, 2)]
MLA_UNITS = ([("mla", 0, h, 4) for h in (0, 4)] + [("mla", 1, h, 2) for h in (0, 2, 4, 6)]
             + [("mla", 2, h, 1) for h in range(H)])
KQ_UNITS = [("k", j, half) for j in range(5) for half in (0, 1)] + [("q", t, half) for t in range(NT) for half in (0, 1)]
NORM_LAG, KQ_LAG, KQ_BUFS = 1, 4, 5
RING = 5


def key_blocks(unit):
    kind, t = unit[0], unit[1]
    if kind == "mem":
        return [128, 128]
    return [[128], [128, 128], [128, 128, 64]][t]


def attention_order(units):
    for n in range(len(units) + 2):
        if n < len(units):
            yield "S", n
        if 1 <= n <= len(units):
            yield "PT", n - 1
        if n >= 2:
            yield "O", n - 2
            if n - 1 == len(units) or units[n - 1][1] != units[n - 2][1]:
                yield "OT", units[n - 2][1]


PACE = 13.5
WORK = {"qm0": 3.4, "qm1": 3.4, "mk0": 3.4, "mk1": 3.4, "mv0": 3.4, "mv1": 3.4, "ql": 5.1, "kv": 3.8,
        "gateC": 4.3, "gateB": 4.3, "gateA": 4.3, "outC": 2.1, "outB": 2.1, "kq": 1.8, "mem": 0.8, "mla": 0.8}


def middle():
    out = []
    fills = []
    later = []
    spent, turn = 0.0, 0

    def put(*step):
        nonlocal spent, turn
        out.append(step)
        spent += WORK.get(step[0], 0.5)
        if later:
            out.append(later.pop(0))
        if started and turn < GP and spent >= turn * PACE and not any(x[0].startswith("turn") for x in later):
            start_turn()

    def start_turn():
        nonlocal turn
        out.append(("turn_in", turn))
        later[0:0] = [("turn_scan", turn, 0), ("turn_scan", turn, 1), ("turn_back", turn)]
        if turn % 4 == 1 and turn > 1:
            gelu_of(turn // 4 - 1)
        turn += 1

    def gelu_of(t):
        later.extend((stage, t) for stage in ("z0", "z1", "z2", "z3"))

    def fill(n=1):
        for _ in range(n):
            if fills:
                put(*fills.pop(0))

    def attention(kind, units, each):
        whole = []
        for step, m in attention_order(units):
            if step == "OT":
                whole.append(m)
                continue
            if m == len(units) - 1 and step in ("PT", "O"):
                fill(1)
            put(kind, step, m)
            if step == "S":
                fill(each)
                while whole:
                    put(kind, "OT", whole.pop(0))
        return whole

    started = False
    for name in ("qm0", "qm1"):
        for t in range(NT):
            put(name, t)
            if (name, t) == ("qm0", 1):
                put("s5_sin")
    for name in ("mk0", "mk1"):
        for t in range(2):
            put(name, t)
    for n in range(4):
        put("s5T", n)
    for t in range(NT):
        put("norm_qm", t)
    started, spent = True, 0.0
    for name in ("mv0", "mv1"):
        for t in range(2):
            put(name, t)
        for t in range(2) if name == "mv0" else ():
            put("norm_mk", t)
    fills = [("ql", t) for t in range(NT)] + [("kv", t) for t in range(NT)] + [("gateC", d) for d in range(KD)]
    for t in range(NT):
        put("qmT", t)
    for src in (1, 0):
        for kt in range(2):
            put("mkT", src, kt)
            fill()
    whole = attention("mem", MEM_UNITS, 1)
    for t in range(NT):
        put("norm_ql", t)
        put("norm_ck", t)
    fill(KD)
    fills = [("outC", d) for d in range(KD)]
    for t in range(NT):
        put("qlT", t)
    for t in whole:
        put("mem", "OT", t)
    for j in range(len(KEYS)):
        put("ckT", j)
    for n in range(len(KQ_UNITS) + KQ_LAG):
        if n < len(KQ_UNITS):
            put("kq", n)
        if n % 2 == 1 and n > 1:
            fill()
        if 0 <= n - NORM_LAG < len(KQ_UNITS):
            put("norm_kq", n - NORM_LAG)
        if n >= KQ_LAG:
            put("kqT", n - KQ_LAG)
    fill(KD)
    fills = [("gateB", d) for d in range(KD)] + [("gateA", d) for d in range(KD)]
    whole = attention("mla", MLA_UNITS, 1)
    fill(1)
    for t in whole:
        put("mla", "OT", t)
    while turn < GP:
        fill(1)
        out.extend(later)
        later.clear()
        start_turn()
    out.extend(later)
    later.clear()
    put("last_y")
    gelu_of(3)
    fill(1)
    put("finals")
    fill(KD)
    for d in range(KD):
        put("outB", d)
    out.extend(later)
    return out


MIDDLE = middle()
NOT_UNITS = ("turn_in", "turn_scan", "turn_back", "norm_qm", "norm_mk", "norm_kq", "norm_ql", "norm_ck",
             "z0", "z1", "z2", "z3", "last_y", "finals", "s5_sin")


def emptier(unit):
    if unit[0] in ("mem", "mla"):
        return {"S": "act", "PT": "act", "O": "dve", "OT": "act"}[unit[1]]
    return "dve" if unit[0].startswith("out") else "act"


def units_in_order():
    out = [(("xT", t, g), "act") for t in range(NT) for g in range(2)]
    out += [(("u", m), "act") for m in range(4)] + [("par", "act")]
    out += [(("memT", t, g), "act") for t in range(2) for g in range(2)]
    out += [(step, emptier(step)) for step in MIDDLE if step[0] not in NOT_UNITS]
    for d in range(KD):
        out += [(("glug", d), "act"), (("gluv", d), "dve")]
    for t in range(NT + 1):
        if t < NT:
            out += [(("wout", g, t), "dve") for g in range(3)]
        if t > 0:
            out += [(("h2T", t - 1, g), "act") for g in range(2)] + [(("route", t - 1), "dve")]
    out += [("rank", "dve"), ("table", "dve")]
    return out


UNITS = units_in_order()
UNIT_NO = {k: n for n, (k, _) in enumerate(UNITS)}


def last_use():
    out = {f"u{n}": ("u", 2 * n + 1) for n in range(2)}
    out |= {c: (c, NT - 1) for c in ("ql", "kv", "qm0", "qm1")}
    out |= {c: (c, 1) for c in ("mk0", "mk1", "mv0", "mv1")}
    out |= {"ukv": ("kq", 9), "uq": ("kq", len(KQ_UNITS) - 1)}
    for g, (d0, nd) in enumerate(DGROUPS):
        for br in "CB":
            out |= {f"gate{br}{g}": (f"gate{br}", d0 + nd - 1)}
        out |= {f"glu{g}": ("gluv", d0 + nd - 1), f"gateA{g}": ("gateA", d0 + nd - 1), f"wout{g}": ("wout", g, NT - 1)}
    for g, (d0, nd) in enumerate(OGROUPS):
        out |= {f"out{br}{g}": (f"out{br}", d0 + nd - 1) for br in "CB"}
    return out


LAST_USE = last_use()

NORMS = ([("x", t) for t in range(NT)] + [("m", t) for t in range(2)] + [("qm", t) for t in range(NT)]
         + [("mk", t) for t in range(2)] + [("ql", t) for t in range(NT)] + [("ck", t) for t in range(NT)]
         + [("kq", n) for n in range(len(KQ_UNITS))] + [("f", t) for t in range(NT)])
NORM_NO = {k: n for n, k in enumerate(NORMS)}
NORM_WIDTH = {"x": D, "m": D, "ql": QL, "ck": KVL, "qm": MD, "mk": MD, "kq": QK, "f": D}
NORM_HEADS = {"x": 1, "m": 1, "ql": 1, "ck": 1, "qm": MH, "mk": MH, "kq": 4, "f": 1}


def norm_rows(key):
    kind, n = key
    if kind == "m" or kind == "mk":
        return 128
    if kind == "kq":
        what, j, _ = KQ_UNITS[n]
        return KEYS[j][1] if what == "k" else TILES[j][1]
    return TILES[n][1]


class Steps:

    def __init__(self, eng, own):
        self.eng, self.own, self.count = eng, own, {}

    def mark(self, ins, sem=None, by=1):
        sem = self.own if sem is None else sem
        ins.then_inc(sem, by)
        self.count[sem] = self.count.get(sem, 0) + by
        return sem, self.count[sem]

    def after(self, *marks):
        for sem, n in marks:
            self.eng.wait_ge(sem, n)


def build(nc, a, o, scratch):
    ctx = ExitStack()
    with ctx:
        def sem(name):
            return ctx.enter_context(nc.semaphore(name))

        def alloc(stack, name, shape, dt=F32):
            return stack.enter_context(nc.sbuf_tensor(name, shape, dt))

        def width(shape):
            return 4 * int(np.prod(shape[1:]))

        def overlay(stack, *groups):
            out, sizes = {}, [sum(width(s) for _, s in g) for g in groups]
            for n, group in enumerate(groups):
                own = stack if n == len(groups) - 1 else ExitStack()
                for name, shape in group:
                    if name in out:
                        alloc(own, f"{name}_again", shape)
                    else:
                        out[name] = alloc(own, name, shape)
                if n == len(groups) - 1:
                    if sizes[n] < max(sizes):
                        alloc(own, f"pad_{group[0][0]}", [128, (max(sizes) - sizes[n]) // 4])
                else:
                    own.close()
            return out

        v = overlay(ctx, [("X0", [128, NT, D])], [("qT", [128, H, TOK])], [("X", [128, NT, D])])
        X0, qT, X = v["X0"], v["qT"], v["X"]
        cst = alloc(ctx, "cst", [128, NCONST])
        sums = alloc(ctx, "sums", [128, len(NORMS), 4])
        rstd = alloc(ctx, "rstd", [128, len(NORMS), 4])
        halves = alloc(ctx, "halves", [128, 4])
        means = alloc(ctx, "means", [128, len(NORMS), 4])
        grow = alloc(ctx, "grow", [128, D])
        junk = ctx.enter_context(nc.sbuf_tensor("junk", [128, D], mybir.dt.bfloat16))
        pre = ExitStack()
        hT = alloc(pre, "hT", [128, KD, TOK])
        uT = alloc(pre, "uT", [128, 4, TOK])
        oTmem = alloc(pre, "oTmem", [128, 4, TOK])
        oTmla = alloc(pre, "oTmla", [128, 4, TOK])
        v = overlay(pre, [("qlat", [128, NT, QL]), ("ckv", [128, 5, KVL + ROPE])], [("gateA", [128, KD, TOK])])
        qlat, ckv, gateA = v["qlat"], v["ckv"], v["gateA"]
        gsmall = alloc(pre, "gsmall", [128, QL + KVL + 2 * QK + 2 * MD])
        s5par = alloc(pre, "s5par", [128, 5, GP])
        s5tmp = alloc(pre, "s5tmp", [128, 19, GP])
        cosT = alloc(pre, "cosT", [128, GP, WIN])
        sinT = alloc(pre, "sinT", [128, GP, WIN])
        wB = alloc(pre, "wB", [128, 2, 4, 128])
        gelu = alloc(pre, "gelu", [128, 2, TOK])
        wC = alloc(pre, "wC", [128, 2, 4, 128])
        dskip = alloc(pre, "dskip", [128, 4])
        rotA = alloc(pre, "rotA", [128, 2, TOK])
        rotB = alloc(pre, "rotB", [128, 2, TOK])
        rotC = alloc(pre, "rotC", [128, 2, TOK])
        hS = alloc(pre, "hS", [128, 2, 2, TOK])
        carry = alloc(pre, "carry", [128, 2, 3, 4])
        finals = alloc(pre, "finals", [128, 2, 2, GP])
        soft = alloc(pre, "soft", [128, 4, 3, 4])
        v = overlay(pre, [("Hn", [128, NT, D])],
                    [("bbar", [128, 2, GP, CH]), ("btmp", [128, 4, GP, CH])],
                    [("KQ", [128, KQ_BUFS, 4, QK]), ("ropet", [128, 2, 2, 4, ROPE])],
                    [("gateB", [128, KD, TOK]), ("mtmp", [128, 2, TOK])])
        Hn, bbar, btmp, KQ, ropet, gateB, mtmp = (v[k] for k in ("Hn", "bbar", "btmp", "KQ", "ropet", "gateB", "mtmp"))
        v = overlay(pre, [("s5raw", [GP, 5, 128]), ("dtraw", [GP, 2]), ("braw", [128, 2, GP, CH]),
                          ("bpad", [128, 2, GP, 2, CH]), ("craw", [128, 2, 4, ST]), ("cpad", [128, 2, 4, 2, ST])],
                    [("P", [128, 2, 512]), ("PT", [128, 2, 512]), ("O", [128, NT, 512])])
        s5raw, dtraw, braw, bpad, craw, cpad = (v[k] for k in ("s5raw", "dtraw", "braw", "bpad", "craw", "cpad"))
        P, PT, O = v["P"], v["PT"], v["O"]
        kv = [("mk", [128, 2, 2, 512]), ("mv", [128, 2, 2, 512]), ("qmem", [128, NT, MH * MD])]
        v = overlay(pre, kv + [("mem", [128, 2, D]), ("memT", [128, KD, MEMT])],
                    kv + [("mkT", [128, 2, MH, MEMT]), ("qmT", [128, MH, TOK])],
                    [("ckT", [128, 2, 576]), ("qlT", [128, 3, TOK]), ("V", [128, 5, 512]),
                     ("kT", [128, H, 576])],
                    [("finrow", [GP, 4, 128]), ("gsig", [128, 2, TOK])])
        mem, memT, mk, mv, qmem, mkT, qmT = (v[k] for k in ("mem", "memT", "mk", "mv", "qmem", "mkT", "qmT"))
        ckT, qlT, V, kT = (v[k] for k in ("ckT", "qlT", "V", "kT"))
        finrow, gsig = v["finrow"], v["gsig"]
        mergedT = alloc(pre, "mergedT", [128, KD, TOK])
        W = [alloc(pre, f"W{i}", [128, WSLOT]) for i in range(WSLOTS)]
        pre.close()
        moe = ExitStack()
        ctx.enter_context(moe)
        h2 = alloc(moe, "h2", [128, NT, D])
        h2T = alloc(moe, "h2T", [128, KD, TOK])
        wr = alloc(moe, "wr", [128, KD, NG + NE])
        brow = alloc(moe, "brow", [128, NG + NE])
        lg = alloc(moe, "lg", [128, NT, 40])
        E13 = [alloc(moe, f"E13_{i}", [128, 2, KD, FF]) for i in range(4)]
        E2 = [alloc(moe, f"E2_{i}", [128, 2, D]) for i in range(4)]
        xg = alloc(moe, "xg", [B, 2, D])
        xT = alloc(moe, "xT", [128, 2, KD, B])
        tg = alloc(moe, "tg", [128, 2, 2, B])
        ug = alloc(moe, "ug", [128, 2, 2, B])
        hid = alloc(moe, "hid", [128, 2, 2, B])
        yb = alloc(moe, "yb", [B, 2, D])
        r8 = alloc(moe, "r8", [128, 4, NT, 8])
        i8 = alloc(moe, "i8", [128, 2, NT, 8], U32)
        rs = alloc(moe, "rs", [128, 24, NT])
        ex4 = alloc(moe, "ex4", [128, 3, NT, NG])
        prod = alloc(moe, "prod", [128, NT, EPG, NG])
        Ek = alloc(moe, "Ek", [128, 3, NT, NE])
        ncmp = alloc(moe, "ncmp", [128, NE, NJ])
        jcmp = alloc(moe, "jcmp", [128, 2, NT, NJ])
        cnt = alloc(moe, "cnt", [128, 6, NE])
        tp = alloc(moe, "tp", [128, 4, NT, NE])
        ohs = alloc(moe, "ohs", [128, 2, NT, B])
        ohb = alloc(moe, "ohb", [128, 4, NT, NBLK])
        idx = alloc(moe, "idx", [B, NBLK], U32)
        idx_ov = alloc(moe, "idx_ov", [B, 2], U32)
        pos = alloc(moe, "pos", [128, 2, NT], U32)
        ovcmp = alloc(moe, "ovcmp", [1, NOV, NE])
        ovf = alloc(moe, "ovf", [1, 2, NOV])
        ovi = alloc(moe, "ovi", [1, NOV + 1], I32)
        rows = alloc(moe, "rows", [128, 2, NT, D])
        PS = ctx.enter_context(nc.psum_tensor("PS", [128, 8, 512], F32))
        BU, YB = 5, 7

        def const(name, rows_=128):
            x, y = CONST[name]
            return cst[0:rows_, x:y]

        ident = const("ident")
        rope = const("rope").rearrange("p (n c d) -> p n c d", n=3, c=2)
        g_ql = gsmall[:, 0:QL]
        g_kv = gsmall[:, QL:QL + KVL]
        o1 = QL + KVL
        g_qn, g_kn = gsmall[:, o1:o1 + QK], gsmall[:, o1 + QK:o1 + 2 * QK]
        g_mq, g_mk = gsmall[:, o1 + 2 * QK:o1 + 2 * QK + MD], gsmall[:, o1 + 2 * QK + MD:]

        names = """x0_loaded x1_loaded x2_loaded x_again gattn_loaded params_loaded const_loaded gains_loaded mem_loaded s5_loaded cache_loaded
            gffn_loaded router_loaded psum_full emptied_act emptied_dve sums_ready rstd_ready h_ready mem_ready
            s5_raw_ready s5_scaled s5_mag_ready s5_reduced s5_sin_ready s5_den s5_rden s5_tables s5_padded
            bu_full bu_free h_state y_full y_skipped y_square y_inner y_tanh z_ready finals_copied finals_full
            finals_out ql_ready ck_ready qm_ready mk_ready scores_max kq_ready merged h2_ready
            logits_in logits_exp onehot_ready tables_in ov_ready gathered0 gathered1 xt_full xt_ready
            ab_full tanh_ready hid_ready y_mm y_act y_dve y_filled y_stored0 y_stored1 h2_stored ov_idx ov_gathered ov_xt_full ov_xt_ready
            ov_ab ov_tanh ov_hid ov_y_mm ov_y_act ov_y_dve ov_stored ov_w rows_gathered0 rows_gathered1 rows_gathered2 out_ready
            stored pe_passed pool_passed act_step dve_step pool_step dve_moe ov_half""".split()
        s = {n: sem(n) for n in names}
        chunk_loaded = [sem(f"chunk_loaded{i}") for i in range(WSLOTS)]
        expert_loaded = [sem(f"expert_loaded{i}") for i in range(4)]

        def bank(key):
            return PS[:, UNIT_NO[key] % RING, :]

        def emptied_at(n):
            who = UNITS[n][1]
            return s["emptied_" + who], sum(1 for _, w in UNITS[:n + 1] if w == who)

        def chunk(name, kt, cols):
            return W[SLOT_OF[CHUNK_NO[name]]][:, 0:kt * cols].rearrange("p (k n) -> p k n", k=kt)

        def chunk_view(name):
            _, kt, cols = CHUNKS[CHUNK_NO[name]]
            return chunk(name, kt, cols)

        def chunk_source(name):
            w_in = a["w_in"][0].rearrange("(p k) n -> p k n", k=KD)
            w_mem = a["w_mem_kv"][0].rearrange("(p k) n -> p k n", k=KD)
            dst = chunk_view(name)
            cols = CHUNKS[CHUNK_NO[name]][2]
            first = {"u0": C_U, "u1": C_U + 256, "ql": C_QL, "kv": C_KV, "qm0": C_QM, "qm1": C_QM + 256}
            if name in first:
                return [(dst, w_in[:, :, first[name]:first[name] + cols])]
            if name[:2] in ("mk", "mv"):
                c = (512 if name[1] == "v" else 0) + 256 * int(name[2])
                return [(dst, w_mem[:, :, c:c + cols])]
            if name == "ukv":
                return [(dst, a["w_ukv"][0].rearrange("(k p) n -> p k n", p=128))]
            if name == "uq":
                return [(dst, a["w_uq"][0].rearrange("(k p) n -> p k n", p=128))]
            d0, nd = groups_of(name)[int(name[-1])]
            if name.startswith("gate"):
                c = C_GATE + D * {"A": BRANCH_A, "B": BRANCH_B, "C": BRANCH_C}[name[4]] + 128 * d0
                return [(dst, w_in[:, :, c:c + cols])]
            if name.startswith("out"):
                w = a["w_o_mem"] if name[3] == "C" else a["w_o_mla"]
                return [(dst, w[0].rearrange("(k p) n -> p k n", p=128)[:, :, 128 * d0:128 * d0 + cols])]
            if name.startswith("glu"):
                w = a["w_glu"][0].rearrange("(k p) n -> p k n", p=128)
                n = 128 * nd
                return [(dst[:, :, 0:n], w[:, :, 128 * d0:128 * d0 + n]),
                        (dst[:, :, n:2 * n], w[:, :, D + 128 * d0:D + 128 * d0 + n])]
            w = a["w_out"][0].rearrange("(k p) n -> p k n", p=128)
            return [(dst, w[:, :, 128 * d0:128 * d0 + cols])]

        DMAS_OF = [len(chunk_source(c[0])) for c in CHUNKS]

        def chunk_loaded_at(name):
            n = CHUNK_NO[name]
            return chunk_loaded[SLOT_OF[n]], 16 * sum(DMAS_OF[m] for m in range(n + 1) if SLOT_OF[m] == SLOT_OF[n])

        e13_src = [a["w_e1"][0].rearrange("e (p k) n -> p e k n", k=KD), a["w_e3"][0].rearrange("e (p k) n -> p e k n", k=KD)]
        e2_src = a["w_e2"][0].rearrange("e (j p) n -> p e j n", p=128)
        LOADS = 3

        xp, xs = a["x_prompt"][0], a["x_sample"][0]
        block = ctx.enter_context(nc.Block())

        @block.sync
        def _(sp):
            st = Steps(sp, None)
            stored = []

            def store(dst, src):
                stored.append(st.mark(sp.dma_start(dst, src), s["stored"], 16))

            def load_chunk(n):
                if FORMER[n] is not None:
                    sp.wait_ge(s["psum_full"], UNIT_NO[LAST_USE[CHUNKS[FORMER[n]][0]]] + 1)
                for dst, src in chunk_source(CHUNKS[n][0]):
                    sp.dma_start(dst, src).then_inc(chunk_loaded[SLOT_OF[n]], 16)

            for t, (f, n) in enumerate(TILES):
                src = xp[f:f + n, :] if t < 2 else xs
                sp.dma_start(X0[0:n, t, :], src).then_inc(s[f"x{t}_loaded"], 16)
                if t == 0:
                    sp.dma_start(grow[:], a["g_attn"][0].partition_broadcast(128)).then_inc(s["gattn_loaded"], 16)
                    sp.dma_start(cst[:], a["consts"]).then_inc(s["const_loaded"], 16)
            load_chunk(0)
            for n, name in enumerate(("ssm_a_re", "ssm_a_im")):
                sp.dma_start(s5raw[:, n, :], a[name][0].rearrange("(q g) p -> q (g p)", g=2)).then_inc(s["s5_loaded"], 16)
            for n, name in enumerate(("cache_ssm_re", "cache_ssm_im")):
                sp.dma_start(s5raw[:, 2 + n, :], a[name][0][0].rearrange("(q g) p -> q (g p)", g=2)).then_inc(s["s5_loaded"], 16)
            sp.dma_start(dtraw[:], a["ssm_log_dt"][0].rearrange("(q g) -> q g", g=2)).then_inc(s["s5_loaded"], 16)
            load_chunk(1)
            load_chunk(2)
            for n in range(2):
                sp.dma_start(mem[:, n, :], a["mem_prompt"][0][128 * n:128 * n + 128, :]).then_inc(s["mem_loaded"], 16)
            sp.dma_start(memT[:, 0:4, :].rearrange("p k n -> p (k n)"),
                         a["g_mem"][0].partition_broadcast(128)).then_inc(s["mem_loaded"], 16)
            for n, name in enumerate(("ssm_b_re", "ssm_b_im")):
                for g2 in range(2):
                    sp.dma_start(braw[64 * g2:64 * g2 + 64, n], a[name][0].rearrange("(q g) p c -> g p q c", g=2)[g2])\
                        .then_inc(s["params_loaded"], 16)
            for n, name in enumerate(("ssm_c_re", "ssm_c_im")):
                sp.dma_start(craw[:, n], a[name][0].rearrange("(t g) c p -> (g c) t p", g=8)).then_inc(s["params_loaded"], 16)
            sp.dma_start(dskip[:], a["ssm_d"][0].rearrange("(t p) -> p t", p=128),
                         allow_slow_non_contiguous=True).then_inc(s["params_loaded"], 16)
            for dst, name in ((g_ql, "g_qlat"), (g_kv, "g_kvlat"), (g_qn, "g_qn"), (g_kn, "g_kn"), (g_mq, "g_mqn"), (g_mk, "g_mkn")):
                sp.dma_start(dst, a[name][0].partition_broadcast(128)).then_inc(s["gains_loaded"], 16)
            load_chunk(3)
            load_chunk(4)
            for n in range(2):
                r = slice(128 * n, 128 * n + 128)
                sp.dma_start(ckv[:, 2 + n, 0:KVL], a["cache_mla_ckv"][0][0][r, :]).then_inc(s["cache_loaded"], 16)
                sp.dma_start(ckv[:, 2 + n, KVL:], a["cache_mla_kpe"][0][0][r, :]).then_inc(s["cache_loaded"], 16)
                sp.dma_start(mk[:, 1, n, :], a["cache_mem_k"][0][0][r].rearrange("t h d -> t (h d)")).then_inc(s["cache_loaded"], 16)
                sp.dma_start(mv[:, 1, n, :], a["cache_mem_v"][0][0][r].rearrange("t h d -> t (h d)")).then_inc(s["cache_loaded"], 16)
            sp.wait_ge(s["x0_loaded"], 16)
            for f, n in FILLS:
                sp.dma_start(scratch["y"][f:f + n, :], X0[0:n, 0, :]).then_inc(s["y_filled"], 16)
            for n in range(5, CHUNK_NO["kv"] + 1):
                load_chunk(n)
            for t in range(2):
                sp.wait_ge(s["mk_ready"], t + 1)
                sp.wait_ge(*emptied_at(UNIT_NO["mv1", t]))
                store(o["mem_k"][128 * t:128 * t + 128, :], mk[:, 0, t, :])
                store(o["mem_v"][128 * t:128 * t + 128, :], mv[:, 0, t, :])
            for n in range(CHUNK_NO["gateC0"], CHUNK_NO["uq"] + 1):
                load_chunk(n)
            for t, (f, n) in enumerate(TILES):
                sp.wait_ge(s["ck_ready"], t + 1)
                j = KEY_OF_TILE[t]
                store(o["ckv_p"][f:f + n, :] if t < 2 else o["ckv_s"], ckv[0:n, j, 0:KVL])
                store(o["kpe_p"][f:f + n, :] if t < 2 else o["kpe_s"], ckv[0:n, j, KVL:])
            for n in range(CHUNK_NO["outC0"], CHUNK_NO["glu0"]):
                load_chunk(n)
            sp.wait_ge(s["psum_full"], UNIT_NO["mla", "S", len(MLA_UNITS) - 1] + 1)
            for t, (f, n) in enumerate(TILES):
                sp.dma_start(X[0:n, t, :], xp[f:f + n, :] if t < 2 else xs).then_inc(s["x_again"], 16)
            sp.wait_ge(s["h_ready"], NT)
            sp.dma_start(grow[:], a["g_ffn"][0].partition_broadcast(128)).then_inc(s["gffn_loaded"], 16)
            sp.wait_ge(s["finals_out"], 1)
            for n, name in enumerate(("sre_p", "sim_p", "sre_s", "sim_s")):
                store(o[name], finrow[:, n, :])
            for n in range(CHUNK_NO["glu0"], len(CHUNKS)):
                load_chunk(n)

            sp.wait_ge(s["y_filled"], 16 * len(FILLS))
            sp.wait_ge(s["merged"], KD)
            st.after(stored[-1])
            sp.dma_start(wr[:, :, 0:NG], a["w_rg"][0].rearrange("(p k) n -> p k n", k=KD)).then_inc(s["router_loaded"], 16)
            sp.dma_start(wr[:, :, NG:], a["w_re"][0].rearrange("(p k) n -> p k n", k=KD)).then_inc(s["router_loaded"], 16)
            sp.dma_start(brow[:, 0:NG], a["b_rg"][0].partition_broadcast(128)).then_inc(s["router_loaded"], 16)
            sp.dma_start(brow[:, NG:], a["b_re"][0].rearrange("g e -> (g e)").partition_broadcast(128)).then_inc(s["router_loaded"], 16)

            def load_expert(u, e):
                for n in range(2):
                    sp.dma_start(E13[u][:, n, :, :], e13_src[n][:, e, :, :]).then_inc(expert_loaded[u], 16)
                sp.dma_start(E2[u][:], e2_src[:, e, :, :]).then_inc(expert_loaded[u], 16)

            for u in range(4):
                load_expert(u, u)
            for t, (f, n) in enumerate(TILES):
                sp.wait_ge(s["h2_ready"], t + 1)
                sp.dma_start(scratch["h2"][f:f + n, :], h2[0:n, t, :]).then_inc(s["h2_stored"], 16)

            def store_rows(u, e):
                sp.wait_ge(s["y_act"], e + 1)
                sp.wait_ge(s["y_dve"], e + 1)
                sp.dma_start(scratch["y"][bass.ts(e, B), :], yb[:, u % 2, :]).then_inc(s[f"y_stored{u % 2}"], 16)

            with sp.Fori(0, NE // 4 - 1) as i:
                for u in range(4):
                    e = i * 4 + u
                    sp.wait_ge(s["y_mm"], e + 1)
                    for n in range(2):
                        sp.dma_start(E13[u][:, n, :, :], e13_src[n][:, bass.ds(e + 4, 1), :, :].rearrange("p e k n -> p (e k) n"))\
                            .then_inc(expert_loaded[u], 16)
                    sp.dma_start(E2[u][:], e2_src[:, bass.ds(e + 4, 1), :, :].rearrange("p e k n -> p (e k) n"))\
                        .then_inc(expert_loaded[u], 16)
                    store_rows(u, e)
            for u in range(4):
                store_rows(u, NE - 4 + u)

            sp.wait_ge(s["ov_ready"], 2)
            blocks = sp.value_load(ovi[0:1, NOV:NOV + 1], min_val=0, max_val=NOV)
            with sp.Fori(0, NOV) as i:
                with sp.If(i < blocks):
                    e = sp.value_load(ovi[0:1, bass.ds(i, 1)], min_val=0, max_val=NE - 1)
                    sp.wait_ge(s["ov_y_mm"], i)
                    for n in range(2):
                        sp.dma_start(E13[0][:, n, :, :], e13_src[n][:, bass.ds(e, 1), :, :].rearrange("p e k n -> p (e k) n"))\
                            .then_inc(s["ov_w"], 16)
                    sp.dma_start(E2[0][:], e2_src[:, bass.ds(e, 1), :, :].rearrange("p e k n -> p (e k) n")).then_inc(s["ov_w"], 16)
                    sp.wait_ge(s["ov_y_act"], i + 1)
                    sp.wait_ge(s["ov_y_dve"], i + 1)
                    sp.dma_start(scratch["y"][bass.ds(i * B + NE * B, B), :], yb[:, 0, :]).then_inc(s["ov_stored"], 16)
            for t, (f, n) in enumerate(TILES):
                sp.wait_ge(s["out_ready"], t + 1)
                store(o["y_p"][f:f + n, :] if t < 2 else o["y_s"], X[0:n, t, :])
            st.after(stored[-1])

        @block.tensor
        def _(pe):
            mm = nc.tensor.matmul

            def begin(key):
                n = UNIT_NO[key]
                if n >= RING:
                    pe.wait_ge(*emptied_at(n - RING))
                return bank(key)

            def end(ins):
                ins.then_inc(s["psum_full"], 1)

            def use(name):
                sem_, value = chunk_loaded_at(name)
                pe.wait_ge(sem_, value)
                return chunk_view(name)

            def emptied(key):
                pe.wait_ge(*emptied_at(UNIT_NO[key]))

            pe.wait_ge(s["const_loaded"], 16)
            for t, (f, n) in enumerate(TILES):
                pe.wait_ge(s["h_ready"], t + 1)
                for g in range(2):
                    out = begin(("xT", t, g))
                    for k in range(4):
                        ins = nc.tensor.transpose(out[:, k * n:k * n + n], Hn[0:n, t, 4 * g + k::KD], ident[0:n, 0:n])
                    end(ins)

            def feature_major(key, w, cols, rhs, kt):
                out = begin(key)
                for k in range(kt):
                    ins = mm(out[:, 0:TOK], w[:, k, cols:cols + 128], rhs[:, k, :], start=(k == 0), stop=(k == kt - 1))
                end(ins)

            def token_major(key, w, c0, cols, lhs, f, n, kt):
                out = begin(key)
                for k in range(kt):
                    ins = mm(out[0:n, 0:cols], lhs[:, k, f:f + n], w[:, k, c0:c0 + cols], start=(k == 0), stop=(k == kt - 1))
                end(ins)

            emptied(("xT", NT - 1, 1))
            for m in range(4):
                w = use(f"u{m // 2}")
                feature_major(("u", m), w, 128 * (m % 2), hT, KD)
            pe.wait_ge(s["s5_raw_ready"], 1)
            out = begin("par")
            for n in range(5):
                ins = nc.tensor.transpose(out[:, GP * n:GP * n + GP], s5raw[:, n, :], ident[0:GP, 0:GP])
            end(ins)
            for t in range(2):
                pe.wait_ge(s["mem_ready"], t + 1)
                for g in range(2):
                    out = begin(("memT", t, g))
                    for k in range(4):
                        ins = nc.tensor.transpose(out[:, 128 * k:128 * k + 128], mem[:, t, 4 * g + k::KD], ident)
                    end(ins)
            emptied(("memT", 1, 1))

            def projection(name, t):
                f, n = TILES[t] if name[0] != "m" else (128 * t, 128)
                token_major((name, t), use(name), 0, CHUNKS[CHUNK_NO[name]][2], memT if name[0] == "m" else hT, f, n, KD)

            def s5_operand(n):
                pe.wait_ge(s["s5_padded"], n + 1)
                out = begin(("s5T", n))
                for t in range(4):
                    src = (bpad[:, n, 4 * t:4 * t + 4].rearrange("p q g c -> p (q g c)") if n < 2
                           else cpad[:, n - 2, t].rearrange("p g s -> p (g s)"))
                    ins = nc.tensor.transpose(out[:, 128 * t:128 * t + 128], src, ident)
                end(ins)

            def s5_y(q):
                t, r = q // 4, 32 * (q % 4)
                pe.wait_ge(s["h_state"], q + 1)
                if q % 4 == 0 and t > 0:
                    pe.wait_ge(s["y_skipped"], t)
                for c in range(2):
                    ins = mm(PS[r:r + 32, YB, 0:TOK], wC[:, c, t, r:r + 32], hS[:, q % 2, c, :], start=(c == 0), stop=(c == 1))
                ins.then_inc(s["y_full"], 1)

            def s5_turn(q):
                t, r = q // 4, 32 * (q % 4)
                if q == 0:
                    emptied(("s5T", 3))
                else:
                    pe.wait_ge(s["bu_free"], q)
                for c in range(2):
                    ins = mm(PS[:, BU + c, 0:TOK], wB[r:r + 32, c, t, :], uT[r:r + 32, t, :], start=True, stop=True)
                ins.then_inc(s["bu_full"], 1)
                if q > 1:
                    s5_y(q - 2)

            def memory_keys(src, kt):
                if src == 0:
                    pe.wait_ge(s["mk_ready"], kt + 1)
                else:
                    pe.wait_ge(s["cache_loaded"], 16 * 8)
                out = begin(("mkT", src, kt))
                for h in range(MH):
                    ins = nc.tensor.transpose(out[:, 128 * h:128 * h + 128], mk[:, src, kt, MD * h:MD * h + MD], ident)
                end(ins)

            def memory_queries(t):
                f, n = TILES[t]
                pe.wait_ge(s["qm_ready"], t + 1)
                out = begin(("qmT", t))
                for h in range(MH):
                    ins = nc.tensor.transpose(out[:, n * h:n * h + n], qmem[0:n, t, MD * h:MD * h + MD], ident[0:n, 0:n])
                end(ins)

            def attention(kind, units, step, m):
                    mem_ = kind == "mem"
                    if (step, m) == ("S", 0):
                        emptied(("mkT", 0, 1) if mem_ else ("kqT", len(KQ_UNITS) - 1))
                    out = begin((kind, step, m))
                    if step == "OT":
                        n = TILES[m][1]
                        emptied((kind, "O", max(k for k, x in enumerate(units) if x[1] == m)))
                        for j in range(4):
                            ins = nc.tensor.transpose(out[:, n * j:n * j + n], O[0:n, m, 128 * j:128 * j + 128], ident[0:n, 0:n])
                        end(ins)
                        return
                    _, t, h0, nh = units[m]
                    f, n = TILES[t]
                    kb = key_blocks(units[m])
                    nk = sum(kb)
                    if step == "S":
                        for h in range(nh):
                            if mem_:
                                lhs, rhs = qmT[:, h0 + h, f:f + n], mkT[:, t // 2, h0 + h, :]
                            else:
                                k0 = 0 if t < 2 else 256
                                lhs, rhs = qT[0:QK, h0 + h, f:f + n], kT[0:QK, h0 + h, k0:k0 + nk]
                            ins = mm(out[0:n, nk * h:nk * h + nk], lhs, rhs, start=True, stop=True)
                        end(ins)
                    elif step == "PT":
                        emptied((kind, "S", m))
                        at = 0
                        for h in range(nh):
                            for b, rows_ in enumerate(kb):
                                src = P[0:n, m % 2, nk * h + 128 * b:nk * h + 128 * b + rows_]
                                ins = nc.tensor.transpose(out[0:rows_, n * at:n * at + n], src, ident[0:n, 0:n])
                                at += 1
                        end(ins)
                    else:
                        emptied((kind, "PT", m))
                        dv = MD if mem_ else VH
                        for h in range(nh):
                            for b, rows_ in enumerate(kb):
                                at = h * len(kb) + b
                                if mem_:
                                    rhs = mv[0:rows_, t // 2, b, MD * (h0 + h):MD * (h0 + h) + MD]
                                else:
                                    rhs = V[0:rows_, (0 if t < 2 else 2) + b, VH * (h0 + h):VH * (h0 + h) + VH]
                                ins = mm(out[0:n, dv * h:dv * h + dv], PT[0:rows_, m % 2, n * at:n * at + n], rhs,
                                         start=(b == 0), stop=(b == len(kb) - 1))
                        end(ins)

            def query_latents(t):
                f, n = TILES[t]
                pe.wait_ge(s["ql_ready"], t + 1)
                out = begin(("qlT", t))
                for k in range(3):
                    ins = nc.tensor.transpose(out[:, n * k:n * k + n], qlat[0:n, t, 128 * k:128 * k + 128], ident[0:n, 0:n])
                end(ins)

            def key_latents(j):
                f, n = KEYS[j]
                if j in (2, 3):
                    pe.wait_ge(s["cache_loaded"], 16 * 8)
                else:
                    pe.wait_ge(s["ck_ready"], KEY_OF_TILE.index(j) + 1)
                out = begin(("ckT", j))
                for k in range(2):
                    ins = nc.tensor.transpose(out[:, n * k:n * k + n], ckv[0:n, j, 128 * k:128 * k + 128], ident[0:n, 0:n])
                end(ins)

            def latents_up(m):
                what, j, half = KQ_UNITS[m]
                if m == 0:
                    emptied(("ckT", 4))
                if what == "k":
                    f, n = KEYS[j]
                    token_major(("kq", m), use("ukv"), 512 * half, 512, ckT, f, n, 2)
                else:
                    f, n = TILES[j]
                    token_major(("kq", m), use("uq"), 384 * half, 384, qlT, f, n, 3)

            def heads_transposed(m):
                what, j, half = KQ_UNITS[m]
                n = KEYS[j][1] if what == "k" else TILES[j][1]
                pe.wait_ge(s["kq_ready"], m + 1)
                out = begin(("kqT", m))
                for h in range(4):
                    ins = nc.tensor.transpose(out[0:QK, n * h:n * h + n], KQ[0:n, m % KQ_BUFS, h, :], ident[0:n, 0:n])
                end(ins)

            def branch(kind, d):
                groups = groups_of(kind)
                g = max(g for g, (d0, _) in enumerate(groups) if d0 <= d)
                col = 128 * (d - groups[g][0])
                if kind.startswith("gate"):
                    feature_major((kind, d), use(f"{kind}{g}"), col, hT, KD)
                else:
                    if d == 0:
                        emptied(("mem" if kind == "outC" else "mla", "OT", NT - 1))
                    feature_major((kind, d), use(f"{kind}{g}"), col, oTmem if kind == "outC" else oTmla, 4)

            def last_states():
                pe.wait_ge(s["finals_copied"], GP)
                pe.wait_ge(s["bu_free"], GP)
                for n in range(4):
                    ins = nc.tensor.transpose(PS[0:GP, BU, 128 * n:128 * n + 128], finals[:, n // 2, n % 2, :], ident)
                ins.then_inc(s["finals_full"], 1)

            run = {"turn_in": s5_turn, "mkT": memory_keys, "qmT": memory_queries, "qlT": query_latents, "ckT": key_latents,
                   "kq": latents_up, "kqT": heads_transposed, "s5T": s5_operand, "finals": last_states}
            for kind, *which in MIDDLE:
                if kind in ("mem", "mla"):
                    attention(kind, MEM_UNITS if kind == "mem" else MLA_UNITS, *which)
                elif kind in run:
                    run[kind](*which)
                elif kind.startswith(("gate", "out")):
                    branch(kind, *which)
                elif kind in CHUNK_NO:
                    projection(kind, *which)
                elif kind == "last_y":
                    s5_y(GP - 2)
                    s5_y(GP - 1)
            pe.wait_ge(s["z_ready"], 4)
            for g, (d0, nd) in enumerate(DGROUPS):
                for d in range(d0, d0 + nd):
                    w = use(f"glu{g}")
                    feature_major(("glug", d), w, 128 * (nd + d - d0), uT, 4)
                    feature_major(("gluv", d), w, 128 * (d - d0), uT, 4)
            pe.wait_ge(s["merged"], KD)

            def route(t):
                f, n = TILES[t]
                pe.wait_ge(s["h2_ready"], t + 1)
                for g in range(2):
                    out = begin(("h2T", t, g))
                    for k in range(4):
                        ins = nc.tensor.transpose(out[:, k * n:k * n + n], h2[0:n, t, 4 * g + k::KD], ident[0:n, 0:n])
                    end(ins)
                emptied(("h2T", t, 1))
                if t == 0:
                    pe.wait_ge(s["router_loaded"], 64)
                token_major(("route", t), wr, 0, NG + NE, h2T, f, n, KD)

            for t, (f, n) in enumerate(TILES):
                for g, (d0, nd) in enumerate(DGROUPS):
                    token_major(("wout", g, t), use(f"wout{g}"), 0, 128 * nd, mergedT, f, n, KD)
                if t > 0:
                    route(t - 1)
            route(NT - 1)
            pe.wait_ge(s["onehot_ready"], 1)
            out = begin("rank")
            both = Ek[:, 2]
            mm(out[:, 0:NE * NT], const("upper"), both.rearrange("p t e -> p (t e)"), start=True, stop=False)
            mm(out[:, NE * NT:NE * NT + NE], const("ones"), both[:, NT - 1, :], start=False, stop=False)
            for t in range(NT - 1):
                ins = mm(out[:, NE * (t + 1):NE * (NT + 1)], const("ones"), both[:, t:t + 1, :].broadcast_to([128, NT - t, NE]),
                         start=False, stop=(t == NT - 2))
            end(ins)
            pe.wait_ge(s["tables_in"], 1)
            out = begin("table")
            for k in range(2):
                for t in range(NT):
                    ins = mm(out[0:B, 0:NBLK], ohs[:, k, t, :], ohb[:, k, t, :], start=(k + t == 0), stop=(k * NT + t == 2 * NT - 1))
            end(ins)
            pe.wait_ge(s["emptied_dve"], sum(1 for _, w in UNITS if w == "dve"))
            pe.wait_ge(s["emptied_act"], sum(1 for _, w in UNITS if w == "act"))

            def x_transposes(par, e, first):
                pe.wait_ge(s[f"gathered{par}"], 8 * (e - par) + 16)
                if not first:
                    pe.wait_ge(s["xt_ready"], e - 1)
                pe.sem_inc(s["pe_passed"], 1)
                for k in range(KD):
                    ins = nc.tensor.transpose(PS[:, par, B * k:B * k + B], xg[:, par, k::KD], ident[0:B, 0:B])
                ins.then_inc(s["xt_full"], 1)

            def up(slot, par, e, first, turn):
                pe.wait_ge(expert_loaded[slot], 16 * LOADS * (turn + 1))
                pe.wait_ge(s["xt_ready"], e + 1)
                if not first:
                    pe.wait_ge(s["hid_ready"], e - 1)
                up_products(slot, par).then_inc(s["ab_full"], 1)

            def up_products(slot, par):
                for w in range(2):
                    for j in range(2):
                        for k in range(KD):
                            ins = mm(PS[:, 2 + par, B * (2 * w + j):B * (2 * w + j) + B], E13[slot][:, w, k, 128 * j:128 * j + 128],
                                     xT[:, par, k, :], start=(k == 0), stop=(k == KD - 1))
                return ins

            def down(slot, par, e, first):
                pe.wait_ge(s["hid_ready"], e + 1)
                if not first:
                    pe.wait_ge(s["y_act"], e - 1)
                    pe.wait_ge(s["y_dve"], e - 1)
                down_products(slot, par).then_inc(s["y_mm"], 1)

            def down_products(slot, par):
                for c in range(2):
                    for j in range(2):
                        ins = mm(PS[0:B, 4 + 2 * par + c, :], hid[:, par, j, :], E2[slot][:, j, 512 * c:512 * c + 512],
                                 start=(j == 0), stop=(j == 1))
                return ins

            x_transposes(0, 0, True)
            for e in range(4):
                up(e, e % 2, e, e < 2, 0)
                x_transposes((e + 1) % 2, e + 1, e + 1 < 2)
                if e > 0:
                    down(e - 1, (e - 1) % 2, e - 1, e - 1 < 2)
            with pe.Fori(1, NE // 4) as i:
                for u in range(4):
                    e = i * 4 + u
                    up(u, u % 2, e, False, i)
                    x_transposes((u + 1) % 2, e + 1, False)
                    down((u - 1) % 4, (u - 1) % 2, e - 1, False)
            down(3, 1, NE - 1, False)

            pe.wait_ge(s["xt_ready"], NE + 1)
            pe.wait_ge(s["y_act"], NE)
            pe.wait_ge(s["y_dve"], NE)
            pe.wait_ge(s["ov_ready"], 2)
            blocks = pe.value_load(ovi[0:1, NOV:NOV + 1], min_val=0, max_val=NOV)
            with pe.Fori(0, NOV) as i:
                with pe.If(i < blocks):
                    pe.wait_ge(s["ov_gathered"], 16 * i + 16)
                    pe.sem_inc(s["pe_passed"], 1)
                    for k in range(KD):
                        ins = nc.tensor.transpose(PS[:, 0, B * k:B * k + B], xg[:, 1, k::KD], ident[0:B, 0:B])
                    ins.then_inc(s["ov_xt_full"], 1)
                    pe.wait_ge(s["ov_xt_ready"], i + 1)
                    pe.wait_ge(s["ov_w"], 16 * LOADS * i + 16 * LOADS)
                    up_products(0, 0).then_inc(s["ov_ab"], 1)
                    pe.wait_ge(s["ov_hid"], i + 1)
                    down_products(0, 0).then_inc(s["ov_y_mm"], 1)

        @block.scalar
        def _(act):
            st = Steps(act, s["act_step"])
            fn = nc.scalar.activation
            junk_at = [None] * 4

            def full(key):
                act.wait_ge(s["psum_full"], UNIT_NO[key] + 1)
                return bank(key)

            def empty(dst, src, func=ACT.Copy, **kw):
                return st.mark(fn(dst, src, func, **kw), s["emptied_act"])

            def sumsq(key, srcs, *after):
                n = norm_rows(key)
                st.after(*after)
                for h, src in enumerate(srcs):
                    w = src.free_size()
                    parts = [h % 4] if w <= 256 else [0, 1, 2, 3]
                    for m in {junk_at[q] for q in parts if junk_at[q]}:
                        st.after(m)
                    q = parts[0]
                    ins = fn(junk[0:n, 256 * q:256 * q + w], src, ACT.Square, accum_out=sums[0:n, NORM_NO[key], h:h + 1])
                    m = st.mark(ins, s["sums_ready"] if h == len(srcs) - 1 else None)
                    for q in parts:
                        junk_at[q] = m

            for t, (f, n) in enumerate(TILES):
                act.wait_ge(s[f"x{t}_loaded"], 16)
                sumsq(("x", t), [X0[0:n, t, :]])
            for t, (f, n) in enumerate(TILES):
                for g in range(2):
                    empty(hT[:, 4 * g:4 * g + 4, f:f + n], full(("xT", t, g))[:, 0:4 * n].rearrange("p (k n) -> p k n", k=4))
            act.wait_ge(s["mem_loaded"], 16 * 3)
            for t in range(2):
                sumsq(("m", t), [mem[:, t, :]])
            act.wait_ge(s["s5_loaded"], 16 * 5)
            fn(s5raw[:, 4, :].rearrange("q (g p) -> q g p", g=2), dtraw[:, :, None].broadcast_to([GP, 2, ST]),
               ACT.Exp).then_inc(s["s5_raw_ready"], 1)
            for m in range(4):
                empty(uT[:, m, :], full(("u", m))[:, 0:TOK])
            empty(s5par[:].rearrange("p n q -> p (n q)"), full("par")[:, 0:5 * GP])
            act.wait_ge(s["mem_ready"], 2)
            for t in range(2):
                for g in range(2):
                    empty(memT[:, 4 * g:4 * g + 4, 128 * t:128 * t + 128],
                          full(("memT", t, g)).rearrange("p (k n) -> p k n", k=4))

            def projection(name, t):
                what, c = name[0:2], int(name[2:] or 0)
                src = full((name, t))
                if what in ("mk", "mv"):
                    m = empty((mk if what == "mk" else mv)[:, 0, t, 256 * c:256 * c + 256], src[:, 0:256])
                    if name == "mk1":
                        sumsq(("mk", t), [mk[:, 0, t, MD * h:MD * h + MD] for h in range(MH)], m)
                    return
                n = TILES[t][1]
                if what == "ql":
                    sumsq(("ql", t), [qlat[0:n, t, :]], empty(qlat[0:n, t, :], src[0:n, 0:QL]))
                elif what == "kv":
                    dst = ckv[0:n, KEY_OF_TILE[t], :]
                    sumsq(("ck", t), [dst[:, 0:KVL]], empty(dst, src[0:n, 0:KVL + ROPE]))
                else:
                    m = empty(qmem[0:n, t, 256 * c:256 * c + 256], src[0:n, 0:256])
                    if c == 1:
                        sumsq(("qm", t), [qmem[0:n, t, MD * h:MD * h + MD] for h in range(MH)], m)

            def s5_functions():
                act.wait_ge(s["s5_scaled"], 1)
                fn(s5tmp[:, 2, :], s5tmp[:, 0, :], ACT.Exp).then_inc(s["s5_mag_ready"], 1)
                act.wait_ge(s["s5_reduced"], 1)
                fn(s5tmp[:, 5, :], s5tmp[:, 4, :], ACT.Sin).then_inc(s["s5_sin_ready"], 1)
                fn(s5tmp[:, 6, :], s5tmp[:, 4, :], ACT.Sin, scale=0.5).then_inc(s["s5_sin_ready"], 1)

            def s5_operand(n):
                empty((wB[:, n] if n < 2 else wC[:, n - 2]).rearrange("p t s -> p (t s)"), full(("s5T", n)))

            def memory_keys(src, kt):
                empty(mkT[:, src, :, 128 * kt:128 * kt + 128], full(("mkT", src, kt)).rearrange("p (h n) -> p h n", h=MH))

            def memory_queries(t):
                f, n = TILES[t]
                empty(qmT[:, :, f:f + n], full(("qmT", t))[:, 0:MH * n].rearrange("p (h n) -> p h n", h=MH))

            def attention(kind, units, step, m):
                unit0, oT = (0, oTmem) if kind == "mem" else (len(MEM_UNITS), oTmla)
                if step == "OT":
                    f, n = TILES[m]
                    empty(oT[:, :, f:f + n], full((kind, "OT", m))[:, 0:4 * n].rearrange("p (j n) -> p j n", j=4))
                    return
                _, t, h0, nh = units[m]
                n = TILES[t][1]
                kb = key_blocks(units[m])
                nk = sum(kb)
                if step == "S":
                    src = full((kind, "S", m))
                    act.wait_ge(s["scores_max"], unit0 + m + 1)
                    w = (unit0 + m) % 4
                    scale = 1.0 if kind == "mla" and t < 2 else SCALE_MEM if kind == "mem" else SCALE_MLA
                    for h in range(nh):
                        ins = fn(P[0:n, m % 2, nk * h:nk * h + nk], src[0:n, nk * h:nk * h + nk], ACT.Exp,
                                 bias=soft[0:n, w, 0, h:h + 1], scale=scale, accum_out=soft[0:n, w, 1, h:h + 1])
                        st.mark(ins, s["emptied_act"] if h == nh - 1 else None)
                elif step == "PT":
                    src = full((kind, "PT", m))
                    if kb[-1] == 128:
                        empty(PT[:, m % 2, 0:n * nh * len(kb)], src[:, 0:n * nh * len(kb)])
                    else:
                        whole = n * (len(kb) - 1)
                        st.mark(fn(PT[:, m % 2, 0:whole], src[:, 0:whole], ACT.Copy))
                        empty(PT[0:kb[-1], m % 2, whole:whole + n], src[0:kb[-1], whole:whole + n])

            def query_latents(t):
                f, n = TILES[t]
                if t == 0:
                    act.wait_ge(s["stored"], 16 * 10)
                empty(qlT[:, :, f:f + n], full(("qlT", t))[:, 0:3 * n].rearrange("p (k n) -> p k n", k=3))

            def key_latents(j):
                f, n = KEYS[j]
                empty(ckT[:, :, f:f + n], full(("ckT", j))[:, 0:2 * n].rearrange("p (k n) -> p k n", k=2))

            def latents_up(m):
                what, j, half = KQ_UNITS[m]
                src = full(("kq", m))
                dst = KQ[:, m % KQ_BUFS]
                if what == "k":
                    n = KEYS[j][1]
                    view = src[0:n, :].rearrange("p (h d) -> p h d", h=4)
                    m1 = st.mark(fn(dst[0:n, :, 0:NOPE], view[:, :, 0:NOPE], ACT.Copy))
                    m2 = st.mark(fn(dst[0:n, :, NOPE:], ckv[0:n, j, None, KVL:].broadcast_to([n, 4, ROPE]), ACT.Copy))
                    empty(V[0:n, j, 256 * half:256 * half + 256].rearrange("p (h d) -> p h d", h=4), view[:, :, NOPE:])
                    sumsq(("kq", m), [dst[0:n, h, :] for h in range(4)], m1, m2)
                else:
                    n = TILES[j][1]
                    m1 = empty(dst[0:n].rearrange("p h d -> p (h d)"), src[0:n, 0:4 * QK])
                    sumsq(("kq", m), [dst[0:n, h, :] for h in range(4)], m1)

            def heads_transposed(m):
                what, j, half = KQ_UNITS[m]
                f, n = KEYS[j] if what == "k" else TILES[j]
                dst = kT if what == "k" else qT
                if (what, j, half) == ("q", 0, 0):
                    act.wait_ge(s["y_filled"], 16 * len(FILLS))
                empty(dst[0:QK, 4 * half:4 * half + 4, f:f + n],
                      full(("kqT", m))[0:QK, 0:4 * n].rearrange("p (h n) -> p h n", h=4))

            def last_states():
                act.wait_ge(s["finals_full"], 1)
                st.mark(fn(finrow[:].rearrange("q n p -> q (n p)"), PS[0:GP, BU, :], ACT.Copy), s["finals_out"])

            def y_squared(t):
                act.wait_ge(s["y_skipped"], t + 1)
                if t >= 2:
                    act.wait_ge(s["z_ready"], t - 1)
                fn(gelu[:, t % 2, :], uT[:, t, :], ACT.Square).then_inc(s["y_square"], 1)

            def y_tanh(t):
                act.wait_ge(s["y_inner"], t + 1)
                fn(gelu[:, t % 2, :], gelu[:, t % 2, :], ACT.Tanh, scale=math.sqrt(2 / math.pi)).then_inc(s["y_tanh"], 1)

            run = {"mkT": memory_keys, "qmT": memory_queries, "qlT": query_latents, "ckT": key_latents, "kq": latents_up,
                   "kqT": heads_transposed, "s5_sin": s5_functions, "s5T": s5_operand, "finals": last_states, "z0": y_squared, "z2": y_tanh}
            for kind, *which in MIDDLE:
                if kind in ("mem", "mla"):
                    attention(kind, MEM_UNITS if kind == "mem" else MLA_UNITS, *which)
                elif kind in run:
                    run[kind](*which)
                elif kind.startswith("gate"):
                    if (kind, which[0]) == ("gateA", 0):
                        act.wait_ge(s["stored"], 16 * 10)
                    dst = {"A": gateA, "B": gateB, "C": mergedT}[kind[-1]]
                    empty(dst[:, which[0], :], full((kind, which[0]))[:, 0:TOK], ACT.Tanh, scale=0.5)
                elif kind in CHUNK_NO:
                    projection(kind, *which)
            for d in range(KD):
                src = full(("glug", d))
                if d >= 2:
                    act.wait_ge(*emptied_at(UNIT_NO["gluv", d - 2]))
                empty(gsig[:, d % 2, :], src[:, 0:TOK], ACT.Tanh, scale=0.5)
            for t, (f, n) in enumerate(TILES):
                act.wait_ge(*emptied_at(UNIT_NO["wout", 2, t]))
                sumsq(("f", t), [X[0:n, t, :]])
                for g in range(2):
                    empty(h2T[:, 4 * g:4 * g + 4, f:f + n], full(("h2T", t, g))[:, 0:4 * n].rearrange("p (k n) -> p k n", k=4))
            act.wait_ge(s["logits_in"], 1)
            fn(ex4[:, 1], ex4[:, 0], ACT.Exp).then_inc(s["logits_exp"], 1)
            act.wait_ge(s["logits_in"], 2)
            fn(rs[:, 5, :], rs[:, 4, :], ACT.Exp).then_inc(s["logits_exp"], 1)
            def x_copy(par, e, first):
                act.wait_ge(s["xt_full"], e + 1)
                if not first:
                    act.wait_ge(s["ab_full"], e - 1)
                fn(xT[:, par].rearrange("p k n -> p (k n)"), PS[:, par, 0:KD * B], ACT.Copy).then_inc(s["xt_ready"], 1)

            def gate(par, e, first):
                act.wait_ge(s["ab_full"], e + 1)
                if not first:
                    act.wait_ge(s["hid_ready"], e - 1)
                fn(tg[:, par].rearrange("p j n -> p (j n)"), PS[:, 2 + par, 0:2 * B], ACT.Tanh, scale=0.5)\
                    .then_inc(s["tanh_ready"], 1)

            def y_copy(par, e, first):
                act.wait_ge(s["y_mm"], e + 1)
                if not first:
                    act.wait_ge(s[f"y_stored{par}"], 8 * (e - par))
                fn(yb[:, par, 0:512], PS[0:B, 4 + 2 * par, :], ACT.Copy).then_inc(s["y_act"], 1)

            x_copy(0, 0, True)
            for e in range(4):
                gate(e % 2, e, e < 2)
                x_copy((e + 1) % 2, e + 1, e + 1 < 2)
                if e > 0:
                    y_copy((e - 1) % 2, e - 1, e - 1 < 2)
            with act.Fori(1, NE // 4) as i:
                for u in range(4):
                    e = i * 4 + u
                    gate(u % 2, e, False)
                    x_copy((u + 1) % 2, e + 1, False)
                    y_copy((u - 1) % 2, e - 1, False)
            y_copy(1, NE - 1, False)
            act.wait_ge(s["ov_ready"], 2)
            blocks = act.value_load(ovi[0:1, NOV:NOV + 1], min_val=0, max_val=NOV)
            with act.Fori(0, NOV) as i:
                with act.If(i < blocks):
                    act.wait_ge(s["ov_xt_full"], i + 1)
                    fn(xT[:, 0].rearrange("p k n -> p (k n)"), PS[:, 0, 0:KD * B], ACT.Copy).then_inc(s["ov_xt_ready"], 1)
                    act.wait_ge(s["ov_ab"], i + 1)
                    fn(tg[:, 0].rearrange("p j n -> p (j n)"), PS[:, 2, 0:2 * B], ACT.Tanh, scale=0.5).then_inc(s["ov_tanh"], 1)
                    act.wait_ge(s["y_stored0"], 8 * NE)
                    act.wait_ge(s["ov_stored"], i * 16)
                    act.wait_ge(s["ov_y_mm"], i + 1)
                    fn(yb[:, 0, 0:512], PS[0:B, 4, :], ACT.Copy).then_inc(s["ov_y_act"], 1)

        @block.vector
        def _(dve):
            st = Steps(dve, s["dve_step"])
            V_ = nc.vector

            def full(key):
                dve.wait_ge(s["psum_full"], UNIT_NO[key] + 1)
                return bank(key)

            def link(ins, sem_=None):
                st.after(st.mark(ins, sem_))

            def norm(key):
                dve.wait_ge(s["rstd_ready"], NORM_NO[key] + 1)
                return rstd[0:norm_rows(key), NORM_NO[key], 0:NORM_HEADS[key[0]]]

            def scaled_rows(dst, src, r, gain, ready):
                V_.scalar_tensor_tensor(dst, src, r, gain, ALU.mult, ALU.mult).then_inc(ready, 1)

            def scaled_heads(rows_, key, heads, gain, ready):
                n = norm_rows(key)
                r = norm(key)
                for h in range(heads):
                    ins = V_.scalar_tensor_tensor(rows_[:, h, :], rows_[:, h, :], r[:, h:h + 1], gain[0:n], ALU.mult, ALU.mult)
                    if h < heads - 1:
                        st.mark(ins)
                return ins

            dve.wait_ge(s["gattn_loaded"], 16)
            for t, (f, n) in enumerate(TILES):
                scaled_rows(Hn[0:n, t, :], X0[0:n, t, :], norm(("x", t)), grow[0:n, :], s["h_ready"])
            gmem = memT[:, 0:4, :].rearrange("p k n -> p (k n)")
            dve.wait_ge(s["mem_loaded"], 16 * 3)
            for t in range(2):
                scaled_rows(mem[:, t, :], mem[:, t, :], norm(("m", t)), gmem, s["mem_ready"])
            dve.wait_ge(s["s5_den"], 1)
            V_.reciprocal(s5tmp[:, 11, :], s5tmp[:, 10, :]).then_inc(s["s5_rden"], 1)
            dve.wait_ge(s["gains_loaded"], 16 * 6)

            def normalised(kind, t):
                n = norm_rows((kind, t))
                if kind == "ql":
                    scaled_rows(qlat[0:n, t, :], qlat[0:n, t, :], norm(("ql", t)), g_ql[0:n], s["ql_ready"])
                elif kind == "ck":
                    c = ckv[0:n, KEY_OF_TILE[t], 0:KVL]
                    scaled_rows(c, c, norm(("ck", t)), g_kv[0:n], s["ck_ready"])
                elif kind == "qm":
                    scaled_heads(qmem[0:n, t].rearrange("p (h d) -> p h d", h=MH), ("qm", t), MH, g_mq, None).then_inc(s["qm_ready"], 1)
                else:
                    scaled_heads(mk[:, 0, t].rearrange("p (h d) -> p h d", h=MH), ("mk", t), MH, g_mk, None).then_inc(s["mk_ready"], 1)

            def win(x):
                return x.rearrange("p (w j) -> p w j", j=WIN)

            def tables(q):
                return (cosT[:, q, None, :].broadcast_to([128, NWIN, WIN]), sinT[:, q, None, :].broadcast_to([128, NWIN, WIN]))

            def turn_in(q):
                cb, sb_ = tables(q)
                if q == 0:
                    dve.wait_ge(s["s5_tables"], 1)
                dve.wait_ge(s["bu_full"], q + 1)
                re, im = PS[:, BU, 0:TOK], PS[:, BU + 1, 0:TOK]
                m1 = st.mark(V_.tensor_tensor(win(rotA[:, 0]), win(re), cb, ALU.mult))
                m2 = st.mark(V_.tensor_tensor(win(rotB[:, 0]), win(im), sb_, ALU.mult))
                m3 = st.mark(V_.tensor_tensor(win(rotA[:, 1]), win(im), cb, ALU.mult))
                m4 = st.mark(V_.tensor_tensor(win(rotB[:, 1]), win(re), sb_, ALU.mult), s["bu_free"])
                st.after(m2)
                m5 = st.mark(V_.tensor_tensor(rotA[:, 0], rotA[:, 0], rotB[:, 0], ALU.add))
                st.after(m4, m3)
                rotated.append(st.mark(V_.tensor_tensor(rotA[:, 1], rotA[:, 1], rotB[:, 1], ALU.subtract)))

            rotated, scanned = [], {}

            def turn_scan(q, part):
                mag = s5tmp[:, 2, q:q + 1].broadcast_to([128, WIN])

                def scan(w, c, initial):
                    return st.mark(V_.tensor_tensor_scan(rotB[:, c, WIN * w:WIN * w + WIN], mag, rotA[:, c, WIN * w:WIN * w + WIN],
                                                         initial, ALU.mult, ALU.add))

                if part == 0:
                    st.after(rotated[q])
                    scanned[q] = [scan(0, 0, 0.0), scan(0, 1, 0.0)]
                    for c in range(2):
                        scan(NWIN - 1, c, s5par[:, 2 + c, q:q + 1])
                for w in (1,) if part == 0 else range(2, NWIN - 1):
                    end = slice(WIN * w - 1, WIN * w)
                    c64, s64, n64 = cosT[:, q, WIN - 1:WIN], sinT[:, q, WIN - 1:WIN], s5tmp[:, 8, q:q + 1]
                    cr = carry[:, q % 2, w - 1]
                    st.after(scanned[q][1])
                    m7 = st.mark(V_.tensor_scalar(cr[:, 0:2], rotB[:, :, end].rearrange("p c o -> p (c o)"), c64, None, ALU.mult))
                    st.after(m7)
                    st.mark(V_.scalar_tensor_tensor(cr[:, 2:3], rotB[:, 1, end], n64, cr[:, 0:1], ALU.mult, ALU.add))
                    m8 = st.mark(V_.scalar_tensor_tensor(cr[:, 3:4], rotB[:, 0, end], s64, cr[:, 1:2], ALU.mult, ALU.add))
                    st.after(m8)
                    scanned[q] = [scan(w, c, cr[:, 2 + c:3 + c]) for c in range(2)]
            def turn_back(q):
                cb, sb_ = tables(q)
                st.after(scanned[q][1])
                dst = hS[:, q % 2]
                m1 = st.mark(V_.tensor_tensor(win(rotA[:, 0]), win(rotB[:, 0]), cb, ALU.mult))
                m2 = st.mark(V_.tensor_tensor(win(rotC[:, 0]), win(rotB[:, 1]), sb_, ALU.mult))
                m3 = st.mark(V_.tensor_tensor(win(rotA[:, 1]), win(rotB[:, 1]), cb, ALU.mult))
                m4 = st.mark(V_.tensor_tensor(win(rotC[:, 1]), win(rotB[:, 0]), sb_, ALU.mult))
                if q >= 2:
                    dve.wait_ge(s["y_full"], q - 1)
                st.after(m2)
                m5 = st.mark(V_.tensor_tensor(dst[:, 0], rotA[:, 0], rotC[:, 0], ALU.subtract))
                st.after(m4)
                m6 = st.mark(V_.tensor_tensor(dst[:, 1], rotA[:, 1], rotC[:, 1], ALU.add), s["h_state"])
                st.after(m6)
                st.mark(V_.tensor_copy(finals[:, :, :, q].rearrange("p s c -> p c s"), dst[:, :, SEQ - 1:TOK:DEC]), s["finals_copied"])
                if q % 4 == 1 and q > 1:
                    y_skip(q // 4 - 1)

            def y_skip(t):
                dve.wait_ge(s["y_full"], 4 * t + 4)
                V_.scalar_tensor_tensor(uT[:, t, :], uT[:, t, :], dskip[:, t:t + 1], PS[:, YB, 0:TOK], ALU.mult, ALU.add)\
                    .then_inc(s["y_skipped"], 1)

            dve.wait_ge(s["params_loaded"], 16 * 7)
            def attention(kind, units, step, m):
                if step not in ("S", "O"):
                    return
                unit0 = 0 if kind == "mem" else len(MEM_UNITS)
                _, t, h0, nh = units[m]
                n = TILES[t][1]
                nk = sum(key_blocks(units[m]))
                w = soft[0:n, (unit0 + m) % 4]
                if step == "S":
                    src = full((kind, "S", m))[0:n, 0:nh * nk]
                    heads = src.rearrange("p (h k) -> p h k", h=nh)
                    if kind == "mla" and t < 2:
                        mask = const(f"mask{t}")[0:n, None, :].broadcast_to([n, nh, nk])
                        link(V_.scalar_tensor_tensor(heads, heads, SCALE_MLA, mask, ALU.mult, ALU.add))
                        V_.tensor_reduce(w[:, 0, 0:nh], heads, AX.X, ALU.max, negate=True).then_inc(s["scores_max"], 1)
                    else:
                        link(V_.tensor_reduce(w[:, 0, 0:nh], heads, AX.X, ALU.max, negate=True))
                        V_.tensor_scalar(w[:, 0, 0:nh], w[:, 0, 0:nh], SCALE_MEM if kind == "mem" else SCALE_MLA, None, ALU.mult)\
                            .then_inc(s["scores_max"], 1)
                else:
                    dv = MD if kind == "mem" else VH
                    src = full((kind, "O", m))[0:n, 0:nh * dv].rearrange("p (h d) -> p h d", h=nh)
                    link(V_.reciprocal(w[:, 2, 0:nh], w[:, 1, 0:nh]))
                    st.mark(V_.tensor_tensor(O[0:n, t, dv * h0:dv * (h0 + nh)].rearrange("p (h d) -> p h d", h=nh), src,
                                             w[:, 2, 0:nh, None].broadcast_to([n, nh, dv]), ALU.mult), s["emptied_dve"])

            def heads_up(m):
                what, j, half = KQ_UNITS[m]
                n = KEYS[j][1] if what == "k" else TILES[j][1]
                where = POS_OF_KEY[j if what == "k" else KEY_OF_TILE[j]]
                x = KQ[0:n, m % KQ_BUFS]
                link(scaled_heads(x, ("kq", m), 4, g_kn if what == "k" else g_qn, None))
                r = x[:, :, NOPE:]
                hr = ROPE // 2
                a_, b_ = ropet[0:n, m % 2, 0], ropet[0:n, m % 2, 1]
                cos_, sin_ = rope[0:n, where, 0, None, :], rope[0:n, where, 1, None, :]
                st.mark(V_.tensor_tensor(a_, r, cos_.broadcast_to([n, 4, ROPE]), ALU.mult))
                st.mark(V_.tensor_tensor(b_[:, :, 0:hr], r[:, :, hr:], sin_[:, :, 0:hr].broadcast_to([n, 4, hr]), ALU.mult))
                link(V_.tensor_tensor(b_[:, :, hr:], r[:, :, 0:hr], sin_[:, :, hr:].broadcast_to([n, 4, hr]), ALU.mult))
                V_.tensor_tensor(r, a_, b_, ALU.add).then_inc(s["kq_ready"], 1)

            def gated(kind, d):
                src = full((kind, d))[:, 0:TOK]
                if kind == "outC":
                    dve.wait_ge(*emptied_at(UNIT_NO["gateC", d]))
                    link(V_.scalar_tensor_tensor(mergedT[:, d, :], mergedT[:, d, :], 1.0, src, ALU.add, ALU.mult), s["emptied_dve"])
                else:
                    dve.wait_ge(*emptied_at(UNIT_NO["gateB", d]))
                    m = mtmp[:, d % 2, :]
                    link(V_.scalar_tensor_tensor(m, gateB[:, d, :], 1.0, src, ALU.add, ALU.mult), s["emptied_dve"])
                    st.mark(V_.tensor_tensor(mergedT[:, d, :], mergedT[:, d, :], m, ALU.add))

            def gelu_inner(t):
                dve.wait_ge(s["y_square"], t + 1)
                link(V_.tensor_scalar(gelu[:, t % 2, :], gelu[:, t % 2, :], 0.044715, 1.0, ALU.mult, ALU.add))
                V_.tensor_tensor(gelu[:, t % 2, :], gelu[:, t % 2, :], uT[:, t, :], ALU.mult).then_inc(s["y_inner"], 1)

            def gelu_outer(t):
                dve.wait_ge(s["y_tanh"], t + 1)
                link(V_.tensor_scalar(gelu[:, t % 2, :], gelu[:, t % 2, :], 0.5, 0.5, ALU.mult, ALU.add))
                V_.tensor_tensor(uT[:, t, :], gelu[:, t % 2, :], uT[:, t, :], ALU.mult).then_inc(s["z_ready"], 1)

            for kind, *which in MIDDLE:
                if kind in ("mem", "mla"):
                    attention(kind, MEM_UNITS if kind == "mem" else MLA_UNITS, *which)
                elif kind == "norm_kq":
                    heads_up(*which)
                elif kind.startswith("norm_"):
                    normalised(kind[5:], *which)
                elif kind == "z1":
                    gelu_inner(*which)
                elif kind == "z3":
                    gelu_outer(*which)
                elif kind == "last_y":
                    y_skip(3)
                elif kind == "turn_in":
                    turn_in(*which)
                elif kind == "turn_scan":
                    turn_scan(*which)
                elif kind == "turn_back":
                    turn_back(*which)
                elif kind.startswith("out"):
                    gated(kind, *which)
            for d in range(KD):
                src = full(("gluv", d))[:, 0:TOK]
                dve.wait_ge(*emptied_at(UNIT_NO["glug", d]))
                m = mtmp[:, d % 2, :]
                link(V_.scalar_tensor_tensor(m, gsig[:, d % 2, :], 1.0, src, ALU.add, ALU.mult), s["emptied_dve"])
                if d == 0:
                    dve.wait_ge(*emptied_at(UNIT_NO["gateA", KD - 1]))
                link(V_.scalar_tensor_tensor(m, gateA[:, d, :], 1.0, m, ALU.add, ALU.mult))
                V_.scalar_tensor_tensor(mergedT[:, d, :], m, 0.5, mergedT[:, d, :], ALU.mult, ALU.add).then_inc(s["merged"], 1)
            dve.wait_ge(s["x_again"], 16 * NT)
            dve.wait_ge(s["gffn_loaded"], 16)
            link(V_.memset(lg[:], NEG))
            for t in range(NT + 1):
                if t < NT:
                    n = TILES[t][1]
                    for g, (d0, nd) in enumerate(DGROUPS):
                        src = full(("wout", g, t))[0:n, 0:128 * nd]
                        x = X[0:n, t, 128 * d0:128 * (d0 + nd)]
                        st.mark(V_.scalar_tensor_tensor(x, src, 0.5, x, ALU.mult, ALU.add), s["emptied_dve"])
                        if g == 0 and t > 0:
                            n1 = TILES[t - 1][1]
                            scaled_rows(h2[0:n1, t - 1, :], X[0:n1, t - 1, :], norm(("f", t - 1)), grow[0:n1, :], s["h2_ready"])
                else:
                    n1 = TILES[t - 1][1]
                    scaled_rows(h2[0:n1, t - 1, :], X[0:n1, t - 1, :], norm(("f", t - 1)), grow[0:n1, :], s["h2_ready"])
                if t > 0:
                    n1 = TILES[t - 1][1]
                    if t == 1:
                        dve.wait_ge(s["router_loaded"], 16 * 4)
                    src = full(("route", t - 1))
                    st.mark(V_.tensor_tensor(lg[0:n1, t - 1, 0:NG], src[0:n1, 0:NG], brow[0:n1, 0:NG], ALU.add))
                    st.mark(V_.tensor_tensor(lg[0:n1, t - 1, 8:40], src[0:n1, NG:NG + NE], brow[0:n1, NG:], ALU.add), s["emptied_dve"])

            st.after((s["emptied_dve"], st.count[s["emptied_dve"]]))
            for t in range(NT):
                st.mark(V_.max(r8[:, 0, t, :], lg[:, t, 0:8]))
            st.after((s["dve_step"], st.count[s["dve_step"]]))
            for t in range(NT):
                st.mark(V_.max_index(i8[:, 0, t, :], r8[:, 0, t, :], lg[:, t, 0:8]))
            V_.tensor_tensor(ex4[:, 0], lg[:, :, 0:NG], r8[:, 0, :, 0:1].broadcast_to([128, NT, NG]), ALU.subtract)\
                .then_inc(s["logits_in"], 1)
            st.after((s["dve_step"], st.count[s["dve_step"]]))
            link(V_.tensor_copy(rs[:, 0, :], i8[:, 0, :, 0]))
            link(V_.tensor_tensor(ex4[:, 2], const("iotae")[:, None, 0:NG].broadcast_to([128, NT, NG]),
                                  rs[:, 0, :, None].broadcast_to([128, NT, NG]), ALU.is_equal))
            link(V_.tensor_tensor(prod[:], lg[:, :, 8:40].rearrange("p t (g e) -> p t e g", g=NG),
                                  ex4[:, 2, :, None, :].broadcast_to([128, NT, EPG, NG]), ALU.mult))
            link(V_.tensor_reduce(r8[:, 1], prod[:], AX.X, ALU.add))
            for t in range(NT):
                st.mark(V_.max(r8[:, 2, t, :], r8[:, 1, t, :]))
            st.after((s["dve_step"], st.count[s["dve_step"]]))
            for t in range(NT):
                st.mark(V_.max_index(i8[:, 1, t, :], r8[:, 2, t, :], r8[:, 1, t, :]))
            V_.tensor_tensor(rs[:, 4, :], r8[:, 2, :, 1], r8[:, 2, :, 0], ALU.subtract).then_inc(s["logits_in"], 1)
            st.after((s["dve_step"], st.count[s["dve_step"]]))
            for k in range(2):
                st.mark(V_.tensor_copy(rs[:, 1 + k, :], i8[:, 1, :, k]))
            st.after((s["dve_step"], st.count[s["dve_step"]]))
            iotae = const("iotae")[:, None, :].broadcast_to([128, NT, NE])

            def spread(x, m):
                return x[:, :, None].broadcast_to([128, NT, m])

            def row(x):
                return x[:, None, :].broadcast_to([128, NT, NE])

            for k in range(2):
                link(V_.scalar_tensor_tensor(rs[:, 1 + k, :], rs[:, 0, :], float(EPG), rs[:, 1 + k, :], ALU.mult, ALU.add))
                link(V_.tensor_tensor(Ek[:, k], iotae, spread(rs[:, 1 + k, :], NE), ALU.is_equal))
                link(V_.tensor_tensor(Ek[:, k], Ek[:, k], spread(const("valid"), NE), ALU.mult))
            V_.tensor_tensor(Ek[:, 2], Ek[:, 0], Ek[:, 1], ALU.add).then_inc(s["onehot_ready"], 1)
            dve.wait_ge(s["logits_exp"], 2)
            link(V_.tensor_reduce(rs[:, 8, :], ex4[:, 1], AX.X, ALU.add))
            link(V_.reciprocal(rs[:, 9, :], rs[:, 8, :]))
            link(V_.tensor_scalar(rs[:, 10, :], rs[:, 5, :], 1.0, None, ALU.add))
            link(V_.reciprocal(rs[:, 11, :], rs[:, 10, :]))
            link(V_.scalar_tensor_tensor(rs[:, 6, :], rs[:, 11, :], 0.5, rs[:, 9, :], ALU.mult, ALU.mult))
            link(V_.tensor_tensor(rs[:, 7, :], rs[:, 6, :], rs[:, 5, :], ALU.mult))
            src = full("rank")
            n_, nb, incl, excl = cnt[:, 0], cnt[:, 1], cnt[:, 2], cnt[:, 3]
            ek2 = rs[:, 1:3, :]
            rank2, j2, slot2, ex2, blk2, pos2 = (rs[:, x:x + 2, :] for x in (12, 14, 16, 18, 20, 22))
            ranks = src[:, 0:NT * NE].rearrange("p (t e) -> p t e", t=NT)

            def of_expert(dst, rows_):
                for k in range(2):
                    st.mark(V_.tensor_tensor(tp[:, k], Ek[:, k], rows_, ALU.mult))
                st.after((s["dve_step"], st.count[s["dve_step"]]))
                return V_.tensor_reduce(dst, tp[:, 0:2], AX.X, ALU.add)

            def wide(x, m):
                return x[:, :, :, None].broadcast_to([128, 2, NT, m])

            link(V_.tensor_copy(n_, src[:, NT * NE:NT * NE + NE]))
            st.mark(V_.tensor_tensor(ncmp[:], n_[:, :, None].broadcast_to([128, NE, NJ]),
                                     const("blocks")[:, None, :].broadcast_to([128, NE, NJ]), ALU.is_gt))
            link(of_expert(rank2, ranks), s["emptied_dve"])
            st.mark(V_.tensor_reduce(nb, ncmp[:], AX.X, ALU.add))
            link(V_.tensor_tensor(jcmp[:], wide(rank2, NJ), const("blocks")[:, None, None, :].broadcast_to([128, 2, NT, NJ]), ALU.is_ge))
            st.mark(V_.tensor_tensor_scan(incl, const("ones")[:, 0:NE], nb, 0.0, ALU.mult, ALU.add))
            link(V_.tensor_reduce(j2, jcmp[:], AX.X, ALU.add))
            st.mark(V_.tensor_tensor(excl, incl, nb, ALU.subtract))
            link(V_.scalar_tensor_tensor(slot2, j2, -float(B), rank2, ALU.mult, ALU.add))
            link(V_.tensor_tensor(ohs[:], const("iotab")[:, None, None, :].broadcast_to([128, 2, NT, B]), wide(slot2, B), ALU.is_equal))
            link(of_expert(ex2, excl[:, None, :].broadcast_to([128, NT, NE])))
            link(V_.scalar_tensor_tensor(ex2, ex2, float(NE - 1), j2, ALU.add, ALU.add))
            link(V_.tensor_tensor(ex2, ex2, ek2, ALU.subtract))
            link(V_.tensor_scalar(pos2, j2, 0.5, None, ALU.is_gt))
            link(V_.tensor_tensor(ex2, pos2, ex2, ALU.mult))
            link(V_.tensor_tensor(blk2, ex2, ek2, ALU.add))
            link(V_.tensor_tensor(ohb[:, 2:4], const("iotablk")[:, None, None, :].broadcast_to([128, 2, NT, NBLK]), wide(blk2, NBLK), ALU.is_equal))
            V_.tensor_tensor(ohb[:, 0:2], ohb[:, 2:4], wide(const("tokid")[:, None, :].broadcast_to([128, 2, NT]), NBLK), ALU.mult)\
                .then_inc(s["tables_in"], 1)
            link(V_.scalar_tensor_tensor(pos2, blk2, float(B), slot2, ALU.mult, ALU.add))
            st.mark(V_.tensor_copy(pos[:], pos2))
            link(V_.tensor_tensor(ovcmp[:], incl[0:1, None, :].broadcast_to([1, NOV, NE]),
                                  const("iotablk")[0:1, 0:NOV, None].broadcast_to([1, NOV, NE]), ALU.is_le))
            link(V_.tensor_reduce(ovf[:, 0, :], ovcmp[:], AX.X, ALU.add))
            V_.tensor_copy(idx[:], full("table")[0:B, 0:NBLK]).then_inc(s["emptied_dve"], 1)
            link(V_.tensor_scalar(ovf[:, 1, :], ovf[:, 0, :], float(NE - 1), None, ALU.min))
            V_.tensor_copy(ovi[:, 0:NOV], ovf[:, 1, :]).then_inc(s["ov_ready"], 1)
            V_.tensor_copy(ovi[:, NOV:], incl[0:1, NE - 1:NE]).then_inc(s["ov_ready"], 1)
            dve.wait_ge(s["ov_ready"], 2)

            def hidden(par, e, first):
                dve.wait_ge(s["tanh_ready"], e + 1)
                if not first:
                    dve.wait_ge(s["y_mm"], e - 1)
                hidden_products(par, s["dve_moe"], e, s["hid_ready"])

            def hidden_products(par, half, e, ready):
                x1 = PS[:, 2 + par, 0:2 * B]
                x3 = PS[:, 2 + par, 2 * B:4 * B]
                u_ = ug[:, par].rearrange("p j n -> p (j n)")
                V_.scalar_tensor_tensor(u_, tg[:, par].rearrange("p j n -> p (j n)"), 1.0, x1, ALU.add, ALU.mult).then_inc(half, 1)
                dve.wait_ge(half, e + 1)
                V_.tensor_tensor(hid[:, par].rearrange("p j n -> p (j n)"), u_, x3, ALU.mult).then_inc(ready, 1)

            def y_copy(par, e, first):
                dve.wait_ge(s["y_mm"], e + 1)
                if not first:
                    dve.wait_ge(s[f"y_stored{par}"], 8 * (e - par))
                V_.tensor_copy(yb[:, par, 512:], PS[0:B, 5 + 2 * par, :]).then_inc(s["y_dve"], 1)

            for e in range(4):
                hidden(e % 2, e, e < 2)
                if e > 0:
                    y_copy((e - 1) % 2, e - 1, e - 1 < 2)
            with dve.Fori(1, NE // 4) as i:
                for u in range(4):
                    e = i * 4 + u
                    hidden(u % 2, e, False)
                    y_copy((u - 1) % 2, e - 1, False)
            y_copy(1, NE - 1, False)
            blocks = dve.value_load(ovi[0:1, NOV:NOV + 1], min_val=0, max_val=NOV)
            with dve.Fori(0, NOV) as i:
                with dve.If(i < blocks):
                    dve.wait_ge(s["ov_tanh"], i + 1)
                    hidden_products(0, s["ov_half"], i, s["ov_hid"])
                    dve.wait_ge(s["y_stored0"], 8 * NE)
                    dve.wait_ge(s["ov_stored"], i * 16)
                    dve.wait_ge(s["ov_y_mm"], i + 1)
                    V_.tensor_copy(yb[:, 0, 512:], PS[0:B, 5, :]).then_inc(s["ov_y_dve"], 1)
            for t, (f, n) in enumerate(TILES):
                dve.wait_ge(s[f"rows_gathered{t}"], 32)
                link(V_.scalar_tensor_tensor(X[0:n, t, :], rows[0:n, 0, t, :], rs[0:n, 6, t:t + 1], X[0:n, t, :], ALU.mult, ALU.add))
                V_.scalar_tensor_tensor(X[0:n, t, :], rows[0:n, 1, t, :], rs[0:n, 7, t:t + 1], X[0:n, t, :], ALU.mult, ALU.add)\
                    .then_inc(s["out_ready"], 1)

        @block.gpsimd
        def _(pool):
            st = Steps(pool, s["pool_step"])
            g_ = nc.gpsimd

            def link(ins, sem_=None):
                st.after(st.mark(ins, sem_))

            def norms(first, last):
                for n in range(first, last):
                    key = NORMS[n]
                    rows_, heads = norm_rows(key), NORM_HEADS[key[0]]
                    pool.wait_ge(s["sums_ready"], n + 1)
                    link(g_.tensor_scalar(means[0:rows_, n, 0:heads], sums[0:rows_, n, 0:heads], 1.0 / NORM_WIDTH[key[0]], EPS, ALU.mult, ALU.add))
                    g_.tensor_tensor(rstd[0:rows_, n, 0:heads], means[0:rows_, n, 0:heads], halves[0:rows_, 0:heads], ALU.pow)\
                        .then_inc(s["rstd_ready"], 1)

            link(g_.memset(halves[:], -0.5))
            norms(0, NORM_NO["qm", 0])

            pool.wait_ge(s["const_loaded"], 16)
            are, aim, dt = s5par[:, 0, :], s5par[:, 1, :], s5par[:, 4, :]
            tmp = [s5tmp[:, n, :] for n in range(19)]
            pool.wait_ge(*emptied_at(UNIT_NO["par"]))
            tt, ts = g_.tensor_tensor, g_.tensor_scalar
            link(tt(tmp[0], are, dt, ALU.mult), s["s5_scaled"])
            link(tt(tmp[1], aim, dt, ALU.mult))
            two_pi = 2 * math.pi
            link(ts(tmp[3], tmp[1], 1.0 / two_pi, None, ALU.mult))
            link(ts(tmp[3], tmp[3], 12582912.0, None, ALU.add))
            link(ts(tmp[3], tmp[3], 12582912.0, None, ALU.subtract))
            c1 = 6.28125
            c2 = float(np.float32(np.round((two_pi - c1) * 2 ** 21) / 2 ** 21))
            c3 = two_pi - c1 - c2
            src = tmp[1]
            for c in (c1, c2, c3):
                link(ts(tmp[9], tmp[3], c, None, ALU.mult))
                link(tt(tmp[4], src, tmp[9], ALU.subtract))
                src = tmp[4]
            link(ts(tmp[4], tmp[4], 3.141592, -3.141592, ALU.min, ALU.max), s["s5_reduced"])
            link(tt(tmp[9], are, are, ALU.mult))
            link(tt(tmp[10], aim, aim, ALU.mult))
            link(tt(tmp[10], tmp[9], tmp[10], ALU.add), s["s5_den"])
            pool.wait_ge(s["s5_sin_ready"], 2)
            link(tt(tmp[7], tmp[6], tmp[6], ALU.mult))
            link(ts(tmp[7], tmp[7], -2.0, 1.0, ALU.mult, ALU.add))
            pool.wait_ge(s["s5_mag_ready"], 1)
            link(tt(tmp[14], tmp[2], tmp[7], ALU.mult))
            link(tt(tmp[15], tmp[2], tmp[5], ALU.mult))
            link(ts(tmp[16], tmp[14], -1.0, None, ALU.add))
            pool.wait_ge(s["s5_rden"], 1)
            for out, x, y, op in ((12, are, aim, ALU.add), (13, None, None, ALU.subtract)):
                if out == 12:
                    link(tt(tmp[17], tmp[16], are, ALU.mult))
                    link(tt(tmp[18], tmp[15], aim, ALU.mult))
                else:
                    link(tt(tmp[17], tmp[15], are, ALU.mult))
                    link(tt(tmp[18], tmp[16], aim, ALU.mult))
                link(tt(tmp[17], tmp[17], tmp[18], op))
                link(tt(tmp[out], tmp[17], tmp[11], ALU.mult))
            pool.wait_ge(s["psum_full"], UNIT_NO["xT", NT - 1, 1] + 1)
            pool.wait_ge(s["params_loaded"], 16 * 7)
            fre, fim = (x[:, :, None].broadcast_to([128, GP, CH]) for x in (tmp[12], tmp[13]))
            br, bi = braw[:, 0], braw[:, 1]
            for c, (p0, p1, op) in enumerate((((fre, br), (fim, bi), ALU.subtract), ((fre, bi), (fim, br), ALU.add))):
                st.mark(tt(btmp[:, 2 * c], p0[0], p0[1], ALU.mult))
                link(tt(btmp[:, 2 * c + 1], p1[0], p1[1], ALU.mult))
                link(tt(bbar[:, c], btmp[:, 2 * c], btmp[:, 2 * c + 1], op))
                st.mark(ts(bpad[:, c, :, 0, :], bbar[:, c], const("sel_b")[:, 0:1], None, ALU.mult))
                st.mark(ts(bpad[:, c, :, 1, :], bbar[:, c], const("sel_b")[:, 1:2], None, ALU.mult), s["s5_padded"])
            for c in range(2):
                st.mark(ts(cpad[:, c, :, 0, :], craw[:, c], const("sel_c")[:, 2 * c:2 * c + 1], None, ALU.mult))
                st.mark(ts(cpad[:, c, :, 1, :], craw[:, c], const("sel_c")[:, 2 * c + 1:2 * c + 2], None, ALU.mult), s["s5_padded"])
            norms(NORM_NO["qm", 0], NORM_NO["mk", 0])
            st.mark(g_.tensor_copy(cosT[:, :, 0], tmp[7]))
            link(g_.tensor_copy(sinT[:, :, 0], tmp[5]))
            flat = btmp[:].rearrange("p n q c -> p (n q c)")
            n = 1
            while n < WIN:
                t1 = flat[:, 0:GP * n].rearrange("p (q j) -> p q j", q=GP)
                t2 = flat[:, 512:512 + GP * n].rearrange("p (q j) -> p q j", q=GP)
                cn, sn = (x[:, :, n - 1:n].broadcast_to([128, GP, n]) for x in (cosT, sinT))
                c0, s0 = cosT[:, :, 0:n], sinT[:, :, 0:n]
                st.mark(tt(t1, c0, cn, ALU.mult))
                link(tt(t2, s0, sn, ALU.mult))
                link(tt(cosT[:, :, n:2 * n], t1, t2, ALU.subtract))
                st.mark(tt(t1, s0, cn, ALU.mult))
                link(tt(t2, c0, sn, ALU.mult))
                link(tt(sinT[:, :, n:2 * n], t1, t2, ALU.add))
                n *= 2
            link(ts(tmp[8], sinT[:, :, WIN - 1], -1.0, None, ALU.mult), s["s5_tables"])
            norms(NORM_NO["mk", 0], len(NORMS))

            pool.wait_ge(s["h2_stored"], 16 * NT)
            pool.wait_ge(*emptied_at(UNIT_NO["table"]))
            for e in range(NE + 1):
                if e >= 2:
                    pool.wait_ge(s["xt_full"], e - 1)
                g_.indirect_dma_start(xg[:, e % 2, :], None, scratch["h2"], bass.IndirectOffsetOnAxis(ap=idx[:, e:e + 1], axis=0))\
                    .then_inc(s[f"gathered{e % 2}"], 16)
            pool.wait_ge(s["ov_ready"], 2)
            blocks = pool.value_load(ovi[0:1, NOV:NOV + 1], min_val=0, max_val=NOV)
            pool.wait_ge(s["xt_full"], NE)
            with pool.Fori(0, NOV) as i:
                with pool.If(i < blocks):
                    pool.wait_ge(s["ov_xt_full"], i)
                    g_.tensor_copy(idx_ov[:, 0:1], idx[:, bass.ds(i + NE, 1)]).then_inc(s["ov_idx"], 1)
                    pool.wait_ge(s["ov_idx"], i + 1)
                    pool.sem_inc(s["pool_passed"], 1)
                    g_.indirect_dma_start(xg[:, 1, :], None, scratch["h2"], bass.IndirectOffsetOnAxis(ap=idx_ov[:, 0:1], axis=0))\
                        .then_inc(s["ov_gathered"], 16)
            pool.wait_ge(s["y_filled"], 16 * len(FILLS))
            pool.wait_ge(s["y_stored0"], 8 * NE)
            pool.wait_ge(s["y_stored1"], 8 * NE)
            pool.wait_ge(s["ov_stored"], blocks * 16)
            pool.sem_inc(s["pool_passed"], 1)
            for t, (f, n) in enumerate(TILES):
                for k in range(2):
                    g_.indirect_dma_start(rows[0:n, k, t, :], None, scratch["y"], bass.IndirectOffsetOnAxis(ap=pos[0:n, k, t:t + 1], axis=0))\
                        .then_inc(s[f"rows_gathered{t}"], 16)


NAMES = ["x_prompt", "x_sample", "cache_mla_ckv", "cache_mla_kpe", "cache_ssm_re", "cache_ssm_im", "cache_mem_k",
         "cache_mem_v", "mem_prompt", "g_attn", "w_in", "ssm_a_re", "ssm_a_im", "ssm_log_dt", "ssm_b_re", "ssm_b_im",
         "ssm_c_re", "ssm_c_im", "ssm_d", "w_glu", "g_qlat", "w_uq", "g_kvlat", "w_ukv", "g_qn", "g_kn", "w_o_mla",
         "g_mem", "w_mem_kv", "g_mqn", "g_mkn", "w_o_mem", "w_out", "g_ffn", "w_rg", "b_rg", "w_re", "b_re", "w_e1",
         "w_e3", "w_e2"]
OUTPUTS = [("y_p", (SEQ, D), (1, SEQ, D)), ("y_s", (DEC, D), (1, DEC, D)),
           ("ckv_p", (SEQ, KVL), (1, 1, SEQ, KVL)), ("kpe_p", (SEQ, ROPE), (1, 1, SEQ, ROPE)),
           ("sre_p", (GP, 128), (1, 1, G, ST)), ("sim_p", (GP, 128), (1, 1, G, ST)),
           ("mem_k", (MEMT, MH * MD), (1, 1, MEMT, MH, MD)), ("mem_v", (MEMT, MH * MD), (1, 1, MEMT, MH, MD)),
           ("ckv_s", (DEC, KVL), (1, 1, DEC, KVL)), ("kpe_s", (DEC, ROPE), (1, 1, DEC, ROPE)),
           ("sre_s", (GP, 128), (1, 1, G, ST)), ("sim_s", (GP, 128), (1, 1, G, ST))]


def kernel(**inputs):
    import concourse.bacc as bacc
    from concourse.bass_utils import run_bass_kernel_spmd

    nc = bacc.Bacc("TRN2", target_bir_lowering=False, num_devices=1)
    arrays = {f"in_{name}": np.ascontiguousarray(inputs[name]) for name in NAMES}
    arrays["in_consts"] = constants()
    a = {name[3:]: nc.dram_tensor(name, x.shape, mybir.dt.from_np(x.dtype), kind="ExternalInput").ap() for name, x in arrays.items()}
    o = {name: nc.dram_tensor(f"out_{name}", shape, F32, kind="ExternalOutput").ap() for name, shape, _ in OUTPUTS}
    scratch = {"h2": nc.dram_tensor("h2_rows", (TOK, D), F32, kind="Internal").ap(),
               "y": nc.dram_tensor("expert_rows", (NBLK * B, D), F32, kind="Internal").ap()}
    build(nc, a, o, scratch)
    r = run_bass_kernel_spmd(nc, [arrays], core_ids=[0])
    return tuple(np.asarray(r.results[0][f"out_{name}"]).reshape(shape) for name, _, shape in OUTPUTS)
```
